# Optimizing a Trainium2 kernel written in Bass

```python
import math
import jax, jax.numpy as jnp
from jax import lax
import numpy as np

D_MODEL = 1024
BATCH = 1
SEQ = 256
DEPTH = 2

GROUP_WIDTH = D_MODEL // 4
HEAD_DIM = 64
N_HEADS_GROUP = GROUP_WIDTH // HEAD_DIM
D_MIX = 4 * GROUP_WIDTH

MOBA_BLOCK = 256
MOBA_TOPK = 3
MOBA_Q_CHUNK = 32
MLA_Q_RANK = 192
MLA_KV_RANK = 128
MLA_NOPE = 64
MLA_ROPE = 32
MLA_V = HEAD_DIM
MLA_QK = MLA_NOPE + MLA_ROPE
SB_Q_BLOCK = 128
SSM_HEADDIM = 64
SSM_HEADS = GROUP_WIDTH // SSM_HEADDIM
SSM_GROUPS = 2
SSM_STATE = 64
SSM_CONV = 4
SSM_CHUNK = 128
SSM_XBC = GROUP_WIDTH + 2 * SSM_GROUPS * SSM_STATE
D_FF = 2816
FFN_CONV = 3
ROPE_THETA = 10000.0
ATTN_Q_BLOCK = 128
EPS = 1e-6

MOBA_COLS = 3 * GROUP_WIDTH
MLA_COLS = MLA_Q_RANK + MLA_KV_RANK + MLA_ROPE
SB_COLS = 3 * GROUP_WIDTH
SSM_COLS = GROUP_WIDTH + SSM_XBC + SSM_HEADS
IN_COLS = MOBA_COLS + MLA_COLS + SB_COLS + SSM_COLS


def _split(x, sizes):
    outs, o = [], 0
    for s in sizes:
        outs.append(x[..., o:o + s])
        o += s
    return outs

def rms_norm(x, g):
    xf = x.astype(jnp.float32)
    y = xf * lax.rsqrt(jnp.mean(xf * xf, axis=-1, keepdims=True) + EPS)
    return (y * g.astype(jnp.float32)).astype(x.dtype)

def rope_tables(positions, dim):
    inv = 1.0 / (ROPE_THETA ** (jnp.arange(0, dim, 2, dtype=jnp.float32) / dim))
    ang = positions.astype(jnp.float32)[..., None] * inv
    return jnp.cos(ang), jnp.sin(ang)

def apply_rope(x, cos, sin):
    x1, x2 = jnp.split(x, 2, axis=-1)
    c = cos[:, :, None, :].astype(x.dtype)
    s = sin[:, :, None, :].astype(x.dtype)
    return jnp.concatenate([x1 * c - x2 * s, x1 * s + x2 * c], axis=-1)

def causal_dwconv(x, w):
    width, ch = w.shape
    return lax.conv_general_dilated(
        x, w[:, None, :], window_strides=(1,), padding=[(width - 1, 0)],
        dimension_numbers=("NWC", "WIO", "NWC"), feature_group_count=ch)

def moba_attention(q, k, v):
    bsz, seq, nh, hd = q.shape
    scale = hd ** -0.5
    nblk = -(-seq // MOBA_BLOCK)
    pad = nblk * MOBA_BLOCK - seq
    kp = jnp.pad(k, ((0, 0), (0, pad), (0, 0), (0, 0)))
    vp = jnp.pad(v, ((0, 0), (0, pad), (0, 0), (0, 0)))
    kbt = kp.reshape(bsz, nblk, MOBA_BLOCK, nh, hd).transpose(0, 3, 1, 2, 4)
    vbt = vp.reshape(bsz, nblk, MOBA_BLOCK, nh, hd).transpose(0, 3, 1, 2, 4)
    kmean = jnp.mean(kbt.astype(jnp.float32), axis=3).astype(k.dtype)
    k_eff = min(MOBA_TOPK, nblk)
    nq = seq // MOBA_Q_CHUNK
    qc = q.reshape(bsz, nq, MOBA_Q_CHUNK, nh, hd).transpose(1, 0, 2, 3, 4)
    blk_ids = jnp.arange(nblk)
    bi = jnp.arange(bsz)[:, None, None, None]
    hi = jnp.arange(nh)[None, :, None, None]

    def one_chunk(args):
        c, qi = args
        cur = (c * MOBA_Q_CHUNK) // MOBA_BLOCK
        gate = jnp.einsum("bqhd,bhnd->bhqn", qi, kmean).astype(jnp.float32)
        gate = jnp.where(blk_ids < cur, gate, -jnp.inf)
        _, idx = lax.top_k(gate, k_eff)
        valid = jnp.arange(k_eff) < cur
        k_sel = kbt[bi, hi, idx]
        v_sel = vbt[bi, hi, idx]
        s_sel = jnp.einsum("bqhd,bhqnjd->bhqnj", qi, k_sel).astype(jnp.float32) * scale
        s_sel = jnp.where(valid[None, None, None, :, None], s_sel, -jnp.inf)
        s_sel = s_sel.reshape(bsz, nh, MOBA_Q_CHUNK, k_eff * MOBA_BLOCK)
        k_own = lax.dynamic_index_in_dim(kbt, cur, axis=2, keepdims=False)
        v_own = lax.dynamic_index_in_dim(vbt, cur, axis=2, keepdims=False)
        s_own = jnp.einsum("bqhd,bhjd->bhqj", qi, k_own).astype(jnp.float32) * scale
        q_local = c * MOBA_Q_CHUNK + jnp.arange(MOBA_Q_CHUNK) - cur * MOBA_BLOCK
        causal = jnp.arange(MOBA_BLOCK)[None, :] <= q_local[:, None]
        s_own = jnp.where(causal, s_own, -jnp.inf)
        p = jax.nn.softmax(jnp.concatenate([s_sel, s_own], axis=-1), axis=-1).astype(v.dtype)
        p_sel = p[..., :k_eff * MOBA_BLOCK].reshape(bsz, nh, MOBA_Q_CHUNK, k_eff, MOBA_BLOCK)
        p_own = p[..., k_eff * MOBA_BLOCK:]
        return (jnp.einsum("bhqnj,bhqnjd->bqhd", p_sel, v_sel)
                + jnp.einsum("bhqj,bhjd->bqhd", p_own, v_own))

    out = lax.map(one_chunk, (jnp.arange(nq), qc))
    return out.transpose(1, 0, 2, 3, 4).reshape(bsz, seq, nh, hd)

def moba_mixer(p, cos, sin, qk_g):
    bsz, seq, _ = p.shape
    q, k, v = [t.reshape(bsz, seq, N_HEADS_GROUP, HEAD_DIM) for t in _split(p, (GROUP_WIDTH,) * 3)]
    q = apply_rope(rms_norm(q, qk_g[0]), cos, sin)
    k = apply_rope(rms_norm(k, qk_g[1]), cos, sin)
    return moba_attention(q, k, v)

def causal_softmax_attention(q, k, v, scale):
    bsz, seq, nh, dk = q.shape
    nb = seq // ATTN_Q_BLOCK
    qb = q.reshape(bsz, nb, ATTN_Q_BLOCK, nh, dk).transpose(1, 0, 2, 3, 4)
    kpos = jnp.arange(seq)

    def one_block(args):
        i, qi = args
        s = jnp.einsum("bqhd,bkhd->bhqk", qi, k).astype(jnp.float32) * scale
        qpos = i * ATTN_Q_BLOCK + jnp.arange(ATTN_Q_BLOCK)
        s = jnp.where(kpos[None, :] <= qpos[:, None], s, -jnp.inf)
        pr = jax.nn.softmax(s, axis=-1).astype(v.dtype)
        return jnp.einsum("bhqk,bkhd->bqhd", pr, v)

    out = lax.map(one_block, (jnp.arange(nb), qb))
    return out.transpose(1, 0, 2, 3, 4).reshape(bsz, seq, nh, v.shape[-1])

def mla_mixer(p, cos, sin, q_norm_g, kv_norm_g, w_uq, w_ukv, qk_g):
    bsz, seq, _ = p.shape
    c_q, c_kv, k_rope = _split(p, (MLA_Q_RANK, MLA_KV_RANK, MLA_ROPE))
    q = jnp.einsum("bsr,rc->bsc", rms_norm(c_q, q_norm_g), w_uq).reshape(bsz, seq, N_HEADS_GROUP, MLA_QK)
    kv = jnp.einsum("bsr,rc->bsc", rms_norm(c_kv, kv_norm_g), w_ukv).reshape(bsz, seq, N_HEADS_GROUP, MLA_NOPE + MLA_V)
    k_nope, v = kv[..., :MLA_NOPE], kv[..., MLA_NOPE:]
    k_pe = jnp.broadcast_to(k_rope[:, :, None, :], (bsz, seq, N_HEADS_GROUP, MLA_ROPE))
    k = jnp.concatenate([k_nope, k_pe], axis=-1)
    q = rms_norm(q, qk_g[0])
    k = rms_norm(k, qk_g[1])
    q = jnp.concatenate([q[..., :MLA_NOPE], apply_rope(q[..., MLA_NOPE:], cos, sin)], axis=-1)
    k = jnp.concatenate([k[..., :MLA_NOPE], apply_rope(k[..., MLA_NOPE:], cos, sin)], axis=-1)
    return causal_softmax_attention(q, k, v, MLA_QK ** -0.5)

def stick_breaking_mixer(p):
    bsz, seq, _ = p.shape
    q, k, v = [t.reshape(bsz, seq, N_HEADS_GROUP, HEAD_DIM) for t in _split(p, (GROUP_WIDTH,) * 3)]
    scale = HEAD_DIM ** -0.5
    nb = seq // SB_Q_BLOCK
    qb = q.reshape(bsz, nb, SB_Q_BLOCK, N_HEADS_GROUP, HEAD_DIM).transpose(1, 0, 2, 3, 4)
    kpos = jnp.arange(seq)

    def one_block(args):
        i, qi = args
        z = jnp.einsum("bqhd,bkhd->bhqk", qi, k).astype(jnp.float32) * scale
        qpos = i * SB_Q_BLOCK + jnp.arange(SB_Q_BLOCK)
        strict = kpos[None, :] < qpos[:, None]
        log_beta = jax.nn.log_sigmoid(z)
        log_1mb = jnp.where(strict, jax.nn.log_sigmoid(-z), 0.0)
        tail = lax.cumsum(log_1mb, axis=3, reverse=True) - log_1mb
        a = jnp.where(strict, jnp.exp(log_beta + tail), 0.0).astype(v.dtype)
        return jnp.einsum("bhqk,bkhd->bqhd", a, v)

    out = lax.map(one_block, (jnp.arange(nb), qb))
    return out.transpose(1, 0, 2, 3, 4).reshape(bsz, seq, N_HEADS_GROUP, HEAD_DIM)

def ssd_chunked(xh, dt, a_head, bm, cm):
    bsz, seq, nh, hp = xh.shape
    ns = bm.shape[-1]
    nc, cl = seq // SSM_CHUNK, SSM_CHUNK
    x = (xh * dt[..., None]).reshape(bsz, nc, cl, nh, hp)
    a = (dt * a_head).reshape(bsz, nc, cl, nh).transpose(0, 3, 1, 2)
    bc = bm.reshape(bsz, nc, cl, nh, ns)
    cc = cm.reshape(bsz, nc, cl, nh, ns)
    a_cum = jnp.cumsum(a, axis=-1)
    tri = jnp.tril(jnp.ones((cl, cl), dtype=bool))
    seg = a_cum[..., :, None] - a_cum[..., None, :]
    lmat = jnp.where(tri, jnp.exp(jnp.where(tri, seg, 0.0)), 0.0)
    y_diag = jnp.einsum("bclhn,bcshn,bhcls,bcshp->bclhp", cc, bc, lmat, x)
    decay_states = jnp.exp(a_cum[..., -1:] - a_cum)
    states = jnp.einsum("bclhn,bhcl,bclhp->bchpn", bc, decay_states, x)
    chunk_decay = jnp.exp(a_cum[..., -1])

    def step(h, inp):
        s_c, d_c = inp
        return d_c[..., None, None] * h + s_c, h

    h0 = jnp.zeros((bsz, nh, hp, ns), jnp.float32)
    _, prev = lax.scan(step, h0, (states.transpose(1, 0, 2, 3, 4), chunk_decay.transpose(2, 0, 1)))
    prev = prev.transpose(1, 0, 2, 3, 4)
    y_off = jnp.einsum("bclhn,bchpn,bhcl->bclhp", cc, prev, jnp.exp(a_cum))
    return (y_diag + y_off).reshape(bsz, seq, nh, hp)

def mamba2_mixer(p, conv_w, conv_b, dt_bias, a_log, d_skip, norm_g):
    bsz, seq, _ = p.shape
    z, xbc, dt_raw = _split(p, (GROUP_WIDTH, SSM_XBC, SSM_HEADS))
    xbc = jax.nn.silu(causal_dwconv(xbc, conv_w) + conv_b)
    xs, bm, cm = _split(xbc, (GROUP_WIDTH, SSM_GROUPS * SSM_STATE, SSM_GROUPS * SSM_STATE))
    rep = SSM_HEADS // SSM_GROUPS
    xh = xs.reshape(bsz, seq, SSM_HEADS, SSM_HEADDIM).astype(jnp.float32)
    bm = jnp.repeat(bm.reshape(bsz, seq, SSM_GROUPS, SSM_STATE), rep, axis=2).astype(jnp.float32)
    cm = jnp.repeat(cm.reshape(bsz, seq, SSM_GROUPS, SSM_STATE), rep, axis=2).astype(jnp.float32)
    dt = jax.nn.softplus(dt_raw.astype(jnp.float32) + dt_bias.astype(jnp.float32))
    a_head = -jnp.exp(a_log.astype(jnp.float32))
    y = ssd_chunked(xh, dt, a_head, bm, cm) + d_skip.astype(jnp.float32)[:, None] * xh
    y = y.reshape(bsz, seq, GROUP_WIDTH).astype(p.dtype)
    return rms_norm(y * jax.nn.silu(z), norm_g)

def first_inputs(seed: int = 0) -> dict:
    key = jax.random.key(seed)
    ks = jax.random.split(key, 24)
    f32 = jnp.float32
    L = DEPTH

    def normal(k, shape, scale):
        return jax.random.normal(k, shape, f32) * scale

    def gain(k, shape):
        return 1.0 + 0.1 * jax.random.normal(k, shape, f32)

    x = normal(ks[0], (BATCH, SEQ, D_MODEL), 1.0)
    positions = (jax.random.randint(ks[1], (BATCH, 1), 0, 4096, dtype=jnp.int32)
                 + jnp.arange(SEQ, dtype=jnp.int32)[None, :])
    dt0 = jnp.exp(jax.random.uniform(ks[13], (L, SSM_HEADS), f32, math.log(1e-3), math.log(1e-1)))
    return {
        "x": x,
        "positions": positions,
        "mix_norm_g": gain(ks[2], (L, D_MODEL)),
        "w_in": normal(ks[3], (L, D_MODEL, IN_COLS), D_MODEL ** -0.5),
        "moba_qk_g": gain(ks[4], (L, 2, HEAD_DIM)),
        "mla_q_norm_g": gain(ks[5], (L, MLA_Q_RANK)),
        "mla_kv_norm_g": gain(ks[6], (L, MLA_KV_RANK)),
        "mla_w_uq": normal(ks[7], (L, MLA_Q_RANK, N_HEADS_GROUP * MLA_QK), MLA_Q_RANK ** -0.5),
        "mla_w_ukv": normal(ks[8], (L, MLA_KV_RANK, N_HEADS_GROUP * (MLA_NOPE + MLA_V)), MLA_KV_RANK ** -0.5),
        "mla_qk_g": gain(ks[9], (L, 2, MLA_QK)),
        "ssm_conv_w": normal(ks[10], (L, SSM_CONV, SSM_XBC), SSM_CONV ** -0.5),
        "ssm_conv_b": normal(ks[11], (L, SSM_XBC), 0.02),
        "ssm_dt_bias": dt0 + jnp.log(-jnp.expm1(-dt0)),
        "ssm_a_log": jnp.log(jax.random.uniform(ks[12], (L, SSM_HEADS), f32, 1.0, 16.0)),
        "ssm_d": gain(ks[14], (L, SSM_HEADS)),
        "ssm_norm_g": gain(ks[15], (L, GROUP_WIDTH)),
        "head_out_g": gain(ks[16], (L, 3, N_HEADS_GROUP, HEAD_DIM)),
        "w_out": normal(ks[17], (L, D_MIX, D_MODEL), D_MIX ** -0.5),
        "ffn_norm_g": gain(ks[18], (L, D_MODEL)),
        "ffn_w_in": normal(ks[19], (L, D_MODEL, 2 * D_FF), D_MODEL ** -0.5),
        "ffn_conv_w": normal(ks[20], (L, FFN_CONV, 2 * D_FF), FFN_CONV ** -0.5),
        "ffn_conv_b": normal(ks[21], (L, 2 * D_FF), 0.02),
        "ffn_w_out": normal(ks[22], (L, D_FF, D_MODEL), D_FF ** -0.5),
    }

def first_block(x, positions, mix_norm_g, w_in, moba_qk_g, mla_q_norm_g, mla_kv_norm_g,
              mla_w_uq, mla_w_ukv, mla_qk_g, ssm_conv_w, ssm_conv_b, ssm_dt_bias, ssm_a_log,
              ssm_d, ssm_norm_g, head_out_g, w_out, ffn_norm_g, ffn_w_in, ffn_conv_w,
              ffn_conv_b, ffn_w_out):
    bsz, seq, _ = x.shape
    cos_a, sin_a = rope_tables(positions, HEAD_DIM)
    cos_m, sin_m = rope_tables(positions, MLA_ROPE)
    for l in range(DEPTH):
        h = rms_norm(x, mix_norm_g[l])
        proj = jnp.einsum("bsd,dc->bsc", h, w_in[l])
        moba_p, mla_p, sb_p, ssm_p = _split(proj, (MOBA_COLS, MLA_COLS, SB_COLS, SSM_COLS))
        o_moba = moba_mixer(moba_p, cos_a, sin_a, moba_qk_g[l])
        o_mla = mla_mixer(mla_p, cos_m, sin_m, mla_q_norm_g[l], mla_kv_norm_g[l],
                          mla_w_uq[l], mla_w_ukv[l], mla_qk_g[l])
        o_sb = stick_breaking_mixer(sb_p)
        o_ssm = mamba2_mixer(ssm_p, ssm_conv_w[l], ssm_conv_b[l], ssm_dt_bias[l],
                             ssm_a_log[l], ssm_d[l], ssm_norm_g[l])
        heads = rms_norm(jnp.stack([o_moba, o_mla, o_sb], axis=2), head_out_g[l])
        mixed = jnp.concatenate([heads.reshape(bsz, seq, 3 * GROUP_WIDTH), o_ssm], axis=-1)
        x = x + jnp.einsum("bsc,cd->bsd", mixed, w_out[l])
        h = rms_norm(x, ffn_norm_g[l])
        u = causal_dwconv(jnp.einsum("bsd,df->bsf", h, ffn_w_in[l]), ffn_conv_w[l]) + ffn_conv_b[l]
        gate, up = _split(u, (D_FF, D_FF))
        x = x + jnp.einsum("bsf,fd->bsd", jax.nn.silu(gate) * up, ffn_w_out[l])
    return x


CHUNK = 64
N_META = 16
META_PAD = CHUNK - N_META
A_HEADS = 8
IDX_HEADS = 8
IDX_DIM = 64
DSA_MAX_K = 256
A_QBLK = 64
B_HEADS = 8
B_VDIM = 2 * HEAD_DIM
C_HEADS = 8
C_KV_HEADS = 2
C_WINDOW = 128
C_WIN_CHUNKS = C_WINDOW // CHUNK
D_WIDTH = 512
POOL_WINDOWS = (2, 4, 8, 16)
D_GROUP = D_WIDTH // len(POOL_WINDOWS)
NEG = -1e30

EVEN_SIZES = ([A_HEADS * HEAD_DIM] * 3 + [IDX_HEADS * IDX_DIM, IDX_DIM, IDX_HEADS]
              + [B_HEADS * HEAD_DIM] * 2 + [B_HEADS * B_VDIM] * 2)
EVEN_IN = sum(EVEN_SIZES)
EVEN_OUT = A_HEADS * HEAD_DIM + B_HEADS * B_VDIM
ODD_SIZES = [C_HEADS * HEAD_DIM, C_KV_HEADS * HEAD_DIM, C_KV_HEADS * HEAD_DIM, D_WIDTH]
ODD_IN = sum(ODD_SIZES)
ODD_OUT = C_HEADS * HEAD_DIM + D_WIDTH
N_EVEN = (DEPTH + 1) // 2
N_ODD = DEPTH // 2


def rms_norm_2(x, gain=None):
    xf = x.astype(jnp.float32)
    y = xf * lax.rsqrt(jnp.mean(xf * xf, axis=-1, keepdims=True) + EPS)
    if gain is not None:
        y = y * gain.astype(jnp.float32)
    return y.astype(x.dtype)

def swiglu(x, w_in, w_out):
    g, u = jnp.split(x @ w_in, 2, axis=-1)
    return (jax.nn.silu(g) * u) @ w_out

def split_cols(a, sizes):
    out, off = [], 0
    for s in sizes:
        out.append(a[..., off:off + s])
        off += s
    return out

def chunk_ids(n):
    return (jnp.arange(n) + META_PAD) // CHUNK

def pad_left(a):
    return jnp.pad(a, [(0, 0), (META_PAD, 0)] + [(0, 0)] * (a.ndim - 2))

def dsa_attention(q, k, v, iq, ik, iw, top_k):
    B, L, H, dh = q.shape
    cid = chunk_ids(L)
    nb = -(-L // A_QBLK)
    padn = nb * A_QBLK - L

    def blocks(a):
        a = jnp.pad(a, [(0, 0), (0, padn)] + [(0, 0)] * (a.ndim - 2))
        return jnp.moveaxis(a.reshape((B, nb, A_QBLK) + a.shape[2:]), 1, 0)

    q_cid = chunk_ids(nb * A_QBLK).reshape(nb, A_QBLK)
    iw = iw * (IDX_HEADS ** -0.5 * IDX_DIM ** -0.5)
    gather = jax.vmap(lambda t, i: t[i])

    def one_block(args):
        qb, iqb, iwb, qc = args
        logits = jnp.einsum('bqhd,bsd->bqhs', iqb, ik)
        score = jnp.einsum('bqh,bqhs->bqs', iwb, jax.nn.relu(logits)).astype(jnp.float32)
        adm = cid[None, :] <= qc[:, None]
        score = jnp.where(adm[None], score, NEG)
        _, idx = lax.top_k(score, top_k)
        valid = cid[idx] <= qc[None, :, None]
        kg = gather(k, idx)
        vg = gather(v, idx)
        s = jnp.einsum('bqhd,bqkhd->bhqk', qb, kg).astype(jnp.float32) * dh ** -0.5
        s = jnp.where(valid[:, None], s, NEG)
        p = jax.nn.softmax(s, axis=-1).astype(v.dtype)
        return jnp.einsum('bhqk,bqkhd->bqhd', p, vg)

    out = lax.map(one_block, (blocks(q), blocks(iq), blocks(iw), q_cid))
    return jnp.moveaxis(out, 0, 1).reshape(B, nb * A_QBLK, H, dh)[:, :L]

def rotary(x, pos):
    d = x.shape[-1]
    inv = 1.0 / (10000.0 ** (jnp.arange(0, d, 2, dtype=jnp.float32) / d))
    ang = pos.astype(jnp.float32)[:, None] * inv[None]
    cos = jnp.cos(ang)[None, :, None, :]
    sin = jnp.sin(ang)[None, :, None, :]
    x1, x2 = jnp.split(x.astype(jnp.float32), 2, axis=-1)
    return jnp.concatenate([x1 * cos - x2 * sin, x1 * sin + x2 * cos], axis=-1).astype(x.dtype)

def retention(q, k, v):
    B, Lp, H, dk = q.shape
    dv = v.shape[-1]
    N = Lp // CHUNK
    pos = jnp.arange(Lp) - META_PAD
    q = rotary(q, pos)
    k = rotary(k, pos) * dk ** -0.5
    log_g = jnp.log(1.0 - 2.0 ** (-5.0 - jnp.arange(H, dtype=jnp.float32)))
    i = jnp.arange(CHUNK, dtype=jnp.float32)
    rel = i[:, None] - i[None, :]
    dmat = jnp.where(rel >= 0, jnp.exp(jnp.maximum(rel, 0.0)[None] * log_g[:, None, None]), 0.0)
    q_dec = jnp.exp((i + 1.0)[:, None] * log_g[None])
    k_dec = jnp.exp((CHUNK - 1.0 - i)[:, None] * log_g[None])
    c_dec = jnp.exp(CHUNK * log_g)
    qc = q.reshape(B, N, CHUNK, H, dk)
    kc = k.reshape(B, N, CHUNK, H, dk)
    vc = v.reshape(B, N, CHUNK, H, dv)
    inner = jnp.einsum('bnihd,bnjhd->bnhij', qc, kc) * dmat.astype(q.dtype)
    inner = jnp.einsum('bnhij,bnjhe->bnihe', inner, vc)

    def step(S, xs):
        qn, kn, vn = xs
        cross = jnp.einsum('bihd,bhde->bihe', qn, S) * q_dec[None, :, :, None]
        S = S * c_dec[None, :, None, None] + jnp.einsum(
            'bjhd,bjhe->bhde', kn * k_dec[None, :, :, None], vn)
        return S, cross

    S0 = jnp.zeros((B, H, dk, dv), jnp.float32)
    _, cross = lax.scan(step, S0, (jnp.moveaxis(qc, 1, 0), jnp.moveaxis(kc, 1, 0),
                                   jnp.moveaxis(vc, 1, 0)))
    out = inner + jnp.moveaxis(cross, 0, 1).astype(inner.dtype)
    return out.reshape(B, Lp, H, dv)

def swa_sinks(q, k, v, sinks):
    B, Lp, H, dh = q.shape
    G = k.shape[2]
    R = H // G
    N = Lp // CHUNK
    W = C_WIN_CHUNKS

    def band(t):
        tc = t.reshape(B, N, CHUNK, G, dh)
        tp = jnp.pad(tc, ((0, 0), (W, 0), (0, 0), (0, 0), (0, 0)))
        bnd = jnp.concatenate([tp[:, j:j + N] for j in range(W + 1)], axis=2)
        meta = jnp.broadcast_to(t[:, META_PAD:CHUNK][:, None], (B, N, N_META, G, dh))
        return jnp.concatenate([meta, bnd], axis=2)

    kb, vb = band(k), band(v)
    key_chunk = jnp.arange(N)[:, None] - W + (jnp.arange((W + 1) * CHUNK) // CHUNK)[None]
    valid = jnp.concatenate([jnp.ones((N, N_META), bool), key_chunk >= 1], axis=1)
    qg = q.reshape(B, N, CHUNK, G, R, dh)
    s = jnp.einsum('bncgrd,bnkgd->bngrck', qg, kb).astype(jnp.float32) * dh ** -0.5
    s = jnp.where(valid[None, :, None, None, None, :], s, NEG)
    sink = jnp.broadcast_to(sinks.reshape(G, R).astype(jnp.float32)[None, None, :, :, None, None],
                            s.shape[:-1] + (1,))
    p = jax.nn.softmax(jnp.concatenate([s, sink], axis=-1), axis=-1)[..., :-1].astype(v.dtype)
    out = jnp.einsum('bngrck,bnkgd->bncgrd', p, vb)
    return out.reshape(B, Lp, H, dh)

def pool_mixer(x, d_mix, d_scale):
    B, L, _ = x.shape
    xg = x.astype(jnp.float32).reshape(B, L, len(POOL_WINDOWS), D_GROUP)
    cs = jnp.pad(jnp.cumsum(xg, axis=1), ((0, 0), (1, 0), (0, 0), (0, 0)))
    t = jnp.arange(L)
    pooled = []
    for gi, w in enumerate(POOL_WINDOWS):
        c = cs[:, :, gi]
        lag = jnp.pad(c, ((0, 0), (w, 0), (0, 0)))[:, 1:L + 1]
        cnt = jnp.minimum(t + 1, w).astype(jnp.float32)[None, :, None]
        pooled.append((c[:, 1:] - lag) / cnt)
    pooled = jnp.stack(pooled, axis=2)
    y = (pooled - xg).astype(x.dtype)
    y = jnp.einsum('blgc,gce->blge', y, d_mix).reshape(B, L, D_WIDTH)
    return y * d_scale

def even_mixer(h, w_in, a_qn, a_kn, w_out, top_k):
    B, L, _ = h.shape
    aq, ak, av, iq, ik, iw, bq, bk, bv, bg = split_cols(h @ w_in, EVEN_SIZES)
    hd = lambda t, n: t.reshape(B, L, n, -1)
    aq = rms_norm_2(hd(aq, A_HEADS), a_qn)
    ak = rms_norm_2(hd(ak, A_HEADS), a_kn)
    ya = dsa_attention(aq, ak, hd(av, A_HEADS), hd(iq, IDX_HEADS), ik, iw, top_k)
    ya = ya.reshape(B, L, -1)
    yb = retention(pad_left(hd(bq, B_HEADS)), pad_left(hd(bk, B_HEADS)),
                   pad_left(hd(bv, B_HEADS)))[:, META_PAD:]
    yb = rms_norm_2(yb).astype(h.dtype).reshape(B, L, -1) * jax.nn.silu(bg)
    return jnp.concatenate([ya, yb], axis=-1) @ w_out

def odd_mixer(h, w_in, c_qn, c_kn, c_sinks, d_mix, d_scale, w_out):
    B, L, _ = h.shape
    cq, ck, cv, dx = split_cols(h @ w_in, ODD_SIZES)
    hd = lambda t, n: t.reshape(B, L, n, -1)
    cq = rms_norm_2(hd(cq, C_HEADS), c_qn)
    ck = rms_norm_2(hd(ck, C_KV_HEADS), c_kn)
    yc = swa_sinks(pad_left(cq), pad_left(ck), pad_left(hd(cv, C_KV_HEADS)), c_sinks)
    yc = yc[:, META_PAD:].reshape(B, L, -1)
    yd = pool_mixer(dx, d_mix, d_scale)
    return jnp.concatenate([yc, yd], axis=-1) @ w_out

def second_inputs(seed: int = 0) -> dict:
    key = jax.random.key(seed)
    ks = jax.random.split(key, 21)
    f32 = jnp.float32
    nrm = lambda k, shape, fan: jax.random.normal(k, shape, f32) * fan ** -0.5
    gain = lambda k, shape: 1.0 + 0.05 * jax.random.normal(k, shape, f32)
    return {
        "x": jax.random.normal(ks[0], (BATCH, SEQ, D_MODEL), f32),
        "meta_tokens": jax.random.normal(ks[1], (N_META, D_MODEL), f32),
        "ffn1_norm": gain(ks[2], (DEPTH, D_MODEL)),
        "ffn1_w_in": nrm(ks[3], (DEPTH, D_MODEL, 2 * D_FF), D_MODEL),
        "ffn1_w_out": nrm(ks[4], (DEPTH, D_FF, D_MODEL), D_FF),
        "mix_norm": gain(ks[5], (DEPTH, D_MODEL)),
        "ffn2_norm": gain(ks[6], (DEPTH, D_MODEL)),
        "ffn2_w_in": nrm(ks[7], (DEPTH, D_MODEL, 2 * D_FF), D_MODEL),
        "ffn2_w_out": nrm(ks[8], (DEPTH, D_FF, D_MODEL), D_FF),
        "ev_w_in": nrm(ks[9], (N_EVEN, D_MODEL, EVEN_IN), D_MODEL),
        "ev_a_q_norm": gain(ks[10], (N_EVEN, HEAD_DIM)),
        "ev_a_k_norm": gain(ks[11], (N_EVEN, HEAD_DIM)),
        "ev_w_out": nrm(ks[12], (N_EVEN, EVEN_OUT, D_MODEL), EVEN_OUT),
        "od_w_in": nrm(ks[13], (N_ODD, D_MODEL, ODD_IN), D_MODEL),
        "od_c_q_norm": gain(ks[14], (N_ODD, HEAD_DIM)),
        "od_c_k_norm": gain(ks[15], (N_ODD, HEAD_DIM)),
        "od_c_sinks": 0.5 * jax.random.normal(ks[16], (N_ODD, C_HEADS), f32),
        "od_d_mix": nrm(ks[17], (N_ODD, len(POOL_WINDOWS), D_GROUP, D_GROUP), D_GROUP),
        "od_d_scale": gain(ks[18], (N_ODD, D_WIDTH)),
        "od_w_out": nrm(ks[19], (N_ODD, ODD_OUT, D_MODEL), ODD_OUT),
    }

def second_block(x, meta_tokens, ffn1_norm, ffn1_w_in, ffn1_w_out, mix_norm, ffn2_norm,
              ffn2_w_in, ffn2_w_out, ev_w_in, ev_a_q_norm, ev_a_k_norm, ev_w_out,
              od_w_in, od_c_q_norm, od_c_k_norm, od_c_sinks, od_d_mix, od_d_scale,
              od_w_out):
    B, S, D = x.shape
    top_k = min(DSA_MAX_K, S // 4)
    h = jnp.concatenate([jnp.broadcast_to(meta_tokens.astype(x.dtype)[None], (B, N_META, D)), x],
                        axis=1)
    for layer in range(DEPTH):
        h = h + (0.5 * swiglu(rms_norm_2(h, ffn1_norm[layer]), ffn1_w_in[layer],
                              ffn1_w_out[layer])).astype(h.dtype)
        hn = rms_norm_2(h, mix_norm[layer])
        if layer % 2 == 0:
            e = layer // 2
            y = even_mixer(hn, ev_w_in[e], ev_a_q_norm[e], ev_a_k_norm[e], ev_w_out[e], top_k)
        else:
            o = layer // 2
            y = odd_mixer(hn, od_w_in[o], od_c_q_norm[o], od_c_k_norm[o], od_c_sinks[o],
                          od_d_mix[o], od_d_scale[o], od_w_out[o])
        h = h + y.astype(h.dtype)
        h = h + (0.5 * swiglu(rms_norm_2(h, ffn2_norm[layer]), ffn2_w_in[layer],
                              ffn2_w_out[layer])).astype(h.dtype)
    return h[:, N_META:]


def setup_inputs(seed=0):
    out = dict(first_inputs(seed))
    for name, value in second_inputs(seed + 1).items():
        if name != "x":
            out[name + "_2"] = value
    return out


def reference(
    x, positions, mix_norm_g, w_in, moba_qk_g, mla_q_norm_g, mla_kv_norm_g, mla_w_uq, mla_w_ukv,
    mla_qk_g, ssm_conv_w, ssm_conv_b, ssm_dt_bias, ssm_a_log, ssm_d, ssm_norm_g, head_out_g,
    w_out, ffn_norm_g, ffn_w_in, ffn_conv_w, ffn_conv_b, ffn_w_out, meta_tokens_2, ffn1_norm_2,
    ffn1_w_in_2, ffn1_w_out_2, mix_norm_2, ffn2_norm_2, ffn2_w_in_2, ffn2_w_out_2, ev_w_in_2,
    ev_a_q_norm_2, ev_a_k_norm_2, ev_w_out_2, od_w_in_2, od_c_q_norm_2, od_c_k_norm_2,
    od_c_sinks_2, od_d_mix_2, od_d_scale_2, od_w_out_2,
):
    x = first_block(
        x, positions, mix_norm_g, w_in, moba_qk_g, mla_q_norm_g, mla_kv_norm_g, mla_w_uq,
        mla_w_ukv, mla_qk_g, ssm_conv_w, ssm_conv_b, ssm_dt_bias, ssm_a_log, ssm_d, ssm_norm_g,
        head_out_g, w_out, ffn_norm_g, ffn_w_in, ffn_conv_w, ffn_conv_b, ffn_w_out,
    )
    return second_block(
        x, meta_tokens_2, ffn1_norm_2, ffn1_w_in_2, ffn1_w_out_2, mix_norm_2, ffn2_norm_2,
        ffn2_w_in_2, ffn2_w_out_2, ev_w_in_2, ev_a_q_norm_2, ev_a_k_norm_2, ev_w_out_2,
        od_w_in_2, od_c_q_norm_2, od_c_k_norm_2, od_c_sinks_2, od_d_mix_2, od_d_scale_2,
        od_w_out_2,
    )


_drawn_inputs = setup_inputs


def setup_inputs(seed=0):
    import zlib

    import numpy as np

    out = dict(_drawn_inputs(seed))
    spreads = {}
    factors = {'ssm_conv_b': 3.555,
     'ffn_conv_b': 2.813,
     'ffn1_norm_2': 3.292,
     'ffn2_norm_2': 3.893,
     'ev_a_q_norm_2': 8.0,
     'ev_a_k_norm_2': 8.0,
     'od_c_q_norm_2': 8.0,
     'od_c_k_norm_2': 8.0,
     'od_c_sinks_2': 8.0,
     'od_d_scale_2': 4.419}
    for name, (base, spread) in spreads.items():
        noise = np.random.default_rng([zlib.crc32(name.encode()), seed]).standard_normal(out[name].shape)
        drawn = base * np.exp(spread * noise) if base else spread * noise
        out[name] = __import__('jax').numpy.asarray(drawn.astype(out[name].dtype))
    for name, factor in factors.items():
        out[name] = (out[name] * factor).astype(out[name].dtype)
    return out
```

```python
from collections import namedtuple
from contextlib import ExitStack

import numpy as np

import concourse.bass as bass
from concourse import mybir

F32 = mybir.dt.float32
I32 = mybir.dt.int32
ALU = mybir.AluOpType
ACT = mybir.ActivationFunctionType
AX = mybir.AxisListType

P = 128
D = 1024
KD = D // P
SEQ = 256
META = 16
TT = SEQ + META
DEPTH = 2
FF = 2816
KF = FF // P
FCH = 256
NFI = FF // FCH
OCH = 256
NFO = D // OCH
HD = 64
TOPK = min(256, SEQ // 4)
EPS = 1e-6
NEG = -1e30
TAKEN = -3e38
IN1 = 2660
TILES1 = [(0, 128), (128, 128)]
TILES2 = [(0, 80), (80, 128), (208, 64)]

NormPlan = namedtuple("NormPlan", "T n src ms dst gains rows width one over_tiles rot norm post")
SoftPlan = namedtuple("SoftPlan", "T tiles heads masks scale head0 sink copy_to")
SIGNALS = '''
    con_in par_in x_in pos_in mask_in swa_in wm_in0 wm_in1 out_written wa0 wa1 wb0 wb1
    dve_chain act_chain rope_ang rope_ready
    x_done squares sumsq rstd_ready h_ready
    prod_done silu_done act_done conv_init conv_done out_done
    nr_raw nr_sq nr_ms nr_rs nr_n nr_rot nr_done
    v_ready v_zero sub_done kr_ready qk_ready pv_done pv_copied
    sm_qk sm_nb sm_exp sm_p sm_pt sm_ptc
    sb_z sb_na sb_l sb_sp sb_tail sb_arg sb_e sb_a
    ssm_init ssm_conv ssm_xc ssm_na ssm_l ssm_dt ssm_tr ssm_cb ssm_arg ssm_e ssm_m ssm_y
    ix_logit ix_relu ix_acc ix_ready iw_ready picked_ready
    rt_s rt_m gate_ready dx_ready pool_y mix_ready'''
Signals = namedtuple("Signals", SIGNALS)


def plan_chunks():
    out, done = [], 0

    def add(source, width, steps):
        nonlocal done
        done += steps
        out.append((source, width, done))

    def ffn(f):
        for j in range(NFI):
            add(("ffn", f, j), KD * 2 * FCH, 2)

    mix = 0

    def mixer(widths):
        nonlocal mix
        for w in widths:
            add(("mix", mix), w, 1)
            mix += 1

    for l in range(DEPTH):
        mixer(MIX1)
        ffn(l)
    ffn(2)
    mixer(MIX_EVEN)
    ffn(3)
    ffn(4)
    mixer(MIX_ODD)
    ffn(5)
    return out


MIX1 = [KD * 512, KD * 512, KD * 420, KD * 512, KD * 512, KD * 256, KD * 512, KD * 512]
MIX_EVEN = [KD * 512] * 4 + [KD * 136] + [KD * 512] * 6 + [12 * 256] * 4
MIX_ODD = [KD * 512, KD * 384, KD * 512, 4 * 128, KD * 512, KD * 512]

WM = 2 * 384 + 4 * 96 + 256


def columns(widths):
    at, out = 0, {}
    for name, w in widths:
        out[name] = at
        at += w
    out["end"] = at
    return out


PC = columns([(f"{n}{l}", w) for l in range(DEPTH) for n, w in [
    ("mixg", 8), ("ffng", 8), ("mobaq", 1), ("mobak", 1), ("mlacq", 2), ("mlackv", 1), ("mlaq", 1), ("mlak", 1),
    ("ssmw", 16), ("ssmb", 4), ("dtb", 1), ("alog", 1), ("dskip", 2), ("ssmg", 2), ("headg", 6),
    ("fconv", KF * 8), ("ffn1g", 8), ("mix2g", 8), ("ffn2g", 8)]]
    + [("evq", 1), ("evk", 1), ("odq", 1), ("odk", 1), ("sink", 8), ("dscale", 4)])
CC = columns([("ident", 128), ("ones", 128), ("blk", 128), ("rot", 128), ("rot_mla", 128), ("later", 128),
              ("softmask", 256), ("ssmmask", 256), ("strict", 256), ("sel", 512), ("inv", 2), ("eps", 1), ("halfpi", 1),
              ("tri", TT), ("rcos", TT), ("rsin", TT), ("rq", 4 * TT), ("kdec", 24), ("cfix", 64)])


def constants():
    c = np.zeros((P, CC["end"]), np.float32)
    p = np.arange(P)

    def put(name, a):
        a = np.asarray(a, np.float32)
        c[:a.shape[0], CC[name]:CC[name] + a.shape[1]] = a

    put("ident", np.eye(P))
    put("ones", np.ones((P, P)))
    put("blk", (p[:, None] // HD == p[None] // HD))
    rot = np.zeros((P, P))
    for m in range(P):
        if m % HD < HD // 2:
            rot[m + HD // 2, m] = -1.0
        else:
            rot[m - HD // 2, m] = 1.0
    put("rot", rot)
    rot = np.zeros((P, P))
    for m in range(64, 80):
        rot[m + 16, m] = -1.0
        rot[m, m + 16] = 1.0
    put("rot_mla", rot)
    put("later", p[:, None] > p[None])
    q = np.arange(SEQ)
    put("softmask", np.where(q[None] <= p[:, None] + P, 0.0, NEG))
    put("ssmmask", np.where(p[:, None] <= q[None], 0.0, NEG))
    put("strict", p[:, None] < q[None])
    sel = np.zeros((4, 4, P))
    for h in range(4):
        sel[h, h] = 1.0
    put("sel", sel.reshape(4, 4 * P))
    inv64 = (np.float32(1.0) / (np.float32(10000.0) ** (np.arange(0, 64, 2, dtype=np.float32) / np.float32(64)))).astype(np.float32)
    inv32 = (np.float32(1.0) / (np.float32(10000.0) ** (np.arange(0, 32, 2, dtype=np.float32) / np.float32(32)))).astype(np.float32)
    inv = np.zeros((P, 2), np.float32)
    inv[:, 0] = inv64[p % 32]
    inv[64:96, 1] = inv32[np.arange(32) % 16]
    put("inv", inv)
    put("eps", np.full((P, 1), EPS))
    put("halfpi", np.full((P, 1), np.pi / 2))
    t = np.arange(TT)
    put("tri", p[:, None] <= t[None])
    ang = (t[None].astype(np.float32) * inv64[p % 32][:, None]).astype(np.float32)
    put("rcos", np.cos(ang.astype(np.float64)))
    put("rsin", np.sin(ang.astype(np.float64)))
    log_g = np.log(1.0 - 2.0 ** (-5.0 - np.arange(8)))
    put("rq", np.stack([np.exp(t[None] * log_g[2 * m + p // HD][:, None]) for m in range(4)], 1).reshape(P, -1))
    kdec = np.zeros((P, 3, 8))
    for kt, (t0, tl) in enumerate(TILES2):
        kdec[:tl, kt] = np.exp(-(t0 + np.arange(tl))[:, None] * log_g[None]) * HD ** -0.5
    put("kdec", kdec.reshape(P, 24))
    cfix = np.stack([w / np.minimum(np.arange(16) + 1, w) for w in (2, 4, 8, 16)])
    put("cfix", np.broadcast_to(cfix.reshape(1, 64), (P, 64)))
    return c


def chunk_masks():
    cid = (np.arange(TT) + 48) // 64
    out = np.zeros((2, P, 3, TT), np.float32)
    for qt, (t0, tl) in enumerate(TILES2):
        cq, ck = cid[t0:t0 + tl, None], cid[None]
        out[0, :tl, qt] = np.where(ck <= cq, 0.0, NEG)
        out[1, :tl, qt] = np.where((ck == 0) | ((ck <= cq) & (ck >= cq - 2)), 0.0, NEG)
    return out.reshape(2, P, 3 * TT)


def build_program(nc, wmix, wfi, wfo, wmla, params, consts, masks, xin, positions, out):
    chunks = plan_chunks()
    mix_at = {}
    at = 0
    for source, width, _ in chunks:
        if source[0] == "mix":
            mix_at[source[1]] = at
            at += P * width

    with ExitStack() as ctx:
        def sb(name, shape, dt=F32):
            return ctx.enter_context(nc.sbuf_tensor(name, shape, dt))

        PS = ctx.enter_context(nc.psum_tensor("PS", [P, 8, 512], F32))
        wa = sb("wa", [P, 2, KD * 512])
        wb = sb("wb", [P, 2, KF * OCH])
        wm = sb("wm", [P, WM])
        X = sb("X", [P, KD, TT])
        H = sb("H", [P, KD, TT])
        hidden = sb("hidden", [P, KF, TT])
        par = sb("par", [P, PC["end"]])
        con = sb("con", [P, CC["end"]])
        mask = sb("mask", [P, 3, TT])
        picked = sb("picked", [P, 3, TT])
        rstd = sb("rstd", [P, TT])
        W0, W1, W2 = (sb(f"W{i}", [P, 4, TT]) for i in range(3))
        QK = sb("QK", [P, 8, TT])
        VP = sb("VP", [P, 3, 8, P])
        MIX = sb("MIX", [P, 12, TT])
        G = sb("G", [P, 8, TT])
        posi = sb("posi", [P, SEQ], I32)
        rope = sb("rope", [P, 4, SEQ])
        small = sb("small", [P, 64])
        PT = hidden[:, 0:12, :].rearrange("p (k h) t -> p k h t", k=3)
        PB = hidden[:, 12:16, :]
        IQ = hidden[:, 16:20, :]
        IK = hidden[:, 20, :]
        dts = hidden[0:4, 21, :]
        rawdt, dt_, acum = G[0:4, 0, :], G[0:4, 1, :], G[0:4, 2, :]
        ea = small[0:4, 0:1]
        ZS = G[:, 4:6, :]
        CQ, CKV, KR = G[:, 4:6, :], G[:, 6, :], G[:, 7, :]
        cols = small[:, 1:17]
        negmax = small[:, 17:21]
        rowsum = small[:, 21:25]
        sinkex = small[:, 25:29]
        iwc = small[:, 29:53]
        top8 = small[:, 53:61]

        S = Signals(*[ctx.enter_context(nc.semaphore(n)) for n in SIGNALS.split()])

        def C(name, width, rows=P):
            return con[0:rows, CC[name]:CC[name] + width]

        def A(name, i=0, rows=P):
            return par[0:rows, PC[name] + i:PC[name] + i + 1]

        ident, ones, blk = C("ident", P), C("ones", P), C("blk", P)

        def wat(slot, n, w):
            return wa[:, slot, 0:n * w].rearrange("p (k c) -> p k c", k=n)

        WA = (S.wa0, S.wa1)
        WB = (S.wb0, S.wb1)
        rope64 = (C("rot", P), rope[:, 0, :], rope[:, 1, :])
        rope_mla = (C("rot_mla", 96, 96), rope[0:96, 2, :], rope[0:96, 3, :])
        rope_ret = (C("rot", P), C("rcos", TT), C("rsin", TT))

        def norm_plan(T, n, src, ms, dst, gains=None, rows=P, width=P, one=None, over_tiles=False, rot=None,
                      norm=True, post=None):
            return NormPlan(T, n, src, ms, dst, gains, rows, width, ones if one is None else one, over_tiles, rot,
                            norm, post)

        def per_head(a, n):
            return a.unsqueeze(1).to_broadcast([a.shape[0], n, a.shape[1]])

        def moba_qk(l):
            return norm_plan(SEQ, 4, 0, 4, QK[:, 0:4, 0:SEQ], [A(f"mobaq{l}")] * 2 + [A(f"mobak{l}")] * 2,
                             width=HD, one=blk, rot=rope64)

        def head_norm(l, m):
            return norm_plan(SEQ, 2, 0, 4, MIX[:, 2 * m:2 * m + 2, 0:SEQ],
                             [A(f"headg{l}", 2 * m), A(f"headg{l}", 2 * m + 1)], width=HD, one=blk)

        def mla_cq(l):
            return norm_plan(SEQ, 2, 0, 4, CQ[0:96, :, 0:SEQ], [A(f"mlacq{l}", i, 96) for i in range(2)], rows=96,
                             width=192, over_tiles=True)

        def mla_ckv(l):
            return norm_plan(SEQ, 1, 2, 5, CKV[:, 0:SEQ].unsqueeze(1), [A(f"mlackv{l}")], width=128)

        def mla_qk(l, k):
            return norm_plan(SEQ, 4, 0, 4, QK[0:96, 4 * k:4 * k + 4, 0:SEQ], [A(f"mlak{l}" if k else f"mlaq{l}", 0, 96)] * 4,
                             rows=96, width=96, rot=rope_mla)

        def ssm_out(l):
            return norm_plan(SEQ, 2, W0[:, 0:2, 0:SEQ], 4, MIX[:, 6:8, 0:SEQ], [A(f"ssmg{l}", i) for i in range(2)],
                             width=256, over_tiles=True)

        def qk2(name, n, t0):
            return norm_plan(TT, n, 0, 4, QK[:, t0:t0 + n, :], [A(name)] * n, width=HD, one=blk)

        def ret_qk(k):
            return norm_plan(TT, 4, 0, 4, QK[:, 4 * k:4 * k + 4, :], rot=rope_ret, norm=False,
                             post=None if k else C("rq", 4 * TT).rearrange("p (m t) -> p m t", m=4))

        def ret_out(g):
            return norm_plan(TT, 4, 4, 0, MIX[:, 4 + 4 * g:8 + 4 * g, :], width=P, post=G[:, 4 * g:4 * g + 4, :])

        def soft_plan(T, tiles, heads, masks, scale, head0=0, sink=False, copy_to=None):
            return SoftPlan(T, tiles, heads, masks, scale, head0, sink, copy_to)

        def half(t, h):
            return QK[HD * (h % 2):HD * (h % 2) + HD, t, :]

        def soft1():
            return [C("softmask", 256)[:, P:2 * P], C("softmask", 256)]

        def moba_soft():
            return soft_plan(SEQ, TILES1, [(half(h // 2, h), half(2 + h // 2, h)) for h in range(4)], soft1(), HD ** -0.5)

        def mla_soft():
            return soft_plan(SEQ, TILES1, [(QK[0:96, h, :], QK[0:96, 4 + h, :]) for h in range(4)], soft1(), 96 ** -0.5)

        def dsa_soft(g):
            return soft_plan(TT, TILES2, [(half(h // 2, h), half(4 + h // 2, h)) for h in range(4 * g, 4 * g + 4)],
                             [picked[:, i, :] for i in range(3)], HD ** -0.5, 4 * g, copy_to=MIX[:, 2 * g:2 * g + 2, :])

        def swa_soft(g):
            return soft_plan(TT, TILES2, [(half(h // 2, h), half(4 + g, h)) for h in range(4 * g, 4 * g + 4)],
                             [mask[:, i, :] for i in range(3)], HD ** -0.5, 4 * g, sink=True,
                             copy_to=MIX[:, 2 * g:2 * g + 2, :])

        def counter():
            seen = {}

            def upto(s, n=1):
                seen[id(s)] = seen.get(id(s), 0) + n
                return seen[id(s)]
            return upto

        def chunk_counter():
            taken = [0]

            def take(n=1):
                taken[0] += n
                return taken[0] - n
            return take

        block = ctx.enter_context(nc.Block())

        @block.sync
        def _(sp):
            sp.dma_start(X[:, :, META:TT], xin[:, 0:KD * SEQ].rearrange("p (k t) -> p k t", k=KD)).then_inc(S.x_in, 16)
            sp.dma_start(X[:, :, 0:META], xin[:, KD * SEQ:KD * TT].rearrange("p (k t) -> p k t", k=KD)).then_inc(S.x_in, 16)
            sp.dma_start(con[:], consts).then_inc(S.con_in, 16)
            sp.dma_start(par[:], params).then_inc(S.par_in, 16)
            sp.dma_start(posi[:], positions.to_broadcast([P, SEQ])).then_inc(S.pos_in, 16)
            sp.dma_start(mask[:].rearrange("p q t -> p (q t)"), masks[0]).then_inc(S.mask_in, 16)
            take = chunk_counter()
            take_b = chunk_counter()

            def slot_free(c):
                if c >= 2:
                    sp.wait_ge(S.prod_done, chunks[c - 2][2])

            def load_mix(n):
                for _ in range(n):
                    c = take()
                    source, width, _done = chunks[c]
                    slot_free(c)
                    src = wmix[mix_at[source[1]]:mix_at[source[1]] + P * width].rearrange("(p w) -> p w", p=P)
                    sp.dma_start(wa[:, c % 2, 0:width], src).then_inc(WA[c % 2], 16)

            def load_out(f, q):
                b = take_b()
                if b >= 2:
                    sp.wait_ge(S.out_done, 2 * (b - 1))
                sp.dma_start(wb[:, b % 2, :], wfo[f * NFO + q]).then_inc(WB[b % 2], 16)

            def load_ffn(f):
                load_out(f, 0)
                load_out(f, 1)
                c = take(NFI)
                done = chunks[c][2] - 2
                slot_free(c)
                with sp.Fori(0, NFI // 2) as i:
                    for s in range(2):
                        sp.wait_ge(S.prod_done, 4 * i + (done - 2 + 2 * s))
                        sp.dma_start(wa[:, (c + s) % 2, :], wfi[bass.ds(i * 2 + (f * NFI + s), 1)].rearrange(
                            "o p w -> (o p) w")).then_inc(WA[(c + s) % 2], 16)
                slot_free(c + NFI - 1)
                sp.dma_start(wa[:, (c + NFI - 1) % 2, :], wfi[f * NFI + NFI - 1]).then_inc(WA[(c + NFI - 1) % 2], 16)
                load_out(f, 2)
                load_out(f, 3)

            def load_mla(l, c_free):
                if l:
                    sp.wait_ge(S.prod_done, c_free)
                sp.dma_start(wm[:], wmla[l]).then_inc((S.wm_in0, S.wm_in1)[l], 16)

            load_mix(2)
            load_mla(0, 0)
            load_mix(len(MIX1) - 2)
            load_ffn(0)
            load_mla(1, chunks[4][2])
            load_mix(len(MIX1))
            load_ffn(1)
            load_ffn(2)
            load_mix(len(MIX_EVEN))
            load_ffn(3)
            sp.wait_ge(S.picked_ready, 3)
            sp.dma_start(mask[:].rearrange("p q t -> p (q t)"), masks[1]).then_inc(S.swa_in, 16)
            load_ffn(4)
            load_mix(len(MIX_ODD))
            load_ffn(5)
            sp.wait_ge(S.x_done, 1 + 2 * DEPTH + 3 * DEPTH)
            sp.dma_start(out, X[:, :, META:TT]).then_inc(S.out_written, 16)
            sp.wait_ge(S.out_written, 16)

        @block.tensor
        def _(pe):
            upto, take, take_b = counter(), chunk_counter(), chunk_counter()
            acts = [4]

            def landed(c):
                pe.wait_ge(WA[c % 2], 16 * (c // 2 + 1))
                return c % 2

            def input_norm(T):
                pe.wait_ge(S.squares, upto(S.squares))
                for k in range(KD):
                    mm = pe.matmul(PS[:, 7, 0:T], ones, H[:, k, 0:T], start=k == 0, stop=k == KD - 1)
                mm.then_inc(S.sumsq, 1)
                pe.wait_ge(S.h_ready, upto(S.h_ready))

            def tiles(w, cuts, T, src=None, kt=KD, rows=P):
                src = H if src is None else src
                for c0, m, bank in cuts:
                    for k in range(kt):
                        mm = pe.matmul(PS[0:m, bank, 0:T], w[0:rows, k, c0:c0 + m], src[0:rows, k, 0:T],
                                       start=k == 0, stop=k == kt - 1)
                return mm

            def tokens(w, c0, n, toks, places, src=None, kt=KD):
                src = H if src is None else src
                for (t0, tl), (bank, at) in zip(toks, places):
                    for k in range(kt):
                        mm = pe.matmul(PS[0:tl, bank, at:at + n], src[:, k, t0:t0 + tl], w[:, k, c0:c0 + n],
                                       start=k == 0, stop=k == kt - 1)
                return mm

            def norm_rope(q):
                if q.norm:
                    pe.wait_ge(S.nr_sq, upto(S.nr_sq))
                    for i in range(q.n):
                        bank, first, last = (q.ms, i == 0, i == q.n - 1) if q.over_tiles else (q.ms + i, True, True)
                        mm = pe.matmul(PS[0:q.rows, bank, 0:q.T], q.one[0:q.rows, 0:q.rows], W1[0:q.rows, i, 0:q.T],
                                       start=first, stop=last)
                    mm.then_inc(S.nr_ms, 1)
                if q.rot:
                    pe.wait_ge(S.nr_n, upto(S.nr_n))
                    for i in range(q.n):
                        mm = pe.matmul(PS[0:q.rows, i, 0:q.T], q.rot[0], W2[0:q.rows, i, 0:q.T], start=True, stop=True)
                    mm.then_inc(S.nr_rot, 1)
                pe.wait_ge(S.nr_done, upto(S.nr_done))

            def values(T, toks, head0=0, banks=(0, 1)):
                for pair, bank in enumerate(banks):
                    seq = [(kt, h) for kt in range(len(toks)) for h in (2 * pair, 2 * pair + 1)]
                    for i, (kt, h) in enumerate(seq):
                        t0, tl = toks[kt]
                        mm = pe.matmul(PS[:, bank, t0:T], VP[0:tl, kt, head0 + h, :], PT[0:tl, kt, h, t0:T],
                                       start=i == 0, stop=i == len(seq) - 1)
                mm.then_inc(S.pv_done, 1)

            def softmax(a):
                for qt, (q0, ql) in enumerate(a.tiles):
                    keys = q0 + ql
                    for h, (q, k) in enumerate(a.heads):
                        mm = pe.matmul(PS[0:ql, h, 0:keys], q[:, q0:q0 + ql], k[:, 0:keys], start=True, stop=True)
                    mm.then_inc(S.sm_qk, 1)
                    pe.wait_ge(S.sm_p, upto(S.sm_p))
                    if qt:
                        pe.wait_ge(S.sm_ptc, upto(S.sm_ptc))
                    for kt in range(qt + 1):
                        t0, tl = a.tiles[kt]
                        for h in range(4):
                            mm = pe.transpose(PS[0:tl, 4 + kt, h * P:h * P + ql], PB[0:ql, h, t0:t0 + tl],
                                              ident[0:ql, 0:ql])
                    mm.then_inc(S.sm_pt, 1)
                pe.wait_ge(S.sm_ptc, upto(S.sm_ptc))
                values(a.T, a.tiles, a.head0)
                if a.copy_to is not None:
                    pe.wait_ge(S.pv_copied, upto(S.pv_copied))

            def mixer1(l):
                input_norm(SEQ)
                c = take()
                w = wat(landed(c), KD, 512)
                tiles(w, [(P * i, P, i) for i in range(4)], SEQ).then_inc(S.prod_done, 1)
                norm_rope(moba_qk(l))
                c = take()
                w = wat(landed(c), KD, 512)
                tokens(w, 0, 512, TILES1, [(4, 0), (5, 0)]).then_inc(S.prod_done, 1)
                pe.wait_ge(S.v_ready, upto(S.v_ready))
                softmax(moba_soft())
                norm_rope(head_norm(l, 0))
                c = take()
                w = wat(landed(c), KD, 420)
                tiles(w, [(0, 96, 0), (96, 96, 1), (192, P, 2), (320, 96, 3), (416, 4, 7)], SEQ).then_inc(S.prod_done, 1)
                norm_rope(mla_cq(l))
                norm_rope(mla_ckv(l))
                pe.wait_ge(S.kr_ready, upto(S.kr_ready))
                pe.wait_ge((S.wm_in0, S.wm_in1)[l], 16)
                tiles(wm[:, 0:768].rearrange("p (k c) -> p k c", k=2), [(96 * h, 96, h) for h in range(4)], SEQ,
                      src=CQ, kt=2, rows=96).then_inc(S.sub_done, 1)
                norm_rope(mla_qk(l, 0))
                for h in range(4):
                    pe.matmul(PS[0:96, h, 0:SEQ], wm[:, 768 + 96 * h:864 + 96 * h], CKV[:, 0:SEQ], start=True, stop=False)
                    mm = pe.matmul(PS[0:96, h, 0:SEQ], ident[0:96, 0:96], KR[0:96, 0:SEQ], start=False, stop=True)
                mm.then_inc(S.sub_done, 1)
                norm_rope(mla_qk(l, 1))
                tokens(wm[:, 1152:1408].unsqueeze(1), 0, 256, TILES1, [(4, 0), (5, 0)], src=CKV.unsqueeze(1),
                       kt=1).then_inc(S.sub_done, 1)
                pe.wait_ge(S.v_ready, upto(S.v_ready))
                softmax(mla_soft())
                norm_rope(head_norm(l, 1))
                c = take()
                w = wat(landed(c), KD, 512)
                tiles(w, [(P * i, P, i) for i in range(4)], SEQ).then_inc(S.prod_done, 1)
                pe.wait_ge(S.qk_ready, upto(S.qk_ready))
                for kt in (1, 0):
                    R = SEQ - P * kt
                    if kt == 0:
                        pe.wait_ge(S.sb_a, upto(S.sb_a))
                    for h in range(4):
                        mm = pe.matmul(PS[:, h, 0:R], half(2 + h // 2, h)[:, P * kt:P * kt + P],
                                       half(h // 2, h)[:, P * kt:SEQ], start=True, stop=True)
                    mm.then_inc(S.sb_z, 1)
                    pe.wait_ge(S.sb_sp, upto(S.sb_sp))
                    for j in range(2):
                        o = PS[:, 4 + j, 0:2 * R].rearrange("p (h t) -> p h t", h=2)
                        own = W2 if kt == 0 else QK[:, 4:8, :]
                        mm = pe.matmul(o, C("later", P), own[:, 2 * j:2 * j + 2, 0:R], start=True, stop=kt == 1)
                        if kt == 0:
                            mm = pe.matmul(o[:, :, P:SEQ], ones, QK[:, 4 + 2 * j:6 + 2 * j, 0:P], start=False, stop=True)
                    mm.then_inc(S.sb_tail, 1)
                pe.wait_ge(S.sb_a, upto(S.sb_a))
                values(SEQ, TILES1, 4)
                norm_rope(head_norm(l, 2))
                c = take()
                w = wat(landed(c), KD, 512)
                tiles(w, [(0, P, 4), (P, P, 5), (2 * P, P, 0), (3 * P, P, 1)], SEQ).then_inc(S.prod_done, 1)
                c = take()
                w = wat(landed(c), KD, 256)
                tiles(w, [(0, P, 2), (P, P, 3)], SEQ).then_inc(S.prod_done, 1)
                pe.wait_ge(S.ssm_dt, upto(S.ssm_dt))
                pe.wait_ge(S.ssm_xc, upto(S.ssm_xc))
                for kt in range(2):
                    pe.transpose(PS[:, 7, 4 * kt:4 * kt + 4], dt_[:, P * kt:P * kt + P], ident[0:4, 0:4])
                    pe.transpose(PS[:, 7, 8 + 4 * kt:12 + 4 * kt], acum[:, P * kt:P * kt + P], ident[0:4, 0:4])
                    for n in range(2):
                        at = (2 * kt + n) * P
                        mm = pe.transpose(PS[:, 6, at:at + P], QK[:, n, P * kt:P * kt + P], ident)
                mm.then_inc(S.ssm_tr, 1)
                for h in range(4):
                    pe.matmul(PS[:, h, 0:SEQ], C("sel", 512, 4)[:, P * h:P * h + P], acum[:, 0:SEQ], start=True, stop=True)
                for kt in range(2):
                    for g in range(2):
                        lo = HD * g
                        at = 256 * kt
                        mm = pe.matmul(PS[:, 4 + g, at:at + SEQ - P * kt], QK[lo:lo + HD, 2, P * kt:P * kt + P],
                                       QK[lo:lo + HD, 3, P * kt:SEQ], start=True, stop=True)
                mm.then_inc(S.ssm_cb, 1)
                pe.wait_ge(S.ssm_m, upto(S.ssm_m, 2))
                values(SEQ, TILES1, 0)
                norm_rope(ssm_out(l))
                for j in range(2):
                    c = take()
                    w = wat(landed(c), KD, 512)
                    tiles(w, [(P * i, P, 4 * j + i) for i in range(4)], SEQ, src=MIX).then_inc(S.prod_done, 1)

            def even():
                input_norm(TT)
                for t0 in (0, 4):
                    c = take()
                    tiles(wat(landed(c), KD, 512), [(P * i, P, i) for i in range(4)], TT).then_inc(S.prod_done, 1)
                    norm_rope(qk2("evq" if t0 == 0 else "evk", 4, t0))
                c = take()
                tokens(wat(landed(c), KD, 512), 0, 512, TILES2, [(4, 0), (5, 0), (6, 0)]).then_inc(S.prod_done, 1)
                c = take()
                tiles(wat(landed(c), KD, 512), [(P * i, P, i) for i in range(4)], TT).then_inc(S.prod_done, 1)
                c = take()
                pe.wait_ge(S.v_ready, upto(S.v_ready))
                w = wat(landed(c), KD, 136)
                tiles(w, [(0, P, 4)], TT)
                tokens(w, P, 8, TILES2, [(5, 0), (5, 8), (5, 16)]).then_inc(S.prod_done, 1)
                pe.wait_ge(S.ix_ready, upto(S.ix_ready))
                pe.wait_ge(S.iw_ready, upto(S.iw_ready))
                for qt, (q0, ql) in enumerate(TILES2):
                    keys = q0 + ql
                    for g in range(2):
                        if qt or g:
                            pe.wait_ge(S.ix_relu, upto(S.ix_relu))
                        for j in range(4):
                            h = 4 * g + j
                            lo = HD * (h % 2)
                            mm = pe.matmul(PS[0:ql, j, 0:keys], IQ[lo:lo + HD, h // 2, q0:q0 + ql], IK[lo:lo + HD, 0:keys],
                                           start=True, stop=True)
                        mm.then_inc(S.ix_logit, 1)
                pe.wait_ge(S.ix_relu, upto(S.ix_relu))
                softmax(dsa_soft(0))
                softmax(dsa_soft(1))
                for k in range(2):
                    c = take()
                    tiles(wat(landed(c), KD, 512), [(P * i, P, i) for i in range(4)], TT).then_inc(S.prod_done, 1)
                    norm_rope(ret_qk(k))
                for g in range(2):
                    c = take()
                    tokens(wat(landed(c), KD, 512), 0, 512, TILES2, [(3 * g, 0), (3 * g + 1, 0), (3 * g + 2, 0)]
                           ).then_inc(S.prod_done, 1)
                pe.wait_ge(S.v_ready, upto(S.v_ready, 2))
                for g in range(2):
                    c = take()
                    tiles(wat(landed(c), KD, 512), [(P * i, P, 4 * g + i) for i in range(4)], TT).then_inc(S.prod_done, 1)
                pe.wait_ge(S.gate_ready, upto(S.gate_ready, 2))
                for g in range(2):
                    for kt, (t0, tl) in enumerate(TILES2):
                        if kt:
                            pe.wait_ge(S.rt_m, upto(S.rt_m))
                        for j in range(4):
                            h = 4 * g + j
                            mm = pe.matmul(PS[0:tl, j, 0:TT - t0], half(4 + h // 2, h)[:, t0:t0 + tl],
                                           half(h // 2, h)[:, t0:TT], start=True, stop=True)
                        mm.then_inc(S.rt_s, 1)
                    pe.wait_ge(S.rt_m, upto(S.rt_m))
                    for j in range(4):
                        for kt, (t0, tl) in enumerate(TILES2):
                            mm = pe.matmul(PS[:, 4 + j, t0:TT], VP[0:tl, kt, 4 * g + j, :], PT[0:tl, kt, j, t0:TT],
                                           start=kt == 0, stop=kt == 2)
                    mm.then_inc(S.pv_done, 1)
                    norm_rope(ret_out(g))
                for j in range(4):
                    c = take()
                    tiles(wat(landed(c), 12, 256), [(P * i, P, 2 * j + i) for i in range(2)], TT, src=MIX, kt=12
                          ).then_inc(S.prod_done, 1)

            def odd():
                input_norm(TT)
                c = take()
                tiles(wat(landed(c), KD, 512), [(P * i, P, i) for i in range(4)], TT).then_inc(S.prod_done, 1)
                norm_rope(qk2("odq", 4, 0))
                c = take()
                w = wat(landed(c), KD, 384)
                tiles(w, [(0, P, 0), (P, P, 1)], TT)
                tokens(w, 256, P, TILES2, [(7, 0), (7, P), (7, 2 * P)]).then_inc(S.prod_done, 1)
                norm_rope(qk2("odk", 2, 4))
                c = take()
                tiles(wat(landed(c), KD, 512), [(P * i, P, i) for i in range(4)], TT).then_inc(S.prod_done, 1)
                pe.wait_ge(S.v_ready, upto(S.v_ready))
                pe.wait_ge(S.dx_ready, upto(S.dx_ready))
                softmax(swa_soft(0))
                softmax(swa_soft(1))
                c = take()
                w = wat(landed(c), 4, P)
                pe.wait_ge(S.pool_y, upto(S.pool_y))
                for g in range(4):
                    mm = pe.matmul(PS[:, g, 0:TT], w[:, g, :], W2[:, g, :], start=True, stop=True)
                mm.then_inc(S.prod_done, 1)
                pe.wait_ge(S.mix_ready, upto(S.mix_ready))
                for j in range(2):
                    c = take()
                    tiles(wat(landed(c), KD, 512), [(P * i, P, 4 * j + i) for i in range(4)], TT, src=MIX
                          ).then_inc(S.prod_done, 1)

            def ffn(T):
                input_norm(T)
                c = take(NFI)

                def pair(slot, i2, r, free):
                    pe.wait_ge(S.act_done, free)
                    w = wat(slot, KD, 2 * FCH)
                    for bank, c0 in ((2 * r, P * i2), (2 * r + 1, FCH + P * i2)):
                        for k in range(KD):
                            mm = pe.matmul(PS[:, bank, 0:T], w[:, k, c0:c0 + P], H[:, k, 0:T], start=k == 0,
                                           stop=k == KD - 1)
                    mm.then_inc(S.prod_done, 1)

                with pe.Fori(0, NFI // 2) as i:
                    for s in range(2):
                        pe.wait_ge(WA[(c + s) % 2], 16 * i + 16 * ((c + s) // 2 + 1))
                        for i2 in range(2):
                            r = 2 * s + i2
                            pair((c + s) % 2, i2, r, 4 * i + (acts[0] + r - 3))
                slot = landed(c + NFI - 1)
                for i2 in range(2):
                    pair(slot, i2, i2, acts[0] + KF - 2 + i2 - 3)
                acts[0] += KF
                pe.wait_ge(S.act_done, acts[0])
                for q in range(NFO):
                    b = take_b()
                    pe.wait_ge(WB[b % 2], 16 * (b // 2 + 1))
                    w = wb[:, b % 2, :].rearrange("p (k c) -> p k c", k=KF)
                    for i2 in range(2):
                        for k in range(KF):
                            mm = pe.matmul(PS[:, 2 * q + i2, 0:T], w[:, k, P * i2:P * i2 + P], hidden[:, k, 0:T],
                                           start=k == 0, stop=k == KF - 1)
                        mm.then_inc(S.out_done, 1)

            pe.wait_ge(S.con_in, 16)
            for l in range(DEPTH):
                mixer1(l)
                ffn(SEQ)
            ffn(TT)
            even()
            ffn(TT)
            ffn(TT)
            odd()
            ffn(TT)

        @block.scalar
        def _(act):
            upto, take = counter(), chunk_counter()
            acts = [4]

            def chain(ins):
                ins.then_inc(S.act_chain, 1)
                act.wait_ge(S.act_chain, upto(S.act_chain))

            def product(c):
                act.wait_ge(S.prod_done, chunks[c][2])

            def input_norm(T, t0):
                act.wait_ge(S.x_done, upto(S.x_done))
                act.activation(H[:, :, 0:T], X[:, :, t0:t0 + T], ACT.Square).then_inc(S.squares, 1)
                act.wait_ge(S.sumsq, upto(S.sumsq))
                chain(act.activation(rstd[:, 0:T], PS[:, 7, 0:T], ACT.Ln, bias=C("eps", 1), scale=1.0 / D))
                act.activation(rstd[:, 0:T], rstd[:, 0:T], ACT.Exp, scale=-0.5).then_inc(S.rstd_ready, 1)

            def norm_rope(q):
                if not q.norm:
                    return
                src = q.src
                if isinstance(q.src, int):
                    act.wait_ge(S.nr_raw, upto(S.nr_raw))
                    src = W0[0:q.rows, 0:q.n, 0:q.T]
                act.activation(W1[0:q.rows, 0:q.n, 0:q.T], src, ACT.Square).then_inc(S.nr_sq, 1)
                act.wait_ge(S.nr_ms, upto(S.nr_ms))
                m = 1 if q.over_tiles else q.n
                w = W1[0:q.rows, 0:m, 0:q.T]
                chain(act.activation(w, PS[0:q.rows, q.ms:q.ms + m, 0:q.T], ACT.Ln, bias=C("eps", 1, q.rows),
                                     scale=1.0 / q.width))
                act.activation(w, w, ACT.Exp, scale=-0.5).then_inc(S.nr_rs, 1)

            def softmax(a):
                for qt, (q0, ql) in enumerate(a.tiles):
                    keys = q0 + ql
                    act.wait_ge(S.sm_nb, upto(S.sm_nb))
                    for h in range(4):
                        ex = act.activation(PB[0:ql, h, 0:keys], PB[0:ql, h, 0:keys], ACT.Exp, bias=negmax[0:ql, h:h + 1],
                                            scale=a.scale, accum_out=rowsum[0:ql, h:h + 1])
                    if a.sink:
                        act.activation(sinkex[0:ql, :], sinkex[0:ql, :], ACT.Exp).then_inc(S.sm_exp, 1)
                    else:
                        ex.then_inc(S.sm_exp, 1)
                    act.wait_ge(S.sm_pt, upto(S.sm_pt))
                    for kt in range(qt + 1):
                        t0, tl = a.tiles[kt]
                        cp = act.copy(PT[0:tl, kt, :, q0:q0 + ql],
                                      PS[0:tl, 4 + kt, :].rearrange("p (h q) -> p h q", h=4)[:, :, 0:ql])
                    cp.then_inc(S.sm_ptc, 1)

            def mixer1(l):
                input_norm(SEQ, META)
                take()
                norm_rope(moba_qk(l))
                take()
                softmax(moba_soft())
                norm_rope(head_norm(l, 0))
                product(take())
                act.copy(KR[0:96, 0:SEQ], PS[0:96, 3, 0:SEQ])
                act.copy(rawdt[:, 0:SEQ], PS[0:4, 7, 0:SEQ]).then_inc(S.kr_ready, 1)
                norm_rope(mla_cq(l))
                norm_rope(mla_ckv(l))
                norm_rope(mla_qk(l, 0))
                norm_rope(mla_qk(l, 1))
                softmax(mla_soft())
                norm_rope(head_norm(l, 1))
                product(take())
                act.copy(QK[:, 0:4, 0:SEQ], PS[:, 0:4, 0:SEQ]).then_inc(S.qk_ready, 1)
                for kt in (1, 0):
                    R = SEQ - P * kt
                    w = W1[:, :, 0:R]
                    act.wait_ge(S.sb_na, upto(S.sb_na))
                    chain(act.activation(w, w, ACT.Exp))
                    act.activation(w, w, ACT.Ln, bias=1.0).then_inc(S.sb_l, 1)
                    act.wait_ge(S.sb_arg, upto(S.sb_arg))
                    act.activation(w, W0[:, :, 0:R], ACT.Exp).then_inc(S.sb_e, 1)
                norm_rope(head_norm(l, 2))
                product(take())
                product(take())
                act.activation(ZS[:, :, 0:SEQ], PS[:, 4:6, 0:SEQ], ACT.Silu)
                for n in range(4):
                    ins = act.activation(W0[:, n, 0:SEQ], PS[:, n, 0:SEQ], ACT.Identity, bias=A(f"ssmb{l}", n),
                                         scale=A(f"ssmw{l}", 4 * n + 3))
                ins.then_inc(S.ssm_init, 1)
                act.wait_ge(S.ssm_conv, upto(S.ssm_conv))
                act.activation(QK[:, 0:4, 0:SEQ], W0[:, :, 0:SEQ], ACT.Silu).then_inc(S.ssm_xc, 1)
                act.wait_ge(S.ssm_na, upto(S.ssm_na))
                chain(act.activation(dts[:, 0:SEQ], dts[:, 0:SEQ], ACT.Exp))
                act.activation(dts[:, 0:SEQ], dts[:, 0:SEQ], ACT.Ln, bias=1.0)
                act.activation(ea, A(f"alog{l}", 0, 4), ACT.Exp).then_inc(S.ssm_l, 1)
                for kt in range(2):
                    R = SEQ - P * kt
                    act.wait_ge(S.ssm_arg, upto(S.ssm_arg))
                    act.activation(W1[:, :, 0:R], W0[:, :, 0:R], ACT.Exp).then_inc(S.ssm_e, 1)
                act.wait_ge(S.ssm_y, upto(S.ssm_y))
                norm_rope(ssm_out(l))
                take(2)

            def even():
                input_norm(TT, 0)
                take()
                norm_rope(qk2("evq", 4, 0))
                take()
                norm_rope(qk2("evk", 4, 4))
                take()
                product(take())
                act.copy(IQ[:, :, :], PS[:, 0:4, 0:TT])
                product(take())
                act.copy(IK, PS[:, 4, 0:TT]).then_inc(S.ix_ready, 1)
                for qt, (q0, ql) in enumerate(TILES2):
                    for g in range(2):
                        act.wait_ge(S.ix_logit, upto(S.ix_logit))
                        if qt or g:
                            act.wait_ge(S.ix_acc, upto(S.ix_acc))
                        act.activation(W0[0:ql, :, 0:q0 + ql], PS[0:ql, 0:4, 0:q0 + ql], ACT.Relu).then_inc(S.ix_relu, 1)
                upto(S.ix_acc)
                softmax(dsa_soft(0))
                softmax(dsa_soft(1))
                take(2)
                take(2)
                for g in range(2):
                    product(take())
                    act.activation(G[:, 4 * g:4 * g + 4, :], PS[:, 4 * g:4 * g + 4, 0:TT], ACT.Silu).then_inc(S.gate_ready, 1)
                for g in range(2):
                    norm_rope(ret_out(g))
                take(4)

            def odd():
                input_norm(TT, 0)
                take()
                norm_rope(qk2("odq", 4, 0))
                take()
                norm_rope(qk2("odk", 2, 4))
                product(take())
                act.copy(IQ[:, :, :], PS[:, 0:4, 0:TT]).then_inc(S.dx_ready, 1)
                softmax(swa_soft(0))
                softmax(swa_soft(1))
                take(3)

            def ffn(T, t0, conv=None):
                input_norm(T, t0)
                c = take(NFI)
                done = chunks[c][2] - 2

                def pair(i, r):
                    act.wait_ge(S.prod_done, i + (done + r + 1))
                    act.wait_ge(S.act_done, i + (acts[0] + r - 1))
                    if conv is None:
                        act.activation(W0[:, r % 2, 0:T], PS[:, 2 * r, 0:T], ACT.Silu).then_inc(S.silu_done, 1)
                        return
                    for j in range(2):
                        at = PC[conv] + 4 * j
                        tap = par[:, bass.ds(i * 8 + (8 * r + at + 2), 1)]
                        bias = par[:, bass.ds(i * 8 + (8 * r + at + 3), 1)]
                        ins = act.activation(W1[:, 2 * (r % 2) + j, 0:T], PS[:, 2 * r + j, 0:T], ACT.Identity, bias=bias,
                                             scale=tap)
                    ins.then_inc(S.conv_init, 1)
                    act.wait_ge(S.conv_done, i + (convs[0] + r + 1))
                    act.activation(W0[:, r % 2, 0:T], W1[:, 2 * (r % 2), 0:T], ACT.Silu).then_inc(S.silu_done, 1)

                with act.Fori(0, NFI // 2) as i:
                    for r in range(4):
                        pair(4 * i, r)
                for r in range(2):
                    pair(KF - 2, r)
                acts[0] += KF
                if conv is not None:
                    convs[0] += KF

            convs = [0]
            act.wait_ge(S.par_in, 16)
            act.wait_ge(S.con_in, 16)
            act.wait_ge(S.rope_ang, 1)
            for j in range(2):
                act.activation(rope[:, 2 * j + 1, :], W1[:, j, 0:SEQ], ACT.Sin)
                ins = act.activation(rope[:, 2 * j, :], W2[:, j, 0:SEQ], ACT.Sin, bias=C("halfpi", 1), scale=-1.0)
            ins.then_inc(S.rope_ready, 1)
            upto(S.rope_ang)
            for l in range(DEPTH):
                mixer1(l)
                ffn(SEQ, META, f"fconv{l}")
            ffn(TT, 0)
            even()
            ffn(TT, 0)
            ffn(TT, 0)
            odd()
            ffn(TT, 0)

        @block.vector
        def _(dve):
            upto, take = counter(), chunk_counter()
            acts, convs, silus = [4], [0], [0]

            def chain(ins):
                ins.then_inc(S.dve_chain, 1)
                dve.wait_ge(S.dve_chain, upto(S.dve_chain))

            def product(c):
                dve.wait_ge(S.prod_done, chunks[c][2])

            def input_norm(T, t0, gain):
                dve.wait_ge(S.rstd_ready, upto(S.rstd_ready))
                for k in range(KD):
                    ins = dve.scalar_tensor_tensor(out=H[:, k, 0:T], in0=X[:, k, t0:t0 + T], scalar=A(gain, k),
                                                   in1=rstd[:, 0:T], op0=ALU.mult, op1=ALU.mult)
                ins.then_inc(S.h_ready, 1)

            def norm_rope(q):
                w0, w1, w2 = (w[0:q.rows, 0:q.n, 0:q.T] for w in (W0, W1, W2))
                tail = q.rot or q.post is not None
                if q.norm:
                    if isinstance(q.src, int):
                        dve.tensor_copy(w0, PS[0:q.rows, q.src:q.src + q.n, 0:q.T]).then_inc(S.nr_raw, 1)
                    dve.wait_ge(S.nr_rs, upto(S.nr_rs))
                    for i in range(q.n):
                        rs = W1[0:q.rows, 0 if q.over_tiles else i, 0:q.T]
                        o = (W2[0:q.rows, i, 0:q.T] if tail else q.dst[:, i, :])
                        if q.gains:
                            ins = dve.scalar_tensor_tensor(out=o, in0=W0[0:q.rows, i, 0:q.T], scalar=q.gains[i], in1=rs,
                                                           op0=ALU.mult, op1=ALU.mult)
                        else:
                            ins = dve.tensor_tensor(out=o, in0=W0[0:q.rows, i, 0:q.T], in1=rs, op=ALU.mult)
                else:
                    ins = dve.tensor_copy(w2, PS[0:q.rows, q.src:q.src + q.n, 0:q.T])
                if not tail:
                    ins.then_inc(S.nr_done, 1)
                    dve.wait_ge(S.nr_done, upto(S.nr_done))
                    return
                if q.rot:
                    ins.then_inc(S.nr_n, 1)
                    _, cos, sin = q.rot
                    dve.wait_ge(S.nr_rot, upto(S.nr_rot))
                    dve.tensor_tensor(out=w0, in0=w2, in1=per_head(cos, q.n), op=ALU.mult)
                    chain(dve.tensor_tensor(out=w1, in0=PS[0:q.rows, 0:q.n, 0:q.T], in1=per_head(sin, q.n), op=ALU.mult))
                    if q.post is None:
                        dve.tensor_tensor(out=q.dst, in0=w0, in1=w1, op=ALU.add).then_inc(S.nr_done, 1)
                        dve.wait_ge(S.nr_done, upto(S.nr_done))
                        return
                    chain(dve.tensor_tensor(out=w2, in0=w0, in1=w1, op=ALU.add))
                else:
                    chain(ins)
                dve.tensor_tensor(out=q.dst, in0=w2, in1=q.post, op=ALU.mult).then_inc(S.nr_done, 1)
                dve.wait_ge(S.nr_done, upto(S.nr_done))

            def softmax(a):
                for qt, (q0, ql) in enumerate(a.tiles):
                    keys = q0 + ql
                    pb = PB[0:ql, :, 0:keys]
                    dve.wait_ge(S.sm_qk, upto(S.sm_qk))
                    if qt:
                        dve.wait_ge(S.sm_pt, upto(S.sm_pt))
                    chain(dve.tensor_tensor(out=pb, in0=PS[0:ql, 0:4, 0:keys], in1=per_head(a.masks[qt][0:ql, 0:keys], 4),
                                            op=ALU.add))
                    chain(dve.tensor_reduce(out=negmax[0:ql, :], in_=pb, axis=AX.X, op=ALU.max))
                    if a.sink:
                        sk = par[0:ql, PC["sink"] + a.head0:PC["sink"] + a.head0 + 4]
                        chain(dve.tensor_scalar(negmax[0:ql, :], negmax[0:ql, :], a.scale, None, ALU.mult))
                        chain(dve.tensor_tensor(out=negmax[0:ql, :], in0=negmax[0:ql, :], in1=sk, op=ALU.max))
                        chain(dve.tensor_scalar(negmax[0:ql, :], negmax[0:ql, :], -1.0, None, ALU.mult))
                        dve.tensor_tensor(out=sinkex[0:ql, :], in0=negmax[0:ql, :], in1=sk, op=ALU.add).then_inc(S.sm_nb, 1)
                    else:
                        dve.tensor_scalar(negmax[0:ql, :], negmax[0:ql, :], -a.scale, None, ALU.mult).then_inc(S.sm_nb, 1)
                    dve.wait_ge(S.sm_exp, upto(S.sm_exp))
                    if a.sink:
                        chain(dve.tensor_tensor(out=rowsum[0:ql, :], in0=rowsum[0:ql, :], in1=sinkex[0:ql, :], op=ALU.add))
                    chain(dve.reciprocal(rowsum[0:ql, :], rowsum[0:ql, :]))
                    dve.tensor_tensor(out=pb, in0=pb, in1=rowsum[0:ql, :].unsqueeze(2).to_broadcast([ql, 4, keys]),
                                      op=ALU.mult).then_inc(S.sm_p, 1)
                upto(S.sm_pt)
                if a.copy_to is not None:
                    dve.wait_ge(S.pv_done, upto(S.pv_done))
                    dve.tensor_copy(a.copy_to, PS[:, 0:2, 0:a.T]).then_inc(S.pv_copied, 1)

            def copy_heads(rows, kt, head0, n, src):
                s = src.rearrange("p (h d) -> p h d", h=n)
                dve.tensor_copy(VP[0:rows, kt, head0:head0 + n:2, 0:HD], s[:, 0:n:2, :])
                return dve.tensor_copy(VP[0:rows, kt, head0 + 1:head0 + n:2, HD:P], s[:, 1:n:2, :])

            def mixer1(l):
                input_norm(SEQ, META, f"mixg{l}")
                product(take())
                norm_rope(moba_qk(l))
                product(take())
                for kt in range(2):
                    ins = copy_heads(P, kt, 0, 8, PS[:, 4 + kt, :])
                ins.then_inc(S.v_ready, 1)
                softmax(moba_soft())
                dve.wait_ge(S.pv_done, upto(S.pv_done))
                norm_rope(head_norm(l, 0))
                product(take())
                norm_rope(mla_cq(l))
                norm_rope(mla_ckv(l))
                dve.wait_ge(S.sub_done, upto(S.sub_done))
                norm_rope(mla_qk(l, 0))
                dve.wait_ge(S.sub_done, upto(S.sub_done))
                norm_rope(mla_qk(l, 1))
                dve.wait_ge(S.sub_done, upto(S.sub_done))
                for kt in range(2):
                    ins = copy_heads(P, kt, 0, 4, PS[:, 4 + kt, 0:256])
                ins.then_inc(S.v_ready, 1)
                softmax(mla_soft())
                dve.wait_ge(S.pv_done, upto(S.pv_done))
                norm_rope(head_norm(l, 1))
                take()
                for kt in (1, 0):
                    R = SEQ - P * kt
                    w0, w1 = W0[:, :, 0:R], W1[:, :, 0:R]
                    sp_ = (W2 if kt == 0 else QK[:, 4:8, :])[:, :, 0:R]
                    strict = per_head(C("strict", SEQ)[:, 0:R], 4)
                    dve.wait_ge(S.sb_z, upto(S.sb_z))
                    chain(dve.tensor_scalar(w0, PS[:, 0:4, 0:R], HD ** -0.5, None, ALU.mult))
                    dve.scalar_tensor_tensor(out=w1, in0=w0, scalar=-1.0, in1=w0, op0=ALU.mult,
                                             op1=ALU.min).then_inc(S.sb_na, 1)
                    dve.wait_ge(S.sb_l, upto(S.sb_l))
                    chain(dve.scalar_tensor_tensor(out=sp_, in0=w0, scalar=0.0, in1=w1, op0=ALU.max, op1=ALU.add))
                    dve.tensor_tensor(out=sp_, in0=sp_, in1=strict, op=ALU.mult).then_inc(S.sb_sp, 1)
                    chain(dve.scalar_tensor_tensor(out=w0, in0=w0, scalar=0.0, in1=w1, op0=ALU.min, op1=ALU.subtract))
                    dve.wait_ge(S.sb_tail, upto(S.sb_tail))
                    for j in range(2):
                        ins = dve.tensor_tensor(out=W0[:, 2 * j:2 * j + 2, 0:R], in0=W0[:, 2 * j:2 * j + 2, 0:R],
                                                in1=PS[:, 4 + j, 0:2 * R].rearrange("p (h t) -> p h t", h=2),
                                                op=ALU.subtract)
                    ins.then_inc(S.sb_arg, 1)
                    dve.wait_ge(S.sb_e, upto(S.sb_e))
                    dve.tensor_tensor(out=PT[:, kt, :, P * kt:SEQ], in0=w1, in1=strict, op=ALU.mult).then_inc(S.sb_a, 1)
                    dve.wait_ge(S.sb_a, upto(S.sb_a))
                dve.wait_ge(S.pv_done, upto(S.pv_done))
                norm_rope(head_norm(l, 2))
                take(2)
                chain(dve.tensor_scalar(rawdt[:, 0:SEQ], rawdt[:, 0:SEQ], A(f"dtb{l}", 0, 4), None, ALU.add))
                dve.scalar_tensor_tensor(out=dts[:, 0:SEQ], in0=rawdt[:, 0:SEQ], scalar=-1.0, in1=rawdt[:, 0:SEQ],
                                         op0=ALU.mult, op1=ALU.min).then_inc(S.ssm_na, 1)
                dve.wait_ge(S.ssm_init, upto(S.ssm_init))
                for s in range(1, 4):
                    for n in range(4):
                        ins = dve.scalar_tensor_tensor(out=W0[:, n, s:SEQ], in0=PS[:, n, 0:SEQ - s],
                                                       scalar=A(f"ssmw{l}", 4 * n + 3 - s), in1=W0[:, n, s:SEQ],
                                                       op0=ALU.mult, op1=ALU.add)
                    if s < 3:
                        chain(ins)
                ins.then_inc(S.ssm_conv, 1)
                dve.wait_ge(S.ssm_l, upto(S.ssm_l))
                chain(dve.scalar_tensor_tensor(out=dt_[:, 0:SEQ], in0=rawdt[:, 0:SEQ], scalar=0.0, in1=dts[:, 0:SEQ],
                                               op0=ALU.max, op1=ALU.add))
                chain(dve.tensor_scalar(dts[:, 0:SEQ], dt_[:, 0:SEQ], ea, -1.0, ALU.mult, ALU.mult))
                dve.tensor_tensor_scan(acum[:, 0:SEQ], C("ones", P, 4)[:, 0:1].to_broadcast([4, SEQ]), dts[:, 0:SEQ], 0.0,
                                       ALU.mult, ALU.add).then_inc(S.ssm_dt, 1)
                dve.wait_ge(S.ssm_tr, upto(S.ssm_tr))
                chain(dve.tensor_copy(cols, PS[:, 7, 0:16]))
                for kt in range(2):
                    copy_heads(P, kt, 0, 4, PS[:, 6, 256 * kt:256 * kt + 256])
                dve.wait_ge(S.ssm_cb, upto(S.ssm_cb))
                for kt in range(2):
                    R = SEQ - P * kt
                    for h in range(4):
                        ins = dve.scalar_tensor_tensor(out=W0[:, h, 0:R], in0=PS[:, h, P * kt:SEQ],
                                                       scalar=cols[:, 8 + 4 * kt + h:9 + 4 * kt + h],
                                                       in1=C("ssmmask", SEQ)[:, 0:R], op0=ALU.subtract, op1=ALU.min)
                    ins.then_inc(S.ssm_arg, 1)
                    dve.wait_ge(S.ssm_e, upto(S.ssm_e))
                    for h in range(4):
                        ins = dve.scalar_tensor_tensor(out=PT[:, kt, h, P * kt:SEQ],
                                                       in0=PS[:, 4 + h // 2, 256 * kt:256 * kt + R],
                                                       scalar=cols[:, 4 * kt + h:4 * kt + h + 1], in1=W1[:, h, 0:R],
                                                       op0=ALU.mult, op1=ALU.mult)
                    ins.then_inc(S.ssm_m, 1)
                dve.wait_ge(S.pv_done, upto(S.pv_done))
                for n in range(2):
                    ins = dve.scalar_tensor_tensor(out=W0[:, n, 0:SEQ], in0=QK[:, n, 0:SEQ], scalar=A(f"dskip{l}", n),
                                                   in1=PS[:, n, 0:SEQ], op0=ALU.mult, op1=ALU.add)
                chain(ins)
                dve.tensor_tensor(out=W0[:, 0:2, 0:SEQ], in0=W0[:, 0:2, 0:SEQ], in1=ZS[:, :, 0:SEQ],
                                  op=ALU.mult).then_inc(S.ssm_y, 1)
                dve.wait_ge(S.ssm_y, upto(S.ssm_y))
                norm_rope(ssm_out(l))
                for j in range(2):
                    product(take())
                    xs = X[:, 4 * j:4 * j + 4, META:TT]
                    ins = dve.tensor_tensor(out=xs, in0=xs, in1=PS[:, 4 * j:4 * j + 4, 0:SEQ], op=ALU.add)
                ins.then_inc(S.x_done, 1)

            def even():
                input_norm(TT, 0, "mix2g0")
                product(take())
                norm_rope(qk2("evq", 4, 0))
                product(take())
                norm_rope(qk2("evk", 4, 4))
                product(take())
                for kt, (t0, tl) in enumerate(TILES2):
                    ins = copy_heads(tl, kt, 0, 8, PS[0:tl, 4 + kt, :])
                ins.then_inc(S.v_ready, 1)
                take()
                product(take())
                for qt, (q0, ql) in enumerate(TILES2):
                    ins = dve.tensor_scalar(iwc[0:ql, 8 * qt:8 * qt + 8], PS[0:ql, 5, 8 * qt:8 * qt + 8],
                                            8 ** -0.5 * HD ** -0.5, None, ALU.mult)
                ins.then_inc(S.iw_ready, 1)
                dve.wait_ge(S.iw_ready, upto(S.iw_ready))
                dve.wait_ge(S.mask_in, 16)
                for qt, (q0, ql) in enumerate(TILES2):
                    keys = q0 + ql
                    sc, adm, pk = W2[0:ql, 0, 0:keys], mask[0:ql, qt, 0:keys], picked[0:ql, qt, 0:keys]
                    for g in range(2):
                        dve.wait_ge(S.ix_relu, upto(S.ix_relu))
                        for j in range(4):
                            h = 4 * g + j
                            ins = dve.scalar_tensor_tensor(out=sc, in0=W0[0:ql, j, 0:keys],
                                                           scalar=iwc[0:ql, 8 * qt + h:8 * qt + h + 1],
                                                           in1=adm if h == 0 else sc, op0=ALU.mult, op1=ALU.add)
                            if j < 3:
                                chain(ins)
                        ins.then_inc(S.ix_acc, 1)
                        dve.wait_ge(S.ix_acc, upto(S.ix_acc))
                    for _ in range(TOPK // 8):
                        chain(dve.max(out=top8[0:ql, :], in_=sc))
                        chain(dve.match_replace(out=sc, in_to_replace=top8[0:ql, :], in_values=sc, imm_value=TAKEN))
                    chain(dve.tensor_scalar(pk, sc, TAKEN / 2, NEG, ALU.is_ge, ALU.mult))
                    dve.tensor_tensor(out=pk, in0=pk, in1=adm, op=ALU.add).then_inc(S.picked_ready, 1)
                    dve.wait_ge(S.picked_ready, upto(S.picked_ready))
                softmax(dsa_soft(0))
                softmax(dsa_soft(1))
                for k in range(2):
                    product(take())
                    norm_rope(ret_qk(k))
                for g in range(2):
                    product(take())
                    for kt, (t0, tl) in enumerate(TILES2):
                        ins = dve.tensor_copy(VP[0:tl, kt, 4 * g:4 * g + 4, :],
                                              PS[0:tl, 3 * g + kt, :].rearrange("p (h d) -> p h d", h=4))
                    ins.then_inc(S.v_ready, 1)
                take(2)
                for g in range(2):
                    for kt, (t0, tl) in enumerate(TILES2):
                        dve.wait_ge(S.rt_s, upto(S.rt_s))
                        for j in range(4):
                            at = CC["kdec"] + 8 * kt + 4 * g + j
                            ins = dve.scalar_tensor_tensor(out=PT[0:tl, kt, j, t0:TT], in0=PS[0:tl, j, 0:TT - t0],
                                                           scalar=con[0:tl, at:at + 1], in1=C("tri", TT)[0:tl, 0:TT - t0],
                                                           op0=ALU.mult, op1=ALU.mult)
                        ins.then_inc(S.rt_m, 1)
                    dve.wait_ge(S.pv_done, upto(S.pv_done))
                    if g == 0:
                        dve.wait_ge(S.gate_ready, upto(S.gate_ready, 2))
                    norm_rope(ret_out(g))
                for j in range(4):
                    product(take())
                    xs = X[:, 2 * j:2 * j + 2, :]
                    ins = dve.tensor_tensor(out=xs, in0=xs, in1=PS[:, 2 * j:2 * j + 2, 0:TT], op=ALU.add)
                ins.then_inc(S.x_done, 1)

            def odd():
                dve.memset(VP[:], 0.0).then_inc(S.v_zero, 1)
                dve.wait_ge(S.v_zero, upto(S.v_zero))
                input_norm(TT, 0, "mix2g1")
                product(take())
                norm_rope(qk2("odq", 4, 0))
                product(take())
                for kt, (t0, tl) in enumerate(TILES2):
                    for g in range(2):
                        src = PS[0:tl, 7, P * kt + HD * g:P * kt + HD * g + HD].unsqueeze(1).to_broadcast([tl, 2, HD])
                        dve.tensor_copy(VP[0:tl, kt, 4 * g:4 * g + 4:2, 0:HD], src)
                        dve.tensor_copy(VP[0:tl, kt, 4 * g + 1:4 * g + 4:2, HD:P], src)
                norm_rope(qk2("odk", 2, 4))
                take()
                dve.memset(small[:, 0:1], 0.0).then_inc(S.v_ready, 1)
                dve.wait_ge(S.dx_ready, upto(S.dx_ready))
                dve.wait_ge(S.swa_in, 16)
                src, bufs = IQ, [W0, W1, W0, W1]
                for lv, w in enumerate(bufs):
                    s = 1 << lv
                    dve.tensor_copy(w[:, lv:4, 0:s], src[:, lv:4, 0:s])
                    chain(dve.tensor_tensor(out=w[:, lv:4, s:TT], in0=src[:, lv:4, s:TT], in1=src[:, lv:4, 0:TT - s],
                                            op=ALU.add))
                    fix = C("cfix", 64)[:, 16 * lv:16 * lv + 16]
                    dve.tensor_copy(W2[:, lv, 16:TT], w[:, lv, 16:TT])
                    chain(dve.tensor_tensor(out=W2[:, lv, 0:16], in0=w[:, lv, 0:16], in1=fix, op=ALU.mult))
                    ins = dve.scalar_tensor_tensor(out=W2[:, lv, :], in0=W2[:, lv, :], scalar=1.0 / (2 << lv),
                                                   in1=IQ[:, lv, :], op0=ALU.mult, op1=ALU.subtract)
                    src = w
                ins.then_inc(S.pool_y, 1)
                softmax(swa_soft(0))
                softmax(swa_soft(1))
                product(take())
                for g in range(4):
                    ins = dve.tensor_scalar(MIX[:, 4 + g, :], PS[:, g, 0:TT], A("dscale", g), None, ALU.mult)
                ins.then_inc(S.mix_ready, 1)
                for j in range(2):
                    product(take())
                    xs = X[:, 4 * j:4 * j + 4, :]
                    ins = dve.tensor_tensor(out=xs, in0=xs, in1=PS[:, 4 * j:4 * j + 4, 0:TT], op=ALU.add)
                ins.then_inc(S.x_done, 1)

            def ffn(T, t0, gain, scale, conv=None):
                input_norm(T, t0, gain)
                take(NFI)

                def pair(i, r, at):
                    if conv is not None:
                        dve.wait_ge(S.conv_init, i + (convs[0] + r + 1))
                        for s in (1, 2):
                            for j in range(2):
                                tap = par[:, bass.ds(i * 8 + (8 * r + PC[conv] + 4 * j + 2 - s), 1)]
                                w = W1[:, 2 * (r % 2) + j, s:T]
                                ins = dve.scalar_tensor_tensor(out=w, in0=PS[:, 2 * r + j, 0:T - s], scalar=tap, in1=w,
                                                               op0=ALU.mult, op1=ALU.add)
                            if s == 1:
                                ins.then_inc(S.dve_chain, 1)
                                dve.wait_ge(S.dve_chain, i + (chains[0] + r + 1))
                        ins.then_inc(S.conv_done, 1)
                    dve.wait_ge(S.silu_done, i + (silus[0] + r + 1))
                    up = PS[:, 2 * r + 1, 0:T] if conv is None else W1[:, 2 * (r % 2) + 1, 0:T]
                    dve.tensor_tensor(out=at, in0=W0[:, r % 2, 0:T], in1=up, op=ALU.mult).then_inc(S.act_done, 1)

                chains = [upto(S.dve_chain, 0)]
                with dve.Fori(0, NFI // 2) as i:
                    for r in range(4):
                        pair(4 * i, r, hidden[:, bass.ds(4 * i + r, 1), 0:T].rearrange("p o t -> p (o t)"))
                for r in range(2):
                    pair(KF - 2, r, hidden[:, KF - 2 + r, 0:T])
                silus[0] += KF
                if conv is not None:
                    convs[0] += KF
                    upto(S.dve_chain, KF)
                for m in range(KD):
                    dve.wait_ge(S.out_done, upto(S.out_done))
                    xs = X[:, m, t0:t0 + T]
                    ins = dve.scalar_tensor_tensor(out=xs, in0=PS[:, m, 0:T], scalar=scale, in1=xs, op0=ALU.mult,
                                                   op1=ALU.add)
                ins.then_inc(S.x_done, 1)

            for h in range(0, 8, 2):
                dve.memset(VP[:, :, h:h + 2, :], 0.0).then_inc(S.act_done, 1)
            dve.wait_ge(S.act_done, 4)
            dve.wait_ge(S.con_in, 16)
            dve.wait_ge(S.par_in, 16)
            dve.wait_ge(S.pos_in, 16)
            pos, turns, ang, mag = W0[:, 0, 0:SEQ], W0[:, 1, 0:SEQ], W1, W2
            chain(dve.tensor_copy(pos, posi[:]))
            two_pi = 2 * np.pi
            c1 = 6.28125
            c2 = float(np.float32(int((two_pi - c1) * 2 ** 20) / 2 ** 20))
            c3 = float(np.float32(two_pi - c1 - c2))
            magic = float(1.5 * 2 ** 23)
            for j in range(2):
                a, m = ang[:, j, 0:SEQ], mag[:, j, 0:SEQ]
                chain(dve.tensor_scalar(a, pos, C("inv", 2)[:, j:j + 1], None, ALU.mult))
                chain(dve.tensor_scalar(turns, a, float(1 / two_pi), magic, ALU.mult, ALU.add))
                chain(dve.tensor_scalar(turns, turns, magic, None, ALU.subtract))
                for part in (c1, c2, c3):
                    chain(dve.scalar_tensor_tensor(out=a, in0=turns, scalar=-part, in1=a, op0=ALU.mult, op1=ALU.add))
                chain(dve.tensor_scalar(a, a, 3.1415925, -3.1415925, ALU.min, ALU.max))
                ins = dve.scalar_tensor_tensor(out=m, in0=a, scalar=-1.0, in1=a, op0=ALU.mult, op1=ALU.max)
            ins.then_inc(S.rope_ang, 1)
            dve.wait_ge(S.rope_ready, 1)
            dve.wait_ge(S.x_in, 32)
            dve.memset(rstd[:], 0.0).then_inc(S.x_done, 1)
            for l in range(DEPTH):
                mixer1(l)
                ffn(SEQ, META, f"ffng{l}", 1.0, conv=f"fconv{l}")
            ffn(TT, 0, "ffn1g0", 0.5)
            even()
            ffn(TT, 0, "ffn2g0", 0.5)
            ffn(TT, 0, "ffn1g1", 0.5)
            odd()
            ffn(TT, 0, "ffn2g1", 0.5)


def tile_rows(w, rows=P):
    k = w.shape[0] // rows
    out = np.zeros((P, k, w.shape[1]), w.dtype)
    out[:rows] = w.reshape(k, rows, w.shape[1]).transpose(1, 0, 2)
    return out.reshape(P, -1)


def layout_weights(i):
    mix = []

    def add(w, rows=P):
        mix.append(tile_rows(w, rows).ravel())

    for l in range(DEPTH):
        w = i["w_in"][l]
        moba, mla, sbk, ssm = 0, 768, 1120, 1888
        add(w[:, moba:moba + 512])
        add(np.concatenate([w[:, moba + 512:moba + 768], w[:, sbk + 512:sbk + 768]], 1))
        pad = np.zeros((D, 64), w.dtype)
        add(np.concatenate([w[:, mla:mla + 320], pad, w[:, mla + 320:mla + 352], w[:, ssm + 768:ssm + 772]], 1))
        add(w[:, sbk:sbk + 512])
        add(w[:, ssm:ssm + 512])
        add(w[:, ssm + 512:ssm + 768])
        for j in range(2):
            add(i["w_out"][l][:, 512 * j:512 * j + 512])
    w = i["ev_w_in_2"][0]
    for c0 in (0, 512, 1024, 1536):
        add(w[:, c0:c0 + 512])
    add(np.concatenate([w[:, 2048:2112], w[:, 2048:2112], w[:, 2112:2120]], 1))
    for c0 in range(2120, 2120 + 3072, 512):
        add(w[:, c0:c0 + 512])
    for j in range(4):
        add(i["ev_w_out_2"][0][:, 256 * j:256 * j + 256])
    w = i["od_w_in_2"][0]
    add(w[:, 0:512])
    add(np.concatenate([w[:, 512:576]] * 2 + [w[:, 576:640]] * 2 + [w[:, 640:768]], 1))
    add(w[:, 768:1280])
    add(i["od_d_mix_2"][0].transpose(1, 0, 2).reshape(P, 512))
    for j in range(2):
        add(i["od_w_out_2"][0][:, 512 * j:512 * j + 512])
    ins = [i["ffn_w_in"][0], i["ffn_w_in"][1], i["ffn1_w_in_2"][0], i["ffn2_w_in_2"][0], i["ffn1_w_in_2"][1], i["ffn2_w_in_2"][1]]
    outs = [i["ffn_w_out"][0], i["ffn_w_out"][1], i["ffn1_w_out_2"][0], i["ffn2_w_out_2"][0], i["ffn1_w_out_2"][1],
            i["ffn2_w_out_2"][1]]
    wfi = np.stack([tile_rows(np.concatenate([w[:, FCH * j:FCH * j + FCH], w[:, FF + FCH * j:FF + FCH * j + FCH]], 1))
                    for w in ins for j in range(NFI)])
    wfo = np.stack([tile_rows(w[:, OCH * j:OCH * j + OCH]) for w in outs for j in range(NFO)])
    wmla = []
    for l in range(DEPTH):
        kv = i["mla_w_ukv"][l].reshape(P, 4, 128)
        wmla.append(np.concatenate([
            tile_rows(i["mla_w_uq"][l], 96),
            np.pad(kv[:, :, 0:64], ((0, 0), (0, 0), (0, 32))).reshape(P, 384),
            kv[:, :, 64:128].reshape(P, 256)], 1))
    return np.concatenate(mix), wfi, wfo, np.stack(wmla)


def layout_params(i):
    par = np.zeros((P, PC["end"]), np.float32)

    def put(name, a, at=0):
        a = np.asarray(a)
        par[:a.shape[1], PC[name] + at:PC[name] + at + a.shape[0]] = a.T

    for l in range(DEPTH):
        put(f"mixg{l}", i["mix_norm_g"][l].reshape(8, P))
        put(f"ffng{l}", i["ffn_norm_g"][l].reshape(8, P))
        put(f"mobaq{l}", np.tile(i["moba_qk_g"][l, 0], 2)[None])
        put(f"mobak{l}", np.tile(i["moba_qk_g"][l, 1], 2)[None])
        put(f"mlacq{l}", i["mla_q_norm_g"][l].reshape(2, 96))
        put(f"mlackv{l}", i["mla_kv_norm_g"][l][None])
        put(f"mlaq{l}", i["mla_qk_g"][l, 0][None])
        put(f"mlak{l}", i["mla_qk_g"][l, 1][None])
        put(f"ssmw{l}", i["ssm_conv_w"][l].reshape(4, 4, P).transpose(1, 0, 2).reshape(16, P))
        put(f"ssmb{l}", i["ssm_conv_b"][l].reshape(4, P))
        put(f"dtb{l}", i["ssm_dt_bias"][l][None])
        put(f"alog{l}", i["ssm_a_log"][l][None])
        put(f"dskip{l}", np.repeat(i["ssm_d"][l], HD).reshape(2, P))
        put(f"ssmg{l}", i["ssm_norm_g"][l].reshape(2, P))
        put(f"headg{l}", i["head_out_g"][l].reshape(6, P))
        taps = np.concatenate([i["ffn_conv_w"][l], i["ffn_conv_b"][l][None]]).reshape(4, 2, KF, P).transpose(2, 1, 0, 3)
        put(f"fconv{l}", taps.reshape(KF * 8, P))
        put(f"ffn1g{l}", i["ffn1_norm_2"][l].reshape(8, P))
        put(f"mix2g{l}", i["mix_norm_2"][l].reshape(8, P))
        put(f"ffn2g{l}", i["ffn2_norm_2"][l].reshape(8, P))
    for name, key in (("evq", "ev_a_q_norm_2"), ("evk", "ev_a_k_norm_2"), ("odq", "od_c_q_norm_2"), ("odk", "od_c_k_norm_2")):
        put(name, np.tile(i[key][0], 2)[None])
    put("sink", np.repeat(i["od_c_sinks_2"][0][:, None], P, 1))
    put("dscale", i["od_d_scale_2"][0].reshape(4, P))
    return par


def kernel(**inputs):
    import concourse.bacc as bacc
    from concourse.bass_utils import run_bass_kernel_spmd

    i = {k: np.asarray(v) for k, v in inputs.items()}
    wmix, wfi, wfo, wmla = layout_weights(i)

    def features(x):
        return x.T.reshape(KD, P, x.shape[0]).transpose(1, 0, 2).reshape(P, -1)

    arrays = {
        "wmix": wmix, "wfi": wfi, "wfo": wfo, "wmla": wmla, "params": layout_params(i), "consts": constants(),
        "masks": chunk_masks(), "xin": np.concatenate([features(i["x"][0]), features(i["meta_tokens_2"])], 1),
        "pos": i["positions"],
    }
    nc = bacc.Bacc("TRN2", target_bir_lowering=False, num_devices=1)
    arrays = {f"in_{n}": np.ascontiguousarray(a) for n, a in arrays.items()}
    args = [nc.dram_tensor(n, a.shape, mybir.dt.from_np(a.dtype), kind="ExternalInput").ap() for n, a in arrays.items()]
    out = nc.dram_tensor("out_y", (P, KD, SEQ), F32, kind="ExternalOutput").ap()
    build_program(nc, *args, out)
    r = run_bass_kernel_spmd(nc, [arrays], core_ids=[0])
    y = r.results[0]["out_y"]
    return y.transpose(1, 0, 2).reshape(D, SEQ).T.reshape(1, SEQ, D)
```

```python
from collections import namedtuple
from contextlib import ExitStack

import numpy as np

import concourse.bass as bass
from concourse import mybir

F32 = mybir.dt.float32
F32R = mybir.dt.float32r
I32 = mybir.dt.int32
ALU = mybir.AluOpType
ACT = mybir.ActivationFunctionType
AX = mybir.AxisListType

P = 128
D = 1024
KD = D // P
SEQ = 256
META = 16
TT = SEQ + META
DEPTH = 2
FF = 2816
KF = FF // P
NSPLIT = KF + KD
WIN, WOUT = KD * 2 * P, KF * P
HD = 64
TOPK = min(256, SEQ // 4)
EPS = 1e-6
NEG = -1e30
TAKEN = -3e38
IN1 = 2660
TILES1 = [(0, 128), (128, 128)]
TILES2 = [(0, 80), (80, 128), (208, 64)]

NormPlan = namedtuple("NormPlan", "T n src ms dst gains rows width one over_tiles rot norm post")
SoftPlan = namedtuple("SoftPlan", "T tiles heads masks scale head0 sink copy_to")
SIGNALS = '''
    con_in par_in x_in pos_in mask_in swa_in wm_in0 wm_in1 out_written wa0 wa1 w_hi w_lo
    dve_chain act_chain rope_ang rope_ready
    x_tile sq_tile sq_sum sumsq rstd_ready hn_half hi_half h_ready
    prod_done ffn_done silu_done act_done conv_init conv_done
    nr_raw nr_sq nr_ms nr_rs nr_n nr_rot nr_done
    v_ready v_zero sub_done kr_ready qk_ready pv_done pv_copied
    sm_qk sm_nb sm_exp sm_p sm_pt sm_ptc
    sb_z sb_na sb_l sb_sp sb_tail sb_arg sb_e sb_a
    ssm_init ssm_conv ssm_xc ssm_na ssm_l ssm_dt ssm_tr ssm_cb ssm_arg ssm_e ssm_m ssm_y
    ix_logit ix_relu ix_acc ix_ready iw_ready picked_ready
    rt_s rt_m gate_ready dx_ready pool_y mix_ready'''
Signals = namedtuple("Signals", SIGNALS)


def plan_chunks():
    out, mix, split = [], 0, 0

    def ffn(f):
        nonlocal split
        for j in range(NSPLIT):
            split += 1
            out.append((("ffn", f, j), WIN if j < KF else WOUT, ("w_lo", split)))

    def mixer(widths):
        nonlocal mix
        for w in widths:
            mix += 1
            out.append((("mix", mix - 1), w, ("prod_done", mix)))

    for l in range(DEPTH):
        mixer(MIX1)
        ffn(l)
    ffn(2)
    mixer(MIX_EVEN)
    ffn(3)
    ffn(4)
    mixer(MIX_ODD)
    ffn(5)
    return out


MIX1 = [KD * 512, KD * 512, KD * 420, KD * 512, KD * 512, KD * 256] + [KD * 256] * 4
MIX_EVEN = [KD * 512] * 4 + [KD * 136] + [KD * 512] * 6 + [12 * 256] * 4
MIX_ODD = [KD * 512, KD * 384, KD * 512, 4 * 128] + [KD * 256] * 4

WM = 2 * 384 + 4 * 96 + 256


def columns(widths):
    at, out = 0, {}
    for name, w in widths:
        out[name] = at
        at += w
    out["end"] = at
    return out


PC = columns([(f"{n}{l}", w) for l in range(DEPTH) for n, w in [
    ("mixg", 8), ("ffng", 8), ("mobaq", 1), ("mobak", 1), ("mlacq", 2), ("mlackv", 1), ("mlaq", 1), ("mlak", 1),
    ("ssmw", 16), ("ssmb", 4), ("dtb", 1), ("alog", 1), ("dskip", 2), ("ssmg", 2), ("headg", 6),
    ("fconv", KF * 8), ("ffn1g", 8), ("mix2g", 8), ("ffn2g", 8)]]
    + [("evq", 1), ("evk", 1), ("odq", 1), ("odk", 1), ("sink", 8), ("dscale", 4)])
CC = columns([("ident", 128), ("ones", 128), ("blk", 128), ("rot", 128), ("rot_mla", 128), ("later", 128),
              ("softmask", 256), ("ssmmask", 256), ("strict", 256), ("sel", 512), ("inv", 2), ("eps", 1), ("halfpi", 1),
              ("tri", TT), ("rcos", TT), ("rsin", TT), ("rq", 4 * TT), ("kdec", 24), ("cfix", 64)])


def constants():
    c = np.zeros((P, CC["end"]), np.float32)
    p = np.arange(P)

    def put(name, a):
        a = np.asarray(a, np.float32)
        c[:a.shape[0], CC[name]:CC[name] + a.shape[1]] = a

    put("ident", np.eye(P))
    put("ones", np.ones((P, P)))
    put("blk", (p[:, None] // HD == p[None] // HD))
    rot = np.zeros((P, P))
    for m in range(P):
        if m % HD < HD // 2:
            rot[m + HD // 2, m] = -1.0
        else:
            rot[m - HD // 2, m] = 1.0
    put("rot", rot)
    rot = np.zeros((P, P))
    for m in range(64, 80):
        rot[m + 16, m] = -1.0
        rot[m, m + 16] = 1.0
    put("rot_mla", rot)
    put("later", p[:, None] > p[None])
    q = np.arange(SEQ)
    put("softmask", np.where(q[None] <= p[:, None] + P, 0.0, NEG))
    put("ssmmask", np.where(p[:, None] <= q[None], 0.0, NEG))
    put("strict", p[:, None] < q[None])
    sel = np.zeros((4, 4, P))
    for h in range(4):
        sel[h, h] = 1.0
    put("sel", sel.reshape(4, 4 * P))
    inv64 = (np.float32(1.0) / (np.float32(10000.0) ** (np.arange(0, 64, 2, dtype=np.float32) / np.float32(64)))).astype(np.float32)
    inv32 = (np.float32(1.0) / (np.float32(10000.0) ** (np.arange(0, 32, 2, dtype=np.float32) / np.float32(32)))).astype(np.float32)
    inv = np.zeros((P, 2), np.float32)
    inv[:, 0] = inv64[p % 32]
    inv[64:96, 1] = inv32[np.arange(32) % 16]
    put("inv", inv)
    put("eps", np.full((P, 1), EPS))
    put("halfpi", np.full((P, 1), np.pi / 2))
    t = np.arange(TT)
    put("tri", p[:, None] <= t[None])
    ang = (t[None].astype(np.float32) * inv64[p % 32][:, None]).astype(np.float32)
    put("rcos", np.cos(ang.astype(np.float64)))
    put("rsin", np.sin(ang.astype(np.float64)))
    log_g = np.log(1.0 - 2.0 ** (-5.0 - np.arange(8)))
    put("rq", np.stack([np.exp(t[None] * log_g[2 * m + p // HD][:, None]) for m in range(4)], 1).reshape(P, -1))
    kdec = np.zeros((P, 3, 8))
    for kt, (t0, tl) in enumerate(TILES2):
        kdec[:tl, kt] = np.exp(-(t0 + np.arange(tl))[:, None] * log_g[None]) * HD ** -0.5
    put("kdec", kdec.reshape(P, 24))
    cfix = np.stack([w / np.minimum(np.arange(16) + 1, w) for w in (2, 4, 8, 16)])
    put("cfix", np.broadcast_to(cfix.reshape(1, 64), (P, 64)))
    return c


def chunk_masks():
    cid = (np.arange(TT) + 48) // 64
    out = np.zeros((2, P, 3, TT), np.float32)
    for qt, (t0, tl) in enumerate(TILES2):
        cq, ck = cid[t0:t0 + tl, None], cid[None]
        out[0, :tl, qt] = np.where(ck <= cq, 0.0, NEG)
        out[1, :tl, qt] = np.where((ck == 0) | ((ck <= cq) & (ck >= cq - 2)), 0.0, NEG)
    return out.reshape(2, P, 3 * TT)


def build_program(nc, wmix, wfi, wfo, wmla, params, consts, masks, xin, positions, out):
    chunks = plan_chunks()
    mix_at = {}
    at = 0
    for source, width, _ in chunks:
        if source[0] == "mix":
            mix_at[source[1]] = at
            at += P * width

    with ExitStack() as ctx:
        def sb(name, shape, dt=F32):
            return ctx.enter_context(nc.sbuf_tensor(name, shape, dt))

        PS = ctx.enter_context(nc.psum_tensor("PS", [P, 8, 512], F32))
        wa = sb("wa", [P, 2, KD * 512])
        whi = [sb(f"whi{i}", [P, WOUT], F32R) for i in range(2)]
        wlo = [sb(f"wlo{i}", [P, WOUT], F32R) for i in range(2)]
        X = sb("X", [P, KD, TT])
        par = sb("par", [P, PC["end"]])
        con = sb("con", [P, CC["end"]])
        mask = sb("mask", [P, 3, TT])
        rstd = sb("rstd", [P, TT])
        sq = sb("sq", [P, 2, TT])
        sqsum = sb("sqsum", [P, TT])
        W0, W1, W2 = (sb(f"W{i}", [P, 4, TT]) for i in range(3))
        rope = sb("rope", [P, 4, SEQ])
        small = sb("small", [P, 64])
        with ExitStack() as ffn_ctx:
            def sbf(name, shape, dt=F32R):
                return ffn_ctx.enter_context(nc.sbuf_tensor(name, shape, dt))

            Hhi, Hlo = sbf("Hhi", [P, KD, TT]), sbf("Hlo", [P, KD, TT])
            hidhi, hidlo = sbf("hidhi", [P, KF, TT]), sbf("hidlo", [P, KF, TT])
        wm = sb("wm", [P, WM])
        H = sb("H", [P, KD, TT])
        picked = sb("picked", [P, 3, TT])
        QK = sb("QK", [P, 8, TT])
        VP = sb("VP", [P, 3, 8, P])
        MIX = sb("MIX", [P, 12, TT])
        G = sb("G", [P, 8, TT])
        PT = sb("PT", [P, 3, 4, TT])
        PB = sb("PB", [P, 4, TT])
        IQ, IK, dts = PT[:, 0, :, :], PT[:, 1, 0, :], PT[0:4, 2, 3, :]
        posi = PT[:, 0, 0, 0:SEQ].bitcast(I32)
        rawdt, dt_, acum = G[0:4, 0, :], G[0:4, 1, :], G[0:4, 2, :]
        ea = small[0:4, 0:1]
        ZS = G[:, 4:6, :]
        CQ, CKV, KR = G[:, 4:6, :], G[:, 6, :], G[:, 7, :]
        cols = small[:, 1:17]
        negmax = small[:, 17:21]
        rowsum = small[:, 21:25]
        sinkex = small[:, 25:29]
        iwc = small[:, 29:53]
        top8 = small[:, 53:61]

        S = Signals(*[ctx.enter_context(nc.semaphore(n)) for n in SIGNALS.split()])

        def C(name, width, rows=P):
            return con[0:rows, CC[name]:CC[name] + width]

        def A(name, i=0, rows=P):
            return par[0:rows, PC[name] + i:PC[name] + i + 1]

        ident, ones, blk = C("ident", P), C("ones", P), C("blk", P)

        def wat(slot, n, w):
            return wa[:, slot, 0:n * w].rearrange("p (k c) -> p k c", k=n)

        WA = (S.wa0, S.wa1)
        FREES = {"prod_done": S.prod_done, "w_lo": S.w_lo}
        rope64 = (C("rot", P), rope[:, 0, :], rope[:, 1, :])
        rope_mla = (C("rot_mla", 96, 96), rope[0:96, 2, :], rope[0:96, 3, :])
        rope_ret = (C("rot", P), C("rcos", TT), C("rsin", TT))

        def norm_plan(T, n, src, ms, dst, gains=None, rows=P, width=P, one=None, over_tiles=False, rot=None,
                      norm=True, post=None):
            return NormPlan(T, n, src, ms, dst, gains, rows, width, ones if one is None else one, over_tiles, rot,
                            norm, post)

        def per_head(a, n):
            return a.unsqueeze(1).to_broadcast([a.shape[0], n, a.shape[1]])

        def moba_qk(l):
            return norm_plan(SEQ, 4, 0, 4, QK[:, 0:4, 0:SEQ], [A(f"mobaq{l}")] * 2 + [A(f"mobak{l}")] * 2,
                             width=HD, one=blk, rot=rope64)

        def head_norm(l, m):
            return norm_plan(SEQ, 2, 0, 4, MIX[:, 2 * m:2 * m + 2, 0:SEQ],
                             [A(f"headg{l}", 2 * m), A(f"headg{l}", 2 * m + 1)], width=HD, one=blk)

        def mla_cq(l):
            return norm_plan(SEQ, 2, 0, 4, CQ[0:96, :, 0:SEQ], [A(f"mlacq{l}", i, 96) for i in range(2)], rows=96,
                             width=192, over_tiles=True)

        def mla_ckv(l):
            return norm_plan(SEQ, 1, 2, 5, CKV[:, 0:SEQ].unsqueeze(1), [A(f"mlackv{l}")], width=128)

        def mla_qk(l, k):
            return norm_plan(SEQ, 4, 0, 4, QK[0:96, 4 * k:4 * k + 4, 0:SEQ], [A(f"mlak{l}" if k else f"mlaq{l}", 0, 96)] * 4,
                             rows=96, width=96, rot=rope_mla)

        def ssm_out(l):
            return norm_plan(SEQ, 2, W0[:, 0:2, 0:SEQ], 4, MIX[:, 6:8, 0:SEQ], [A(f"ssmg{l}", i) for i in range(2)],
                             width=256, over_tiles=True)

        def qk2(name, n, t0):
            return norm_plan(TT, n, 0, 4, QK[:, t0:t0 + n, :], [A(name)] * n, width=HD, one=blk)

        def ret_qk(k):
            return norm_plan(TT, 4, 0, 4, QK[:, 4 * k:4 * k + 4, :], rot=rope_ret, norm=False,
                             post=None if k else C("rq", 4 * TT).rearrange("p (m t) -> p m t", m=4))

        def ret_out(g):
            return norm_plan(TT, 4, 4, 0, MIX[:, 4 + 4 * g:8 + 4 * g, :], width=P, post=G[:, 4 * g:4 * g + 4, :])

        def soft_plan(T, tiles, heads, masks, scale, head0=0, sink=False, copy_to=None):
            return SoftPlan(T, tiles, heads, masks, scale, head0, sink, copy_to)

        def half(t, h):
            return QK[HD * (h % 2):HD * (h % 2) + HD, t, :]

        def soft1():
            return [C("softmask", 256)[:, P:2 * P], C("softmask", 256)]

        def moba_soft():
            return soft_plan(SEQ, TILES1, [(half(h // 2, h), half(2 + h // 2, h)) for h in range(4)], soft1(), HD ** -0.5)

        def mla_soft():
            return soft_plan(SEQ, TILES1, [(QK[0:96, h, :], QK[0:96, 4 + h, :]) for h in range(4)], soft1(), 96 ** -0.5)

        def dsa_soft(g):
            return soft_plan(TT, TILES2, [(half(h // 2, h), half(4 + h // 2, h)) for h in range(4 * g, 4 * g + 4)],
                             [picked[:, i, :] for i in range(3)], HD ** -0.5, 4 * g, copy_to=MIX[:, 2 * g:2 * g + 2, :])

        def swa_soft(g):
            return soft_plan(TT, TILES2, [(half(h // 2, h), half(4 + g, h)) for h in range(4 * g, 4 * g + 4)],
                             [mask[:, i, :] for i in range(3)], HD ** -0.5, 4 * g, sink=True,
                             copy_to=MIX[:, 2 * g:2 * g + 2, :])

        def counter():
            seen = {}

            def upto(s, n=1):
                seen[id(s)] = seen.get(id(s), 0) + n
                return seen[id(s)]
            return upto

        def chunk_counter():
            taken = [0]

            def take(n=1):
                taken[0] += n
                return taken[0] - n
            return take

        block = ctx.enter_context(nc.Block())

        @block.sync
        def _(sp):
            sp.dma_start(X[:, :, META:TT], xin[:, 0:KD * SEQ].rearrange("p (k t) -> p k t", k=KD)).then_inc(S.x_in, 16)
            sp.dma_start(X[:, :, 0:META], xin[:, KD * SEQ:KD * TT].rearrange("p (k t) -> p k t", k=KD)).then_inc(S.x_in, 16)
            sp.dma_start(con[:], consts).then_inc(S.con_in, 16)
            sp.dma_start(par[:], params).then_inc(S.par_in, 16)
            sp.dma_start(posi, positions.to_broadcast([P, SEQ])).then_inc(S.pos_in, 16)
            sp.dma_start(mask[:].rearrange("p q t -> p (q t)"), masks[0]).then_inc(S.mask_in, 16)
            take = chunk_counter()

            def slot_free(c):
                if c >= 2:
                    name, value = chunks[c - 2][2]
                    sp.wait_ge(FREES[name], value)

            def load_mix(n):
                for _ in range(n):
                    c = take()
                    source, width, _done = chunks[c]
                    slot_free(c)
                    src = wmix[mix_at[source[1]]:mix_at[source[1]] + P * width].rearrange("(p w) -> p w", p=P)
                    sp.dma_start(wa[:, c % 2, 0:width], src).then_inc(WA[c % 2], 16)

            def load_ffn(f):
                c = take(NSPLIT)
                for j in range(2):
                    slot_free(c + j)
                    sp.dma_start(wa[:, (c + j) % 2, 0:WIN], wfi[f * KF + j]).then_inc(WA[(c + j) % 2], 16)
                with sp.Fori(0, (KF - 2) // 4) as i:
                    for r in range(4):
                        slot = (c + r) % 2
                        sp.wait_ge(S.w_lo, 4 * i + (NSPLIT * f + r + 1))
                        sp.dma_start(wa[:, slot, 0:WIN], wfi[bass.ds(i * 4 + (f * KF + 2 + r), 1)].rearrange(
                            "o p w -> (o p) w")).then_inc(WA[slot], 16)
                for m in range(KD):
                    slot_free(c + KF + m)
                    sp.dma_start(wa[:, (c + m) % 2, 0:WOUT], wfo[f * KD + m]).then_inc(WA[(c + m) % 2], 16)

            def load_mla(l):
                if l:
                    sp.wait_ge(S.ffn_done, NSPLIT * l)
                sp.dma_start(wm[:], wmla[l]).then_inc((S.wm_in0, S.wm_in1)[l], 16)

            load_mix(2)
            load_mla(0)
            load_mix(len(MIX1) - 2)
            load_ffn(0)
            load_mix(2)
            load_mla(1)
            load_mix(len(MIX1) - 2)
            load_ffn(1)
            load_ffn(2)
            load_mix(len(MIX_EVEN))
            load_ffn(3)
            sp.wait_ge(S.picked_ready, 3)
            sp.dma_start(mask[:].rearrange("p q t -> p (q t)"), masks[1]).then_inc(S.swa_in, 16)
            load_ffn(4)
            load_mix(len(MIX_ODD))
            load_ffn(5)
            sp.wait_ge(S.x_tile, KD * 5 * DEPTH)
            sp.dma_start(out, X[:, :, META:TT]).then_inc(S.out_written, 16)
            sp.wait_ge(S.out_written, 16)

        @block.tensor
        def _(pe):
            upto, take = counter(), chunk_counter()
            acts, xs, ffns = [4], [0], [0]

            def landed(c):
                pe.wait_ge(WA[c % 2], 16 * (c // 2 + 1))
                return c % 2

            def input_norm(T):
                pe.wait_ge(S.sq_sum, upto(S.sq_sum, KD))
                pe.matmul(PS[:, 0, 0:T], ones, sqsum[:, 0:T], start=True, stop=True).then_inc(S.sumsq, 1)

            def project_out(T, kt):
                for j in range(KD // 2):
                    c = take()
                    w = wat(landed(c), kt, 256)
                    if j >= 2:
                        pe.wait_ge(S.x_tile, xs[0] + 2 * j - 2)
                    tiles(w, [(P * i, P, 4 + (2 * j + i) % 4) for i in range(2)], T, src=MIX, kt=kt).then_inc(S.prod_done, 1)
                xs[0] += KD

            def tiles(w, cuts, T, src=None, kt=KD, rows=P):
                src = H if src is None else src
                for c0, m, bank in cuts:
                    for k in range(kt):
                        mm = pe.matmul(PS[0:m, bank, 0:T], w[0:rows, k, c0:c0 + m], src[0:rows, k, 0:T],
                                       start=k == 0, stop=k == kt - 1)
                return mm

            def tokens(w, c0, n, toks, places, src=None, kt=KD):
                src = H if src is None else src
                for (t0, tl), (bank, at) in zip(toks, places):
                    for k in range(kt):
                        mm = pe.matmul(PS[0:tl, bank, at:at + n], src[:, k, t0:t0 + tl], w[:, k, c0:c0 + n],
                                       start=k == 0, stop=k == kt - 1)
                return mm

            def norm_rope(q):
                if q.norm:
                    pe.wait_ge(S.nr_sq, upto(S.nr_sq))
                    for i in range(q.n):
                        bank, first, last = (q.ms, i == 0, i == q.n - 1) if q.over_tiles else (q.ms + i, True, True)
                        mm = pe.matmul(PS[0:q.rows, bank, 0:q.T], q.one[0:q.rows, 0:q.rows], W1[0:q.rows, i, 0:q.T],
                                       start=first, stop=last)
                    mm.then_inc(S.nr_ms, 1)
                if q.rot:
                    pe.wait_ge(S.nr_n, upto(S.nr_n))
                    for i in range(q.n):
                        mm = pe.matmul(PS[0:q.rows, i, 0:q.T], q.rot[0], W2[0:q.rows, i, 0:q.T], start=True, stop=True)
                    mm.then_inc(S.nr_rot, 1)
                pe.wait_ge(S.nr_done, upto(S.nr_done))

            def values(T, toks, head0=0, banks=(0, 1)):
                for pair, bank in enumerate(banks):
                    seq = [(kt, h) for kt in range(len(toks)) for h in (2 * pair, 2 * pair + 1)]
                    for i, (kt, h) in enumerate(seq):
                        t0, tl = toks[kt]
                        mm = pe.matmul(PS[:, bank, t0:T], VP[0:tl, kt, head0 + h, :], PT[0:tl, kt, h, t0:T],
                                       start=i == 0, stop=i == len(seq) - 1)
                mm.then_inc(S.pv_done, 1)

            def softmax(a):
                for qt, (q0, ql) in enumerate(a.tiles):
                    keys = q0 + ql
                    for h, (q, k) in enumerate(a.heads):
                        mm = pe.matmul(PS[0:ql, h, 0:keys], q[:, q0:q0 + ql], k[:, 0:keys], start=True, stop=True)
                    mm.then_inc(S.sm_qk, 1)
                    pe.wait_ge(S.sm_p, upto(S.sm_p))
                    if qt:
                        pe.wait_ge(S.sm_ptc, upto(S.sm_ptc))
                    for kt in range(qt + 1):
                        t0, tl = a.tiles[kt]
                        for h in range(4):
                            mm = pe.transpose(PS[0:tl, 4 + kt, h * P:h * P + ql], PB[0:ql, h, t0:t0 + tl],
                                              ident[0:ql, 0:ql])
                    mm.then_inc(S.sm_pt, 1)
                pe.wait_ge(S.sm_ptc, upto(S.sm_ptc))
                values(a.T, a.tiles, a.head0)
                if a.copy_to is not None:
                    pe.wait_ge(S.pv_copied, upto(S.pv_copied))

            def mixer1(l):
                input_norm(SEQ)
                pe.wait_ge(S.h_ready, upto(S.h_ready))
                c = take()
                w = wat(landed(c), KD, 512)
                tiles(w, [(P * i, P, i) for i in range(4)], SEQ).then_inc(S.prod_done, 1)
                norm_rope(moba_qk(l))
                c = take()
                w = wat(landed(c), KD, 512)
                tokens(w, 0, 512, TILES1, [(4, 0), (5, 0)]).then_inc(S.prod_done, 1)
                pe.wait_ge(S.v_ready, upto(S.v_ready))
                softmax(moba_soft())
                norm_rope(head_norm(l, 0))
                c = take()
                w = wat(landed(c), KD, 420)
                tiles(w, [(0, 96, 0), (96, 96, 1), (192, P, 2), (320, 96, 3), (416, 4, 7)], SEQ).then_inc(S.prod_done, 1)
                norm_rope(mla_cq(l))
                norm_rope(mla_ckv(l))
                pe.wait_ge(S.kr_ready, upto(S.kr_ready))
                pe.wait_ge((S.wm_in0, S.wm_in1)[l], 16)
                tiles(wm[:, 0:768].rearrange("p (k c) -> p k c", k=2), [(96 * h, 96, h) for h in range(4)], SEQ,
                      src=CQ, kt=2, rows=96).then_inc(S.sub_done, 1)
                norm_rope(mla_qk(l, 0))
                for h in range(4):
                    pe.matmul(PS[0:96, h, 0:SEQ], wm[:, 768 + 96 * h:864 + 96 * h], CKV[:, 0:SEQ], start=True, stop=False)
                    mm = pe.matmul(PS[0:96, h, 0:SEQ], ident[0:96, 0:96], KR[0:96, 0:SEQ], start=False, stop=True)
                mm.then_inc(S.sub_done, 1)
                norm_rope(mla_qk(l, 1))
                tokens(wm[:, 1152:1408].unsqueeze(1), 0, 256, TILES1, [(4, 0), (5, 0)], src=CKV.unsqueeze(1),
                       kt=1).then_inc(S.sub_done, 1)
                pe.wait_ge(S.v_ready, upto(S.v_ready))
                softmax(mla_soft())
                norm_rope(head_norm(l, 1))
                c = take()
                w = wat(landed(c), KD, 512)
                tiles(w, [(P * i, P, i) for i in range(4)], SEQ).then_inc(S.prod_done, 1)
                pe.wait_ge(S.qk_ready, upto(S.qk_ready))
                for kt in (1, 0):
                    R = SEQ - P * kt
                    if kt == 0:
                        pe.wait_ge(S.sb_a, upto(S.sb_a))
                    for h in range(4):
                        mm = pe.matmul(PS[:, h, 0:R], half(2 + h // 2, h)[:, P * kt:P * kt + P],
                                       half(h // 2, h)[:, P * kt:SEQ], start=True, stop=True)
                    mm.then_inc(S.sb_z, 1)
                    pe.wait_ge(S.sb_sp, upto(S.sb_sp))
                    for j in range(2):
                        o = PS[:, 4 + j, 0:2 * R].rearrange("p (h t) -> p h t", h=2)
                        own = W2 if kt == 0 else QK[:, 4:8, :]
                        mm = pe.matmul(o, C("later", P), own[:, 2 * j:2 * j + 2, 0:R], start=True, stop=kt == 1)
                        if kt == 0:
                            mm = pe.matmul(o[:, :, P:SEQ], ones, QK[:, 4 + 2 * j:6 + 2 * j, 0:P], start=False, stop=True)
                    mm.then_inc(S.sb_tail, 1)
                pe.wait_ge(S.sb_a, upto(S.sb_a))
                values(SEQ, TILES1, 4)
                norm_rope(head_norm(l, 2))
                c = take()
                w = wat(landed(c), KD, 512)
                tiles(w, [(0, P, 4), (P, P, 5), (2 * P, P, 0), (3 * P, P, 1)], SEQ).then_inc(S.prod_done, 1)
                c = take()
                w = wat(landed(c), KD, 256)
                tiles(w, [(0, P, 2), (P, P, 3)], SEQ).then_inc(S.prod_done, 1)
                pe.wait_ge(S.ssm_dt, upto(S.ssm_dt))
                pe.wait_ge(S.ssm_xc, upto(S.ssm_xc))
                for kt in range(2):
                    pe.transpose(PS[:, 7, 4 * kt:4 * kt + 4], dt_[:, P * kt:P * kt + P], ident[0:4, 0:4])
                    pe.transpose(PS[:, 7, 8 + 4 * kt:12 + 4 * kt], acum[:, P * kt:P * kt + P], ident[0:4, 0:4])
                    for n in range(2):
                        at = (2 * kt + n) * P
                        mm = pe.transpose(PS[:, 6, at:at + P], QK[:, n, P * kt:P * kt + P], ident)
                mm.then_inc(S.ssm_tr, 1)
                for h in range(4):
                    pe.matmul(PS[:, h, 0:SEQ], C("sel", 512, 4)[:, P * h:P * h + P], acum[:, 0:SEQ], start=True, stop=True)
                for kt in range(2):
                    for g in range(2):
                        lo = HD * g
                        at = 256 * kt
                        mm = pe.matmul(PS[:, 4 + g, at:at + SEQ - P * kt], QK[lo:lo + HD, 2, P * kt:P * kt + P],
                                       QK[lo:lo + HD, 3, P * kt:SEQ], start=True, stop=True)
                mm.then_inc(S.ssm_cb, 1)
                pe.wait_ge(S.ssm_m, upto(S.ssm_m, 2))
                values(SEQ, TILES1, 0)
                norm_rope(ssm_out(l))
                project_out(SEQ, KD)

            def even():
                input_norm(TT)
                pe.wait_ge(S.h_ready, upto(S.h_ready))
                for t0 in (0, 4):
                    c = take()
                    tiles(wat(landed(c), KD, 512), [(P * i, P, i) for i in range(4)], TT).then_inc(S.prod_done, 1)
                    norm_rope(qk2("evq" if t0 == 0 else "evk", 4, t0))
                c = take()
                tokens(wat(landed(c), KD, 512), 0, 512, TILES2, [(4, 0), (5, 0), (6, 0)]).then_inc(S.prod_done, 1)
                c = take()
                tiles(wat(landed(c), KD, 512), [(P * i, P, i) for i in range(4)], TT).then_inc(S.prod_done, 1)
                c = take()
                pe.wait_ge(S.v_ready, upto(S.v_ready))
                w = wat(landed(c), KD, 136)
                tiles(w, [(0, P, 4)], TT)
                tokens(w, P, 8, TILES2, [(5, 0), (5, 8), (5, 16)]).then_inc(S.prod_done, 1)
                pe.wait_ge(S.ix_ready, upto(S.ix_ready))
                pe.wait_ge(S.iw_ready, upto(S.iw_ready))
                for qt, (q0, ql) in enumerate(TILES2):
                    keys = q0 + ql
                    for g in range(2):
                        if qt or g:
                            pe.wait_ge(S.ix_relu, upto(S.ix_relu))
                        for j in range(4):
                            h = 4 * g + j
                            lo = HD * (h % 2)
                            mm = pe.matmul(PS[0:ql, j, 0:keys], IQ[lo:lo + HD, h // 2, q0:q0 + ql], IK[lo:lo + HD, 0:keys],
                                           start=True, stop=True)
                        mm.then_inc(S.ix_logit, 1)
                pe.wait_ge(S.ix_relu, upto(S.ix_relu))
                softmax(dsa_soft(0))
                softmax(dsa_soft(1))
                for k in range(2):
                    c = take()
                    tiles(wat(landed(c), KD, 512), [(P * i, P, i) for i in range(4)], TT).then_inc(S.prod_done, 1)
                    norm_rope(ret_qk(k))
                for g in range(2):
                    c = take()
                    tokens(wat(landed(c), KD, 512), 0, 512, TILES2, [(3 * g, 0), (3 * g + 1, 0), (3 * g + 2, 0)]
                           ).then_inc(S.prod_done, 1)
                pe.wait_ge(S.v_ready, upto(S.v_ready, 2))
                for g in range(2):
                    c = take()
                    tiles(wat(landed(c), KD, 512), [(P * i, P, 4 * g + i) for i in range(4)], TT).then_inc(S.prod_done, 1)
                pe.wait_ge(S.gate_ready, upto(S.gate_ready, 2))
                for g in range(2):
                    for kt, (t0, tl) in enumerate(TILES2):
                        if kt:
                            pe.wait_ge(S.rt_m, upto(S.rt_m))
                        for j in range(4):
                            h = 4 * g + j
                            mm = pe.matmul(PS[0:tl, j, 0:TT - t0], half(4 + h // 2, h)[:, t0:t0 + tl],
                                           half(h // 2, h)[:, t0:TT], start=True, stop=True)
                        mm.then_inc(S.rt_s, 1)
                    pe.wait_ge(S.rt_m, upto(S.rt_m))
                    for j in range(4):
                        for kt, (t0, tl) in enumerate(TILES2):
                            mm = pe.matmul(PS[:, 4 + j, t0:TT], VP[0:tl, kt, 4 * g + j, :], PT[0:tl, kt, j, t0:TT],
                                           start=kt == 0, stop=kt == 2)
                    mm.then_inc(S.pv_done, 1)
                    norm_rope(ret_out(g))
                project_out(TT, 12)

            def odd():
                input_norm(TT)
                pe.wait_ge(S.h_ready, upto(S.h_ready))
                c = take()
                tiles(wat(landed(c), KD, 512), [(P * i, P, i) for i in range(4)], TT).then_inc(S.prod_done, 1)
                norm_rope(qk2("odq", 4, 0))
                c = take()
                w = wat(landed(c), KD, 384)
                tiles(w, [(0, P, 0), (P, P, 1)], TT)
                tokens(w, 256, P, TILES2, [(7, 0), (7, P), (7, 2 * P)]).then_inc(S.prod_done, 1)
                norm_rope(qk2("odk", 2, 4))
                c = take()
                tiles(wat(landed(c), KD, 512), [(P * i, P, i) for i in range(4)], TT).then_inc(S.prod_done, 1)
                pe.wait_ge(S.v_ready, upto(S.v_ready))
                pe.wait_ge(S.dx_ready, upto(S.dx_ready))
                softmax(swa_soft(0))
                softmax(swa_soft(1))
                c = take()
                w = wat(landed(c), 4, P)
                pe.wait_ge(S.pool_y, upto(S.pool_y))
                for g in range(4):
                    mm = pe.matmul(PS[:, g, 0:TT], w[:, g, :], W2[:, g, :], start=True, stop=True)
                mm.then_inc(S.prod_done, 1)
                pe.wait_ge(S.mix_ready, upto(S.mix_ready))
                project_out(TT, KD)

            def product3(o, hi, lo, xhi, xlo, first, last):
                pe.matmul(o, hi, xhi, start=first, stop=False)
                pe.matmul(o, hi, xlo, start=False, stop=False)
                return pe.matmul(o, lo, xhi, start=False, stop=last)

            def ffn(T):
                input_norm(T)
                take(NSPLIT)
                n = ffns[0]

                def pair(i, r, second_half=None):
                    pe.wait_ge(S.w_lo, i + (n + r + 1))
                    pe.wait_ge(S.act_done, i + (acts[0] + r - 3))
                    hi, lo = (w[r % 2][:, 0:WIN].rearrange("p (k c) -> p k c", k=KD) for w in (whi, wlo))
                    for j in range(2):
                        for k in range(KD):
                            if second_half is not None and j == 0 and k == KD // 2:
                                pe.wait_ge(S.h_ready, second_half)
                            mm = product3(PS[:, 2 * r + j, 0:T], hi[:, k, P * j:P * j + P], lo[:, k, P * j:P * j + P],
                                          Hhi[:, k, 0:T], Hlo[:, k, 0:T], k == 0, k == KD - 1)
                    mm.then_inc(S.ffn_done, 1)

                pe.wait_ge(S.h_ready, upto(S.h_ready))
                h_all = upto(S.h_ready)
                with pe.Fori(0, KF // 4) as i:
                    for r in range(4):
                        pair(4 * i, r, h_all if r == 0 else None)
                for r in range(2):
                    pair(KF - 2, r)
                acts[0] += KF
                with pe.Fori(0, 2) as i:
                    for r in range(4):
                        pe.wait_ge(S.w_lo, 4 * i + (n + KF + r + 1))
                        pe.wait_ge(S.x_tile, 4 * i + (xs[0] - 4 + r + 1)) if xs[0] >= 4 else None
                        hi, lo = (w[r % 2][:, 0:WOUT].rearrange("p (k c) -> p k c", k=KF) for w in (whi, wlo))
                        for k in range(KF):
                            if r == 0 and k == 0:
                                pe.wait_ge(S.act_done, acts[0] - 2)
                            if r == 0 and k == KF - 2:
                                pe.wait_ge(S.act_done, acts[0])
                            mm = product3(PS[:, 4 + r, 0:T], hi[:, k, :], lo[:, k, :], hidhi[:, k, 0:T], hidlo[:, k, 0:T],
                                          k == 0, k == KF - 1)
                        mm.then_inc(S.ffn_done, 1)
                xs[0] += KD
                ffns[0] += NSPLIT

            pe.wait_ge(S.con_in, 16)
            for l in range(DEPTH):
                mixer1(l)
                ffn(SEQ)
            ffn(TT)
            even()
            ffn(TT)
            ffn(TT)
            odd()
            ffn(TT)

        @block.scalar
        def _(act):
            upto, take = counter(), chunk_counter()
            acts, ffns = [4], [0]

            def chain(ins):
                ins.then_inc(S.act_chain, 1)
                act.wait_ge(S.act_chain, upto(S.act_chain))

            def product(c):
                act.wait_ge(S.prod_done, chunks[c][2][1])

            def use_exp_and_ln():
                act.preload_act_table_set("natural_log_exp_and_others")

            def square(T, t0, m):
                act.wait_ge(S.x_tile, upto(S.x_tile))
                count = upto(S.sq_tile)
                if count > 2:
                    act.wait_ge(S.sq_sum, count - 2)
                act.activation(sq[:, m % 2, 0:T], X[:, m, t0:t0 + T], ACT.Square).then_inc(S.sq_tile, 1)

            def reciprocal_root(T):
                act.wait_ge(S.sumsq, upto(S.sumsq))
                chain(act.activation(rstd[:, 0:T], PS[:, 0, 0:T], ACT.Ln, bias=C("eps", 1), scale=1.0 / D))
                act.activation(rstd[:, 0:T], rstd[:, 0:T], ACT.Exp, scale=-0.5).then_inc(S.rstd_ready, 1)

            def round_chunk(c, n, width, i=0):
                slot = c % 2
                act.wait_ge(WA[slot], 8 * i + 16 * (c // 2 + 1))
                if n >= 2:
                    act.wait_ge(S.ffn_done, i + (n - 1))
                act.copy(whi[n % 2][:, 0:width], wa[:, slot, 0:width]).then_inc(S.w_hi, 1)

            def finish(T, t0, tail, following):
                use_exp_and_ln()
                for m in tail:
                    square(T, t0, m)
                reciprocal_root(T)
                if following is not None:
                    round_input(T)
                    round_chunk(following[0] + 1, following[1] + 1, WIN)

            def norm_rope(q):
                if not q.norm:
                    return
                src = q.src
                if isinstance(q.src, int):
                    act.wait_ge(S.nr_raw, upto(S.nr_raw))
                    src = W0[0:q.rows, 0:q.n, 0:q.T]
                act.activation(W1[0:q.rows, 0:q.n, 0:q.T], src, ACT.Square).then_inc(S.nr_sq, 1)
                act.wait_ge(S.nr_ms, upto(S.nr_ms))
                m = 1 if q.over_tiles else q.n
                w = W1[0:q.rows, 0:m, 0:q.T]
                chain(act.activation(w, PS[0:q.rows, q.ms:q.ms + m, 0:q.T], ACT.Ln, bias=C("eps", 1, q.rows),
                                     scale=1.0 / q.width))
                act.activation(w, w, ACT.Exp, scale=-0.5).then_inc(S.nr_rs, 1)

            def softmax(a):
                for qt, (q0, ql) in enumerate(a.tiles):
                    keys = q0 + ql
                    act.wait_ge(S.sm_nb, upto(S.sm_nb))
                    for h in range(4):
                        ex = act.activation(PB[0:ql, h, 0:keys], PB[0:ql, h, 0:keys], ACT.Exp, bias=negmax[0:ql, h:h + 1],
                                            scale=a.scale, accum_out=rowsum[0:ql, h:h + 1])
                    if a.sink:
                        act.activation(sinkex[0:ql, :], sinkex[0:ql, :], ACT.Exp).then_inc(S.sm_exp, 1)
                    else:
                        ex.then_inc(S.sm_exp, 1)
                    act.wait_ge(S.sm_pt, upto(S.sm_pt))
                    for kt in range(qt + 1):
                        t0, tl = a.tiles[kt]
                        cp = act.copy(PT[0:tl, kt, :, q0:q0 + ql],
                                      PS[0:tl, 4 + kt, :].rearrange("p (h q) -> p h q", h=4)[:, :, 0:ql])
                    cp.then_inc(S.sm_ptc, 1)

            def mixer1(l):
                take()
                norm_rope(moba_qk(l))
                take()
                softmax(moba_soft())
                norm_rope(head_norm(l, 0))
                product(take())
                act.copy(KR[0:96, 0:SEQ], PS[0:96, 3, 0:SEQ])
                act.copy(rawdt[:, 0:SEQ], PS[0:4, 7, 0:SEQ]).then_inc(S.kr_ready, 1)
                norm_rope(mla_cq(l))
                norm_rope(mla_ckv(l))
                norm_rope(mla_qk(l, 0))
                norm_rope(mla_qk(l, 1))
                softmax(mla_soft())
                norm_rope(head_norm(l, 1))
                product(take())
                act.copy(QK[:, 0:4, 0:SEQ], PS[:, 0:4, 0:SEQ]).then_inc(S.qk_ready, 1)
                for kt in (1, 0):
                    R = SEQ - P * kt
                    w = W1[:, :, 0:R]
                    act.wait_ge(S.sb_na, upto(S.sb_na))
                    chain(act.activation(w, w, ACT.Exp))
                    act.activation(w, w, ACT.Ln, bias=1.0).then_inc(S.sb_l, 1)
                    act.wait_ge(S.sb_arg, upto(S.sb_arg))
                    act.activation(w, W0[:, :, 0:R], ACT.Exp).then_inc(S.sb_e, 1)
                norm_rope(head_norm(l, 2))
                product(take())
                product(take())
                act.activation(ZS[:, :, 0:SEQ], PS[:, 4:6, 0:SEQ], ACT.Silu)
                for n in range(4):
                    ins = act.activation(W0[:, n, 0:SEQ], PS[:, n, 0:SEQ], ACT.Identity, bias=A(f"ssmb{l}", n),
                                         scale=A(f"ssmw{l}", 4 * n + 3))
                ins.then_inc(S.ssm_init, 1)
                act.wait_ge(S.ssm_conv, upto(S.ssm_conv))
                act.activation(QK[:, 0:4, 0:SEQ], W0[:, :, 0:SEQ], ACT.Silu).then_inc(S.ssm_xc, 1)
                use_exp_and_ln()
                act.wait_ge(S.ssm_na, upto(S.ssm_na))
                chain(act.activation(dts[:, 0:SEQ], dts[:, 0:SEQ], ACT.Exp))
                act.activation(dts[:, 0:SEQ], dts[:, 0:SEQ], ACT.Ln, bias=1.0)
                act.activation(ea, A(f"alog{l}", 0, 4), ACT.Exp).then_inc(S.ssm_l, 1)
                for kt in range(2):
                    R = SEQ - P * kt
                    act.wait_ge(S.ssm_arg, upto(S.ssm_arg))
                    act.activation(W1[:, :, 0:R], W0[:, :, 0:R], ACT.Exp).then_inc(S.ssm_e, 1)
                act.wait_ge(S.ssm_y, upto(S.ssm_y))
                norm_rope(ssm_out(l))
                project_out(SEQ, META)

            def even():
                take()
                norm_rope(qk2("evq", 4, 0))
                take()
                norm_rope(qk2("evk", 4, 4))
                take()
                product(take())
                act.copy(IQ[:, :, :], PS[:, 0:4, 0:TT])
                product(take())
                act.copy(IK, PS[:, 4, 0:TT]).then_inc(S.ix_ready, 1)
                for qt, (q0, ql) in enumerate(TILES2):
                    for g in range(2):
                        act.wait_ge(S.ix_logit, upto(S.ix_logit))
                        if qt or g:
                            act.wait_ge(S.ix_acc, upto(S.ix_acc))
                        act.activation(W0[0:ql, :, 0:q0 + ql], PS[0:ql, 0:4, 0:q0 + ql], ACT.Relu).then_inc(S.ix_relu, 1)
                upto(S.ix_acc)
                softmax(dsa_soft(0))
                softmax(dsa_soft(1))
                take(2)
                take(2)
                for g in range(2):
                    product(take())
                    act.activation(G[:, 4 * g:4 * g + 4, :], PS[:, 4 * g:4 * g + 4, 0:TT], ACT.Silu).then_inc(S.gate_ready, 1)
                use_exp_and_ln()
                for g in range(2):
                    norm_rope(ret_out(g))
                project_out(TT, 0)

            def odd():
                take()
                norm_rope(qk2("odq", 4, 0))
                take()
                norm_rope(qk2("odk", 2, 4))
                product(take())
                act.copy(IQ[:, :, :], PS[:, 0:4, 0:TT]).then_inc(S.dx_ready, 1)
                softmax(swa_soft(0))
                softmax(swa_soft(1))
                take()
                project_out(TT, 0)

            def project_out(T, t0):
                c = take(KD // 2) + KD // 2
                for m in range(4):
                    square(T, t0, m)
                round_chunk(c, ffns[0], WIN)
                finish(T, t0, range(4, 8), (c, ffns[0]))

            def ffn(T, nxt, conv=None):
                c, n = take(NSPLIT), ffns[0]
                ffns[0] += NSPLIT

                def pair(i, r):
                    act.wait_ge(S.ffn_done, i + (n + r + 1))
                    act.wait_ge(S.act_done, i + (acts[0] + r - 1))
                    if conv is None:
                        act.activation(W2[:, r % 2, 0:T], PS[:, 2 * r, 0:T], ACT.Silu).then_inc(S.silu_done, 1)
                        return
                    for j in range(2):
                        at = PC[conv] + 4 * j
                        tap = par[:, bass.ds(i * 8 + (8 * r + at + 2), 1)]
                        bias = par[:, bass.ds(i * 8 + (8 * r + at + 3), 1)]
                        ins = act.activation(W1[:, 2 * (r % 2) + j, 0:T], PS[:, 2 * r + j, 0:T], ACT.Identity, bias=bias,
                                             scale=tap)
                    ins.then_inc(S.conv_init, 1)
                    act.wait_ge(S.conv_done, i + (convs[0] + r + 1))
                    act.activation(W2[:, r % 2, 0:T], W1[:, 2 * (r % 2), 0:T], ACT.Silu).then_inc(S.silu_done, 1)

                act.preload_act_table(ACT.Silu)
                with act.Fori(0, KF // 4) as i:
                    for r in range(4):
                        round_chunk(c + r + 2, n + r + 2, WIN, 4 * i)
                        pair(4 * i, r)
                for r in range(2):
                    round_chunk(c + KF + r, n + KF + r, WOUT)
                    pair(KF - 2, r)
                acts[0] += KF
                if conv is not None:
                    convs[0] += KF
                for m in range(KD - 1):
                    if m < KD - 2:
                        round_chunk(c + KF + m + 2, n + KF + m + 2, WOUT)
                    elif nxt and nxt[2]:
                        round_chunk(c + NSPLIT, n + NSPLIT, WIN)
                    if nxt:
                        square(nxt[0], nxt[1], m)
                if nxt:
                    finish(nxt[0], nxt[1], [KD - 1], (c + NSPLIT, n + NSPLIT) if nxt[2] else None)

            def round_input(T):
                for j, w in enumerate((W0, W1)):
                    act.wait_ge(S.hn_half, upto(S.hn_half))
                    act.copy(Hhi[:, 4 * j:4 * j + 4, 0:T], w[:, :, 0:T]).then_inc(S.hi_half, 1)

            convs = [0]
            act.wait_ge(S.par_in, 16)
            act.wait_ge(S.con_in, 16)
            act.wait_ge(S.rope_ang, 1)
            for j in range(2):
                act.activation(rope[:, 2 * j + 1, :], W1[:, j, 0:SEQ], ACT.Sin)
                ins = act.activation(rope[:, 2 * j, :], W2[:, j, 0:SEQ], ACT.Sin, bias=C("halfpi", 1), scale=-1.0)
            ins.then_inc(S.rope_ready, 1)
            upto(S.rope_ang)
            act.wait_ge(S.x_in, 32)
            use_exp_and_ln()
            for m in range(KD):
                count = upto(S.sq_tile)
                if count > 2:
                    act.wait_ge(S.sq_sum, count - 2)
                act.activation(sq[:, m % 2, 0:SEQ], X[:, m, META:TT], ACT.Square).then_inc(S.sq_tile, 1)
            reciprocal_root(SEQ)
            for l in range(DEPTH):
                mixer1(l)
                ffn(SEQ, (SEQ, META, False) if l < DEPTH - 1 else (TT, 0, True), f"fconv{l}")
            ffn(TT, (TT, 0, False))
            even()
            ffn(TT, (TT, 0, True))
            ffn(TT, (TT, 0, False))
            odd()
            ffn(TT, None)

        @block.vector
        def _(dve):
            upto, take = counter(), chunk_counter()
            acts, convs, silus, ffns = [4], [0], [0], [0]

            def chain(ins):
                ins.then_inc(S.dve_chain, 1)
                dve.wait_ge(S.dve_chain, upto(S.dve_chain))

            def product(c):
                dve.wait_ge(S.prod_done, chunks[c][2][1])

            def input_norm(T, t0, gain):
                dve.wait_ge(S.rstd_ready, upto(S.rstd_ready))
                for k in range(KD):
                    ins = dve.scalar_tensor_tensor(out=H[:, k, 0:T], in0=X[:, k, t0:t0 + T], scalar=A(gain, k),
                                                   in1=rstd[:, 0:T], op0=ALU.mult, op1=ALU.mult)
                ins.then_inc(S.h_ready, 1)

            def input_norm_split(T, t0, gain, c, n):
                dve.wait_ge(S.rstd_ready, upto(S.rstd_ready))
                for j, w in enumerate((W0, W1)):
                    for k in range(4):
                        ins = dve.scalar_tensor_tensor(out=w[:, k, 0:T], in0=X[:, 4 * j + k, t0:t0 + T],
                                                       scalar=A(gain, 4 * j + k), in1=rstd[:, 0:T], op0=ALU.mult,
                                                       op1=ALU.mult)
                    ins.then_inc(S.hn_half, 1)
                for j, w in enumerate((W0, W1)):
                    dve.wait_ge(S.hi_half, upto(S.hi_half))
                    dve.tensor_tensor(out=Hlo[:, 4 * j:4 * j + 4, 0:T], in0=w[:, :, 0:T],
                                      in1=Hhi[:, 4 * j:4 * j + 4, 0:T].bitcast(F32), op=ALU.subtract).then_inc(S.h_ready, 1)
                rest_of_chunk(c, n, WIN)

            def rest_of_chunk(c, n, width, i=0):
                dve.wait_ge(S.w_hi, i + (n + 1))
                dve.tensor_tensor(out=wlo[n % 2][:, 0:width], in0=wa[:, c % 2, 0:width],
                                  in1=whi[n % 2][:, 0:width].bitcast(F32), op=ALU.subtract).then_inc(S.w_lo, 1)

            def clear_sum(T):
                dve.memset(sqsum[:, 0:T], 0.0).then_inc(S.dve_chain, 1)
                dve.wait_ge(S.dve_chain, upto(S.dve_chain))

            def add_square(T):
                count = upto(S.sq_tile)
                dve.wait_ge(S.sq_tile, count)
                dve.tensor_tensor(out=sqsum[:, 0:T], in0=sqsum[:, 0:T], in1=sq[:, (count - 1) % 2, 0:T],
                                  op=ALU.add).then_inc(S.sq_sum, 1)
                dve.wait_ge(S.sq_sum, count)

            def add_tile(m, T, t0, scale):
                x = X[:, m, t0:t0 + T]
                dve.scalar_tensor_tensor(out=x, in0=PS[:, 4 + m % 4, 0:T], scalar=scale, in1=x, op0=ALU.mult,
                                         op1=ALU.add).then_inc(S.x_tile, 1)

            def project_out(T, t0):
                c = 0
                clear_sum(T)
                for j in range(KD // 2):
                    c = take()
                    product(c)
                    for i in range(2):
                        add_tile(2 * j + i, T, t0, 1.0)
                    for i in range(2):
                        add_square(T)
                    if j == 1:
                        rest_of_chunk(c + 3, ffns[0], WIN)

            def norm_rope(q):
                w0, w1, w2 = (w[0:q.rows, 0:q.n, 0:q.T] for w in (W0, W1, W2))
                tail = q.rot or q.post is not None
                if q.norm:
                    if isinstance(q.src, int):
                        dve.tensor_copy(w0, PS[0:q.rows, q.src:q.src + q.n, 0:q.T]).then_inc(S.nr_raw, 1)
                    dve.wait_ge(S.nr_rs, upto(S.nr_rs))
                    for i in range(q.n):
                        rs = W1[0:q.rows, 0 if q.over_tiles else i, 0:q.T]
                        o = (W2[0:q.rows, i, 0:q.T] if tail else q.dst[:, i, :])
                        if q.gains:
                            ins = dve.scalar_tensor_tensor(out=o, in0=W0[0:q.rows, i, 0:q.T], scalar=q.gains[i], in1=rs,
                                                           op0=ALU.mult, op1=ALU.mult)
                        else:
                            ins = dve.tensor_tensor(out=o, in0=W0[0:q.rows, i, 0:q.T], in1=rs, op=ALU.mult)
                else:
                    ins = dve.tensor_copy(w2, PS[0:q.rows, q.src:q.src + q.n, 0:q.T])
                if not tail:
                    ins.then_inc(S.nr_done, 1)
                    dve.wait_ge(S.nr_done, upto(S.nr_done))
                    return
                if q.rot:
                    ins.then_inc(S.nr_n, 1)
                    _, cos, sin = q.rot
                    dve.wait_ge(S.nr_rot, upto(S.nr_rot))
                    dve.tensor_tensor(out=w0, in0=w2, in1=per_head(cos, q.n), op=ALU.mult)
                    chain(dve.tensor_tensor(out=w1, in0=PS[0:q.rows, 0:q.n, 0:q.T], in1=per_head(sin, q.n), op=ALU.mult))
                    if q.post is None:
                        dve.tensor_tensor(out=q.dst, in0=w0, in1=w1, op=ALU.add).then_inc(S.nr_done, 1)
                        dve.wait_ge(S.nr_done, upto(S.nr_done))
                        return
                    chain(dve.tensor_tensor(out=w2, in0=w0, in1=w1, op=ALU.add))
                else:
                    chain(ins)
                dve.tensor_tensor(out=q.dst, in0=w2, in1=q.post, op=ALU.mult).then_inc(S.nr_done, 1)
                dve.wait_ge(S.nr_done, upto(S.nr_done))

            def softmax(a):
                for qt, (q0, ql) in enumerate(a.tiles):
                    keys = q0 + ql
                    pb = PB[0:ql, :, 0:keys]
                    dve.wait_ge(S.sm_qk, upto(S.sm_qk))
                    if qt:
                        dve.wait_ge(S.sm_pt, upto(S.sm_pt))
                    chain(dve.tensor_tensor(out=pb, in0=PS[0:ql, 0:4, 0:keys], in1=per_head(a.masks[qt][0:ql, 0:keys], 4),
                                            op=ALU.add))
                    chain(dve.tensor_reduce(out=negmax[0:ql, :], in_=pb, axis=AX.X, op=ALU.max))
                    if a.sink:
                        sk = par[0:ql, PC["sink"] + a.head0:PC["sink"] + a.head0 + 4]
                        chain(dve.tensor_scalar(negmax[0:ql, :], negmax[0:ql, :], a.scale, None, ALU.mult))
                        chain(dve.tensor_tensor(out=negmax[0:ql, :], in0=negmax[0:ql, :], in1=sk, op=ALU.max))
                        chain(dve.tensor_scalar(negmax[0:ql, :], negmax[0:ql, :], -1.0, None, ALU.mult))
                        dve.tensor_tensor(out=sinkex[0:ql, :], in0=negmax[0:ql, :], in1=sk, op=ALU.add).then_inc(S.sm_nb, 1)
                    else:
                        dve.tensor_scalar(negmax[0:ql, :], negmax[0:ql, :], -a.scale, None, ALU.mult).then_inc(S.sm_nb, 1)
                    dve.wait_ge(S.sm_exp, upto(S.sm_exp))
                    if a.sink:
                        chain(dve.tensor_tensor(out=rowsum[0:ql, :], in0=rowsum[0:ql, :], in1=sinkex[0:ql, :], op=ALU.add))
                    chain(dve.reciprocal(rowsum[0:ql, :], rowsum[0:ql, :]))
                    dve.tensor_tensor(out=pb, in0=pb, in1=rowsum[0:ql, :].unsqueeze(2).to_broadcast([ql, 4, keys]),
                                      op=ALU.mult).then_inc(S.sm_p, 1)
                upto(S.sm_pt)
                if a.copy_to is not None:
                    dve.wait_ge(S.pv_done, upto(S.pv_done))
                    dve.tensor_copy(a.copy_to, PS[:, 0:2, 0:a.T]).then_inc(S.pv_copied, 1)

            def copy_heads(rows, kt, head0, n, src):
                s = src.rearrange("p (h d) -> p h d", h=n)
                dve.tensor_copy(VP[0:rows, kt, head0:head0 + n:2, 0:HD], s[:, 0:n:2, :])
                return dve.tensor_copy(VP[0:rows, kt, head0 + 1:head0 + n:2, HD:P], s[:, 1:n:2, :])

            def clear_values():
                dve.memset(VP[:], 0.0).then_inc(S.v_zero, 1)
                dve.wait_ge(S.v_zero, upto(S.v_zero))

            def mixer1(l):
                clear_values()
                input_norm(SEQ, META, f"mixg{l}")
                product(take())
                norm_rope(moba_qk(l))
                product(take())
                for kt in range(2):
                    ins = copy_heads(P, kt, 0, 8, PS[:, 4 + kt, :])
                ins.then_inc(S.v_ready, 1)
                softmax(moba_soft())
                dve.wait_ge(S.pv_done, upto(S.pv_done))
                norm_rope(head_norm(l, 0))
                product(take())
                norm_rope(mla_cq(l))
                norm_rope(mla_ckv(l))
                dve.wait_ge(S.sub_done, upto(S.sub_done))
                norm_rope(mla_qk(l, 0))
                dve.wait_ge(S.sub_done, upto(S.sub_done))
                norm_rope(mla_qk(l, 1))
                dve.wait_ge(S.sub_done, upto(S.sub_done))
                for kt in range(2):
                    ins = copy_heads(P, kt, 0, 4, PS[:, 4 + kt, 0:256])
                ins.then_inc(S.v_ready, 1)
                softmax(mla_soft())
                dve.wait_ge(S.pv_done, upto(S.pv_done))
                norm_rope(head_norm(l, 1))
                take()
                for kt in (1, 0):
                    R = SEQ - P * kt
                    w0, w1 = W0[:, :, 0:R], W1[:, :, 0:R]
                    sp_ = (W2 if kt == 0 else QK[:, 4:8, :])[:, :, 0:R]
                    strict = per_head(C("strict", SEQ)[:, 0:R], 4)
                    dve.wait_ge(S.sb_z, upto(S.sb_z))
                    chain(dve.tensor_scalar(w0, PS[:, 0:4, 0:R], HD ** -0.5, None, ALU.mult))
                    dve.scalar_tensor_tensor(out=w1, in0=w0, scalar=-1.0, in1=w0, op0=ALU.mult,
                                             op1=ALU.min).then_inc(S.sb_na, 1)
                    dve.wait_ge(S.sb_l, upto(S.sb_l))
                    chain(dve.scalar_tensor_tensor(out=sp_, in0=w0, scalar=0.0, in1=w1, op0=ALU.max, op1=ALU.add))
                    dve.tensor_tensor(out=sp_, in0=sp_, in1=strict, op=ALU.mult).then_inc(S.sb_sp, 1)
                    chain(dve.scalar_tensor_tensor(out=w0, in0=w0, scalar=0.0, in1=w1, op0=ALU.min, op1=ALU.subtract))
                    dve.wait_ge(S.sb_tail, upto(S.sb_tail))
                    for j in range(2):
                        ins = dve.tensor_tensor(out=W0[:, 2 * j:2 * j + 2, 0:R], in0=W0[:, 2 * j:2 * j + 2, 0:R],
                                                in1=PS[:, 4 + j, 0:2 * R].rearrange("p (h t) -> p h t", h=2),
                                                op=ALU.subtract)
                    ins.then_inc(S.sb_arg, 1)
                    dve.wait_ge(S.sb_e, upto(S.sb_e))
                    dve.tensor_tensor(out=PT[:, kt, :, P * kt:SEQ], in0=w1, in1=strict, op=ALU.mult).then_inc(S.sb_a, 1)
                    dve.wait_ge(S.sb_a, upto(S.sb_a))
                dve.wait_ge(S.pv_done, upto(S.pv_done))
                norm_rope(head_norm(l, 2))
                take(2)
                chain(dve.tensor_scalar(rawdt[:, 0:SEQ], rawdt[:, 0:SEQ], A(f"dtb{l}", 0, 4), None, ALU.add))
                dve.scalar_tensor_tensor(out=dts[:, 0:SEQ], in0=rawdt[:, 0:SEQ], scalar=-1.0, in1=rawdt[:, 0:SEQ],
                                         op0=ALU.mult, op1=ALU.min).then_inc(S.ssm_na, 1)
                dve.wait_ge(S.ssm_init, upto(S.ssm_init))
                for s in range(1, 4):
                    for n in range(4):
                        ins = dve.scalar_tensor_tensor(out=W0[:, n, s:SEQ], in0=PS[:, n, 0:SEQ - s],
                                                       scalar=A(f"ssmw{l}", 4 * n + 3 - s), in1=W0[:, n, s:SEQ],
                                                       op0=ALU.mult, op1=ALU.add)
                    if s < 3:
                        chain(ins)
                ins.then_inc(S.ssm_conv, 1)
                dve.wait_ge(S.ssm_l, upto(S.ssm_l))
                chain(dve.scalar_tensor_tensor(out=dt_[:, 0:SEQ], in0=rawdt[:, 0:SEQ], scalar=0.0, in1=dts[:, 0:SEQ],
                                               op0=ALU.max, op1=ALU.add))
                chain(dve.tensor_scalar(dts[:, 0:SEQ], dt_[:, 0:SEQ], ea, -1.0, ALU.mult, ALU.mult))
                dve.tensor_tensor_scan(acum[:, 0:SEQ], C("ones", P, 4)[:, 0:1].to_broadcast([4, SEQ]), dts[:, 0:SEQ], 0.0,
                                       ALU.mult, ALU.add).then_inc(S.ssm_dt, 1)
                dve.wait_ge(S.ssm_tr, upto(S.ssm_tr))
                chain(dve.tensor_copy(cols, PS[:, 7, 0:16]))
                for kt in range(2):
                    copy_heads(P, kt, 0, 4, PS[:, 6, 256 * kt:256 * kt + 256])
                dve.wait_ge(S.ssm_cb, upto(S.ssm_cb))
                for kt in range(2):
                    R = SEQ - P * kt
                    for h in range(4):
                        ins = dve.scalar_tensor_tensor(out=W0[:, h, 0:R], in0=PS[:, h, P * kt:SEQ],
                                                       scalar=cols[:, 8 + 4 * kt + h:9 + 4 * kt + h],
                                                       in1=C("ssmmask", SEQ)[:, 0:R], op0=ALU.subtract, op1=ALU.min)
                    ins.then_inc(S.ssm_arg, 1)
                    dve.wait_ge(S.ssm_e, upto(S.ssm_e))
                    for h in range(4):
                        ins = dve.scalar_tensor_tensor(out=PT[:, kt, h, P * kt:SEQ],
                                                       in0=PS[:, 4 + h // 2, 256 * kt:256 * kt + R],
                                                       scalar=cols[:, 4 * kt + h:4 * kt + h + 1], in1=W1[:, h, 0:R],
                                                       op0=ALU.mult, op1=ALU.mult)
                    ins.then_inc(S.ssm_m, 1)
                dve.wait_ge(S.pv_done, upto(S.pv_done))
                for n in range(2):
                    ins = dve.scalar_tensor_tensor(out=W0[:, n, 0:SEQ], in0=QK[:, n, 0:SEQ], scalar=A(f"dskip{l}", n),
                                                   in1=PS[:, n, 0:SEQ], op0=ALU.mult, op1=ALU.add)
                chain(ins)
                dve.tensor_tensor(out=W0[:, 0:2, 0:SEQ], in0=W0[:, 0:2, 0:SEQ], in1=ZS[:, :, 0:SEQ],
                                  op=ALU.mult).then_inc(S.ssm_y, 1)
                dve.wait_ge(S.ssm_y, upto(S.ssm_y))
                norm_rope(ssm_out(l))
                project_out(SEQ, META)

            def even():
                clear_values()
                input_norm(TT, 0, "mix2g0")
                product(take())
                norm_rope(qk2("evq", 4, 0))
                product(take())
                norm_rope(qk2("evk", 4, 4))
                product(take())
                for kt, (t0, tl) in enumerate(TILES2):
                    ins = copy_heads(tl, kt, 0, 8, PS[0:tl, 4 + kt, :])
                ins.then_inc(S.v_ready, 1)
                take()
                product(take())
                for qt, (q0, ql) in enumerate(TILES2):
                    ins = dve.tensor_scalar(iwc[0:ql, 8 * qt:8 * qt + 8], PS[0:ql, 5, 8 * qt:8 * qt + 8],
                                            8 ** -0.5 * HD ** -0.5, None, ALU.mult)
                ins.then_inc(S.iw_ready, 1)
                dve.wait_ge(S.iw_ready, upto(S.iw_ready))
                dve.wait_ge(S.mask_in, 16)
                for qt, (q0, ql) in enumerate(TILES2):
                    keys = q0 + ql
                    sc, adm, pk = W2[0:ql, 0, 0:keys], mask[0:ql, qt, 0:keys], picked[0:ql, qt, 0:keys]
                    for g in range(2):
                        dve.wait_ge(S.ix_relu, upto(S.ix_relu))
                        for j in range(4):
                            h = 4 * g + j
                            ins = dve.scalar_tensor_tensor(out=sc, in0=W0[0:ql, j, 0:keys],
                                                           scalar=iwc[0:ql, 8 * qt + h:8 * qt + h + 1],
                                                           in1=adm if h == 0 else sc, op0=ALU.mult, op1=ALU.add)
                            if j < 3:
                                chain(ins)
                        ins.then_inc(S.ix_acc, 1)
                        dve.wait_ge(S.ix_acc, upto(S.ix_acc))
                    for _ in range(TOPK // 8):
                        chain(dve.max(out=top8[0:ql, :], in_=sc))
                        chain(dve.match_replace(out=sc, in_to_replace=top8[0:ql, :], in_values=sc, imm_value=TAKEN))
                    chain(dve.tensor_scalar(pk, sc, TAKEN / 2, NEG, ALU.is_ge, ALU.mult))
                    dve.tensor_tensor(out=pk, in0=pk, in1=adm, op=ALU.add).then_inc(S.picked_ready, 1)
                    dve.wait_ge(S.picked_ready, upto(S.picked_ready))
                softmax(dsa_soft(0))
                softmax(dsa_soft(1))
                for k in range(2):
                    product(take())
                    norm_rope(ret_qk(k))
                for g in range(2):
                    product(take())
                    for kt, (t0, tl) in enumerate(TILES2):
                        ins = dve.tensor_copy(VP[0:tl, kt, 4 * g:4 * g + 4, :],
                                              PS[0:tl, 3 * g + kt, :].rearrange("p (h d) -> p h d", h=4))
                    ins.then_inc(S.v_ready, 1)
                take(2)
                for g in range(2):
                    for kt, (t0, tl) in enumerate(TILES2):
                        dve.wait_ge(S.rt_s, upto(S.rt_s))
                        for j in range(4):
                            at = CC["kdec"] + 8 * kt + 4 * g + j
                            ins = dve.scalar_tensor_tensor(out=PT[0:tl, kt, j, t0:TT], in0=PS[0:tl, j, 0:TT - t0],
                                                           scalar=con[0:tl, at:at + 1], in1=C("tri", TT)[0:tl, 0:TT - t0],
                                                           op0=ALU.mult, op1=ALU.mult)
                        ins.then_inc(S.rt_m, 1)
                    dve.wait_ge(S.pv_done, upto(S.pv_done))
                    if g == 0:
                        dve.wait_ge(S.gate_ready, upto(S.gate_ready, 2))
                    norm_rope(ret_out(g))
                project_out(TT, 0)

            def odd():
                clear_values()
                input_norm(TT, 0, "mix2g1")
                product(take())
                norm_rope(qk2("odq", 4, 0))
                product(take())
                for kt, (t0, tl) in enumerate(TILES2):
                    for g in range(2):
                        src = PS[0:tl, 7, P * kt + HD * g:P * kt + HD * g + HD].unsqueeze(1).to_broadcast([tl, 2, HD])
                        dve.tensor_copy(VP[0:tl, kt, 4 * g:4 * g + 4:2, 0:HD], src)
                        dve.tensor_copy(VP[0:tl, kt, 4 * g + 1:4 * g + 4:2, HD:P], src)
                norm_rope(qk2("odk", 2, 4))
                take()
                dve.memset(small[:, 0:1], 0.0).then_inc(S.v_ready, 1)
                dve.wait_ge(S.dx_ready, upto(S.dx_ready))
                dve.wait_ge(S.swa_in, 16)
                src, bufs = IQ, [W0, W1, W0, W1]
                for lv, w in enumerate(bufs):
                    s = 1 << lv
                    dve.tensor_copy(w[:, lv:4, 0:s], src[:, lv:4, 0:s])
                    chain(dve.tensor_tensor(out=w[:, lv:4, s:TT], in0=src[:, lv:4, s:TT], in1=src[:, lv:4, 0:TT - s],
                                            op=ALU.add))
                    fix = C("cfix", 64)[:, 16 * lv:16 * lv + 16]
                    dve.tensor_copy(W2[:, lv, 16:TT], w[:, lv, 16:TT])
                    chain(dve.tensor_tensor(out=W2[:, lv, 0:16], in0=w[:, lv, 0:16], in1=fix, op=ALU.mult))
                    ins = dve.scalar_tensor_tensor(out=W2[:, lv, :], in0=W2[:, lv, :], scalar=1.0 / (2 << lv),
                                                   in1=IQ[:, lv, :], op0=ALU.mult, op1=ALU.subtract)
                    src = w
                ins.then_inc(S.pool_y, 1)
                softmax(swa_soft(0))
                softmax(swa_soft(1))
                product(take())
                for g in range(4):
                    ins = dve.tensor_scalar(MIX[:, 4 + g, :], PS[:, g, 0:TT], A("dscale", g), None, ALU.mult)
                ins.then_inc(S.mix_ready, 1)
                project_out(TT, 0)

            def ffn(T, t0, gain, scale, nxt, conv=None):
                c, n = take(NSPLIT), ffns[0]
                ffns[0] += NSPLIT
                input_norm_split(T, t0, gain, c + 1, n + 1)

                def pair(i, r, hi, lo):
                    if conv is not None:
                        dve.wait_ge(S.conv_init, i + (convs[0] + r + 1))
                        for s in (1, 2):
                            for j in range(2):
                                tap = par[:, bass.ds(i * 8 + (8 * r + PC[conv] + 4 * j + 2 - s), 1)]
                                w = W1[:, 2 * (r % 2) + j, s:T]
                                ins = dve.scalar_tensor_tensor(out=w, in0=PS[:, 2 * r + j, 0:T - s], scalar=tap, in1=w,
                                                               op0=ALU.mult, op1=ALU.add)
                            if s == 1:
                                link(ins, i, r, 0)
                        ins.then_inc(S.conv_done, 1)
                    dve.wait_ge(S.silu_done, i + (silus[0] + r + 1))
                    up = PS[:, 2 * r + 1, 0:T] if conv is None else W1[:, 2 * (r % 2) + 1, 0:T]
                    full = W2[:, 2 + r % 2, 0:T]
                    link(dve.tensor_tensor(out=full, in0=W2[:, r % 2, 0:T], in1=up, op=ALU.mult), i, r, per - 2)
                    link(dve.tensor_copy(hi, full), i, r, per - 1)
                    dve.tensor_tensor(out=lo, in0=full, in1=hi.bitcast(F32), op=ALU.subtract).then_inc(S.act_done, 1)

                per = 2 if conv is None else 3
                chained = upto(S.dve_chain, 0)

                def link(ins, i, r, step):
                    ins.then_inc(S.dve_chain, 1)
                    dve.wait_ge(S.dve_chain, per * i + (chained + per * r + step + 1))

                with dve.Fori(0, KF // 4) as i:
                    for r in range(4):
                        rest_of_chunk(c + r + 2, n + r + 2, WIN, 4 * i)
                        hi, lo = (t[:, bass.ds(4 * i + r, 1), 0:T].rearrange("p o t -> p (o t)") for t in (hidhi, hidlo))
                        pair(4 * i, r, hi, lo)
                for r in range(2):
                    rest_of_chunk(c + KF + r, n + KF + r, WOUT)
                    pair(KF - 2, r, hidhi[:, KF - 2 + r, 0:T], hidlo[:, KF - 2 + r, 0:T])
                upto(S.dve_chain, per * KF)
                silus[0] += KF
                if conv is not None:
                    convs[0] += KF
                if nxt:
                    clear_sum(nxt[0])
                for m in range(KD):
                    if m < KD - 2:
                        rest_of_chunk(c + KF + m + 2, n + KF + m + 2, WOUT)
                    elif m == KD - 2 and nxt and nxt[1]:
                        rest_of_chunk(c + NSPLIT, n + NSPLIT, WIN)
                    dve.wait_ge(S.ffn_done, n + KF + m + 1)
                    add_tile(m, T, t0, scale)
                    if nxt:
                        add_square(nxt[0])

            for m in range(4):
                dve.memset(W0[:, m, :], 0.0).then_inc(S.act_done, 1)
            dve.wait_ge(S.act_done, 4)
            dve.wait_ge(S.con_in, 16)
            dve.wait_ge(S.par_in, 16)
            dve.wait_ge(S.pos_in, 16)
            pos, turns, ang, mag = W0[:, 0, 0:SEQ], W0[:, 1, 0:SEQ], W1, W2
            chain(dve.tensor_copy(pos, posi))
            two_pi = 2 * np.pi
            c1 = 6.28125
            c2 = float(np.float32(int((two_pi - c1) * 2 ** 20) / 2 ** 20))
            c3 = float(np.float32(two_pi - c1 - c2))
            magic = float(1.5 * 2 ** 23)
            for j in range(2):
                a, m = ang[:, j, 0:SEQ], mag[:, j, 0:SEQ]
                chain(dve.tensor_scalar(a, pos, C("inv", 2)[:, j:j + 1], None, ALU.mult))
                chain(dve.tensor_scalar(turns, a, float(1 / two_pi), magic, ALU.mult, ALU.add))
                chain(dve.tensor_scalar(turns, turns, magic, None, ALU.subtract))
                for part in (c1, c2, c3):
                    chain(dve.scalar_tensor_tensor(out=a, in0=turns, scalar=-part, in1=a, op0=ALU.mult, op1=ALU.add))
                chain(dve.tensor_scalar(a, a, 3.1415925, -3.1415925, ALU.min, ALU.max))
                ins = dve.scalar_tensor_tensor(out=m, in0=a, scalar=-1.0, in1=a, op0=ALU.mult, op1=ALU.max)
            ins.then_inc(S.rope_ang, 1)
            dve.wait_ge(S.rope_ready, 1)
            clear_sum(SEQ)
            for m in range(KD):
                add_square(SEQ)
            for l in range(DEPTH):
                mixer1(l)
                ffn(SEQ, META, f"ffng{l}", 1.0, (SEQ, False) if l < DEPTH - 1 else (TT, True), conv=f"fconv{l}")
            ffn(TT, 0, "ffn1g0", 0.5, (TT, False))
            even()
            ffn(TT, 0, "ffn2g0", 0.5, (TT, True))
            ffn(TT, 0, "ffn1g1", 0.5, (TT, False))
            odd()
            ffn(TT, 0, "ffn2g1", 0.5, None)


def tile_rows(w, rows=P):
    k = w.shape[0] // rows
    out = np.zeros((P, k, w.shape[1]), w.dtype)
    out[:rows] = w.reshape(k, rows, w.shape[1]).transpose(1, 0, 2)
    return out.reshape(P, -1)


def layout_weights(i):
    mix = []

    def add(w, rows=P):
        mix.append(tile_rows(w, rows).ravel())

    for l in range(DEPTH):
        w = i["w_in"][l]
        moba, mla, sbk, ssm = 0, 768, 1120, 1888
        add(w[:, moba:moba + 512])
        add(np.concatenate([w[:, moba + 512:moba + 768], w[:, sbk + 512:sbk + 768]], 1))
        pad = np.zeros((D, 64), w.dtype)
        add(np.concatenate([w[:, mla:mla + 320], pad, w[:, mla + 320:mla + 352], w[:, ssm + 768:ssm + 772]], 1))
        add(w[:, sbk:sbk + 512])
        add(w[:, ssm:ssm + 512])
        add(w[:, ssm + 512:ssm + 768])
        for j in range(4):
            add(i["w_out"][l][:, 256 * j:256 * j + 256])
    w = i["ev_w_in_2"][0]
    for c0 in (0, 512, 1024, 1536):
        add(w[:, c0:c0 + 512])
    add(np.concatenate([w[:, 2048:2112], w[:, 2048:2112], w[:, 2112:2120]], 1))
    for c0 in range(2120, 2120 + 3072, 512):
        add(w[:, c0:c0 + 512])
    for j in range(4):
        add(i["ev_w_out_2"][0][:, 256 * j:256 * j + 256])
    w = i["od_w_in_2"][0]
    add(w[:, 0:512])
    add(np.concatenate([w[:, 512:576]] * 2 + [w[:, 576:640]] * 2 + [w[:, 640:768]], 1))
    add(w[:, 768:1280])
    add(i["od_d_mix_2"][0].transpose(1, 0, 2).reshape(P, 512))
    for j in range(4):
        add(i["od_w_out_2"][0][:, 256 * j:256 * j + 256])
    ins = [i["ffn_w_in"][0], i["ffn_w_in"][1], i["ffn1_w_in_2"][0], i["ffn2_w_in_2"][0], i["ffn1_w_in_2"][1], i["ffn2_w_in_2"][1]]
    outs = [i["ffn_w_out"][0], i["ffn_w_out"][1], i["ffn1_w_out_2"][0], i["ffn2_w_out_2"][0], i["ffn1_w_out_2"][1],
            i["ffn2_w_out_2"][1]]
    wfi = np.stack([tile_rows(np.concatenate([w[:, P * j:P * j + P], w[:, FF + P * j:FF + P * j + P]], 1))
                    for w in ins for j in range(KF)])
    wfo = np.stack([tile_rows(w[:, P * j:P * j + P]) for w in outs for j in range(KD)])
    wmla = []
    for l in range(DEPTH):
        kv = i["mla_w_ukv"][l].reshape(P, 4, 128)
        wmla.append(np.concatenate([
            tile_rows(i["mla_w_uq"][l], 96),
            np.pad(kv[:, :, 0:64], ((0, 0), (0, 0), (0, 32))).reshape(P, 384),
            kv[:, :, 64:128].reshape(P, 256)], 1))
    return np.concatenate(mix), wfi, wfo, np.stack(wmla)


def layout_params(i):
    par = np.zeros((P, PC["end"]), np.float32)

    def put(name, a, at=0):
        a = np.asarray(a)
        par[:a.shape[1], PC[name] + at:PC[name] + at + a.shape[0]] = a.T

    for l in range(DEPTH):
        put(f"mixg{l}", i["mix_norm_g"][l].reshape(8, P))
        put(f"ffng{l}", i["ffn_norm_g"][l].reshape(8, P))
        put(f"mobaq{l}", np.tile(i["moba_qk_g"][l, 0], 2)[None])
        put(f"mobak{l}", np.tile(i["moba_qk_g"][l, 1], 2)[None])
        put(f"mlacq{l}", i["mla_q_norm_g"][l].reshape(2, 96))
        put(f"mlackv{l}", i["mla_kv_norm_g"][l][None])
        put(f"mlaq{l}", i["mla_qk_g"][l, 0][None])
        put(f"mlak{l}", i["mla_qk_g"][l, 1][None])
        put(f"ssmw{l}", i["ssm_conv_w"][l].reshape(4, 4, P).transpose(1, 0, 2).reshape(16, P))
        put(f"ssmb{l}", i["ssm_conv_b"][l].reshape(4, P))
        put(f"dtb{l}", i["ssm_dt_bias"][l][None])
        put(f"alog{l}", i["ssm_a_log"][l][None])
        put(f"dskip{l}", np.repeat(i["ssm_d"][l], HD).reshape(2, P))
        put(f"ssmg{l}", i["ssm_norm_g"][l].reshape(2, P))
        put(f"headg{l}", i["head_out_g"][l].reshape(6, P))
        taps = np.concatenate([i["ffn_conv_w"][l], i["ffn_conv_b"][l][None]]).reshape(4, 2, KF, P).transpose(2, 1, 0, 3)
        put(f"fconv{l}", taps.reshape(KF * 8, P))
        put(f"ffn1g{l}", i["ffn1_norm_2"][l].reshape(8, P))
        put(f"mix2g{l}", i["mix_norm_2"][l].reshape(8, P))
        put(f"ffn2g{l}", i["ffn2_norm_2"][l].reshape(8, P))
    for name, key in (("evq", "ev_a_q_norm_2"), ("evk", "ev_a_k_norm_2"), ("odq", "od_c_q_norm_2"), ("odk", "od_c_k_norm_2")):
        put(name, np.tile(i[key][0], 2)[None])
    put("sink", np.repeat(i["od_c_sinks_2"][0][:, None], P, 1))
    put("dscale", i["od_d_scale_2"][0].reshape(4, P))
    return par


def kernel(**inputs):
    import concourse.bacc as bacc
    from concourse.bass_utils import run_bass_kernel_spmd

    i = {k: np.asarray(v) for k, v in inputs.items()}
    wmix, wfi, wfo, wmla = layout_weights(i)

    def features(x):
        return x.T.reshape(KD, P, x.shape[0]).transpose(1, 0, 2).reshape(P, -1)

    arrays = {
        "wmix": wmix, "wfi": wfi, "wfo": wfo, "wmla": wmla, "params": layout_params(i), "consts": constants(),
        "masks": chunk_masks(), "xin": np.concatenate([features(i["x"][0]), features(i["meta_tokens_2"])], 1),
        "pos": i["positions"],
    }
    nc = bacc.Bacc("TRN2", target_bir_lowering=False, num_devices=1)
    arrays = {f"in_{n}": np.ascontiguousarray(a) for n, a in arrays.items()}
    args = [nc.dram_tensor(n, a.shape, mybir.dt.from_np(a.dtype), kind="ExternalInput").ap() for n, a in arrays.items()]
    out = nc.dram_tensor("out_y", (P, KD, SEQ), F32, kind="ExternalOutput").ap()
    build_program(nc, *args, out)
    r = run_bass_kernel_spmd(nc, [arrays], core_ids=[0])
    y = r.results[0]["out_y"]
    return y.transpose(1, 0, 2).reshape(D, SEQ).T.reshape(1, SEQ, D)
```

```python
from collections import namedtuple
from contextlib import ExitStack

import numpy as np

import concourse.bass as bass
from concourse import mybir

F32 = mybir.dt.float32
F32R = mybir.dt.float32r
I32 = mybir.dt.int32
ALU = mybir.AluOpType
ACT = mybir.ActivationFunctionType
AX = mybir.AxisListType

P = 128
D = 1024
KD = D // P
SEQ = 256
META = 16
TT = SEQ + META
DEPTH = 2
FF = 2816
KF = FF // P
NSPLIT = KF + KD
WIN, WOUT = KD * 2 * P, KF * P
HD = 64
TOPK = min(256, SEQ // 4)
EPS = 1e-6
NEG = -1e30
TAKEN = -3e38
IN1 = 2660
TILES1 = [(0, 128), (128, 128)]
TILES2 = [(0, 80), (80, 128), (208, 64)]

HEADS1 = [0, 2, 1, 3]

NormPlan = namedtuple("NormPlan", "lane T n src ms dst gains rows widths one groups rot norm post")
Lane = namedtuple("Lane", "at W QK VP PT PB negmax rowsum sinkex")
SoftPlan = namedtuple("SoftPlan", "lane T tiles heads masks scale head0 sink copy_to")
SIGNALS = '''
    con_in con2_in par_in x_in meta_in pos_in mask_in swa_in wm_in0 wm_in1 out_written wa0 wa1 w_hi w_lo
    dve_chain act_chain rope_ang rope_ready
    x_tile sq_tile sq_sum sumsq rstd_ready xg_ready hn_part hi_part h_ready
    prod_done ffn_done silu_done act_done conv_init gate_in
    nr_sq nr_ms nr_rs nr_n nr_rot nr_done
    v_ready vb_ready v_zero sub_done kr_ready qk_ready pv_done pv_copied
    sm_qk sm_nb sm_exp sm_p sm_pt sm_ptc
    sb_z sb_na sb_l sb_sp sb_tail sb_arg sb_e sb_a
    ssm_init ssm_conv ssm_xc ssm_na ssm_l ssm_dt ssm_tr ssm_cb ssm_arg ssm_e ssm_m ssm_y
    iq_ready ix_logit ix_relu ix_acc ix_ready iw_ready picked_ready
    rt_s rt_m rt_pv gate_ready dx_ready pool_y mix_ready'''
Signals = namedtuple("Signals", SIGNALS)


def others(n=1):
    for _ in range(n):
        yield


def together(*lanes):
    lanes = list(lanes)
    while lanes:
        for lane in list(lanes):
            if next(lane, lanes) is lanes:
                lanes.remove(lane)


def plan_chunks():
    out, mix, products, split = [], 0, 0, 0

    def ffn(f):
        nonlocal split
        for j in range(NSPLIT):
            split += 1
            out.append((("ffn", f, j), WIN if j < KF else WOUT, ("w_lo", split)))

    def mixer(widths, per=2):
        nonlocal mix, products
        for i, w in enumerate(widths):
            mix += 1
            products += per // 2 if i >= len(widths) - KD // per else 1
            out.append((("mix", mix - 1), w, ("prod_done", products)))

    for l in range(DEPTH):
        mixer(MIX1, PER1)
        ffn(l)
    ffn(2)
    mixer(MIX_EVEN)
    ffn(3)
    ffn(4)
    mixer(MIX_ODD)
    ffn(5)
    return out


PER1 = 4
MIX1 = [KD * 512, KD * 484, KD * 512, KD * 512, KD * 512, KD * 256] + [KD * P * PER1] * (KD // PER1)
MIX_EVEN = [KD * 136] + [KD * 512] * 10 + [12 * 256] * 4
MIX_ODD = [KD * 512, KD * 384, KD * 512, 4 * 128] + [KD * 256] * 4

WM = 2 * 384 + 4 * 96 + 256


def columns(widths):
    at, out = 0, {}
    for name, w in widths:
        out[name] = at
        at += w
    out["end"] = at
    return out


PC = columns([(f"{n}{l}", w) for l in range(DEPTH) for n, w in [
    ("mixg", 8), ("ffng", 8), ("mobaq", 1), ("mobak", 1), ("mlacq", 2), ("mlackv", 1), ("mlaq", 1), ("mlak", 1),
    ("ssmw", 16), ("ssmb", 4), ("dtb", 1), ("alog", 1), ("dskip", 2), ("ssmg", 2), ("headg", 6),
    ("fconv", KF * 8), ("ffn1g", 8), ("mix2g", 8), ("ffn2g", 8)]]
    + [("evq", 1), ("evk", 1), ("odq", 1), ("odk", 1), ("sink", 8), ("dscale", 4)])
CC = columns([("ident", 128), ("ones", 128), ("blk", 128), ("rot", 128), ("rot_mla", 128), ("later", 128),
              ("softmask", 256), ("ssmmask", 256), ("strict", 256), ("sel", 512), ("inv", 2), ("eps", 1), ("halfpi", 1),
              ("tri", TT), ("rcos", TT), ("rsin", TT), ("rq", 4 * TT), ("kdec", 24), ("cfix", 64)])


def constants():
    c = np.zeros((P, CC["end"]), np.float32)
    p = np.arange(P)

    def put(name, a):
        a = np.asarray(a, np.float32)
        c[:a.shape[0], CC[name]:CC[name] + a.shape[1]] = a

    put("ident", np.eye(P))
    put("ones", np.ones((P, P)))
    put("blk", (p[:, None] // HD == p[None] // HD))
    rot = np.zeros((P, P))
    for m in range(P):
        if m % HD < HD // 2:
            rot[m + HD // 2, m] = -1.0
        else:
            rot[m - HD // 2, m] = 1.0
    put("rot", rot)
    rot = np.zeros((P, P))
    for m in range(64, 80):
        rot[m + 16, m] = -1.0
        rot[m, m + 16] = 1.0
    put("rot_mla", rot)
    put("later", p[:, None] > p[None])
    q = np.arange(SEQ)
    put("softmask", np.where(q[None] <= p[:, None] + P, 0.0, NEG))
    put("ssmmask", np.where(p[:, None] <= q[None], 0.0, NEG))
    put("strict", p[:, None] < q[None])
    sel = np.zeros((4, 4, P))
    for h in range(4):
        sel[h, h] = 1.0
    put("sel", sel.reshape(4, 4 * P))
    inv64 = (np.float32(1.0) / (np.float32(10000.0) ** (np.arange(0, 64, 2, dtype=np.float32) / np.float32(64)))).astype(np.float32)
    inv32 = (np.float32(1.0) / (np.float32(10000.0) ** (np.arange(0, 32, 2, dtype=np.float32) / np.float32(32)))).astype(np.float32)
    inv = np.zeros((P, 2), np.float32)
    inv[:, 0] = inv64[p % 32]
    inv[64:96, 1] = inv32[np.arange(32) % 16]
    put("inv", inv)
    put("eps", np.full((P, 1), EPS))
    put("halfpi", np.full((P, 1), np.pi / 2))
    t = np.arange(TT)
    put("tri", p[:, None] <= t[None])
    ang = (t[None].astype(np.float32) * inv64[p % 32][:, None]).astype(np.float32)
    put("rcos", np.cos(ang.astype(np.float64)))
    put("rsin", np.sin(ang.astype(np.float64)))
    log_g = np.log(1.0 - 2.0 ** (-5.0 - np.arange(8)))
    put("rq", np.stack([np.exp(t[None] * log_g[2 * m + p // HD][:, None]) for m in range(4)], 1).reshape(P, -1))
    kdec = np.zeros((P, 3, 8))
    for kt, (t0, tl) in enumerate(TILES2):
        kdec[:tl, kt] = np.exp(-(t0 + np.arange(tl))[:, None] * log_g[None]) * HD ** -0.5
    put("kdec", kdec.reshape(P, 24))
    cfix = np.stack([w / np.minimum(np.arange(16) + 1, w) for w in (2, 4, 8, 16)])
    put("cfix", np.broadcast_to(cfix.reshape(1, 64), (P, 64)))
    return c


def chunk_masks():
    cid = (np.arange(TT) + 48) // 64
    out = np.zeros((2, P, 3, TT), np.float32)
    for qt, (t0, tl) in enumerate(TILES2):
        cq, ck = cid[t0:t0 + tl, None], cid[None]
        out[0, :tl, qt] = np.where(ck <= cq, 0.0, NEG)
        out[1, :tl, qt] = np.where((ck == 0) | ((ck <= cq) & (ck >= cq - 2)), 0.0, NEG)
    return out.reshape(2, P, 3 * TT)


def build_program(nc, wmix, wfi, wfo, wmla, params, consts, masks, xin, positions, out):
    chunks = plan_chunks()
    mix_at = {}
    at = 0
    for source, width, _ in chunks:
        if source[0] == "mix":
            mix_at[source[1]] = at
            at += P * width

    with ExitStack() as ctx:
        def sb(name, shape, dt=F32):
            return ctx.enter_context(nc.sbuf_tensor(name, shape, dt))

        PS = ctx.enter_context(nc.psum_tensor("PS", [P, 8, 512], F32))
        wa = sb("wa", [P, 2, KD * 512])
        X = sb("X", [P, KD, TT])
        par = sb("par", [P, PC["end"]])
        con = sb("con", [P, CC["end"]])
        mask = sb("mask", [P, 3, TT])
        rstd = sb("rstd", [P, TT])
        sq = sb("sq", [P, 2, TT])
        sqsum = sb("sqsum", [P, TT])
        W0, W1, W2 = (sb(f"W{i}", [P, 4, TT]) for i in range(3))
        rope = sb("rope", [P, 4, SEQ])
        small = sb("small", [P, 64])
        with ExitStack() as ffn_ctx:
            def sbf(name, shape, dt=F32R):
                return ffn_ctx.enter_context(nc.sbuf_tensor(name, shape, dt))

            split = sbf("split", [P, 4, WOUT])
            whi, wlo = [split[:, i, :] for i in range(2)], [split[:, 2 + i, :] for i in range(2)]
            Hhi, Hlo = sbf("Hhi", [P, KD, TT]), sbf("Hlo", [P, KD, TT])
            hidhi, hidlo = sbf("hidhi", [P, KF, TT]), sbf("hidlo", [P, KF, TT])
        more = sb("more", [P, 4 * WOUT])
        wm = sb("wm", [P, WM])
        H = sb("H", [P, KD, TT])
        picked = sb("picked", [P, 3, TT])
        QK = sb("QK", [P, 8, TT])
        VP = sb("VP", [P, 3, 8, P])
        MIX = sb("MIX", [P, 12, TT])
        G = sb("G", [P, 8, TT])
        PT = sb("PT", [P, 3, 4, TT])
        PB = sb("PB", [P, 4, TT])
        IQ, IK, dts = PT[:, 0, :, :], PT[:, 1, 0, :], PT[0:4, 2, 3, :]
        posi = PT[:, 0, 0, 0:SEQ].bitcast(I32)
        rawdt, dt_, acum = G[0:4, 0, :], G[0:4, 1, :], G[0:4, 2, :]
        ea = small[0:4, 0:1]
        ZS = G[:, 4:6, :]
        CQKV, CQ, CKV, KR = G[:, 4:7, :], G[:, 4:6, :], G[:, 6, :], G[:, 7, :]
        cols = small[:, 29:45]
        negmax = small[:, 17:21]
        rowsum = small[:, 21:25]
        sinkex = small[:, 25:29]
        iwc = small[:, 29:53]
        top8 = small[:, 53:61]

        def spare(at, shape):
            flat = more[:, at:at + int(np.prod(shape))]
            names = "abc"[:len(shape)]
            return flat.rearrange(f"p ({' '.join(names)}) -> p {' '.join(names)}", **dict(zip(names, shape)))

        W1_AT, QK_AT = 4 * TT, 12 * TT
        PB_AT, PT_AT = QK_AT + 8 * TT, QK_AT + 12 * TT
        wb = tuple(spare(i * W1_AT, [4, TT]) for i in range(3))
        vb = VP[:, 2, :, :].rearrange("p (k h) d -> p k h d", k=2)
        lane_a = Lane(0, (W0, W1, W2), QK, VP, PT, PB, negmax, rowsum, sinkex)
        lane_b1 = Lane(8, wb, spare(QK_AT, [8, TT]), vb, spare(PT_AT, [2, 4, SEQ]), spare(PB_AT, [4, TT]),
                       small[:, 1:5], small[:, 5:9], None)
        ret_pt, place = [], QK_AT + 8 * TT + 24 * P
        for t0, _ in TILES2:
            ret_pt.append(spare(place, [4, TT - t0]))
            place += 4 * (TT - t0)
        lane_b2 = Lane(4, wb, spare(QK_AT, [8, TT]), spare(QK_AT + 8 * TT, [3, 8, P]), ret_pt, None, None, None, None)
        lane_b3 = Lane(4, wb, QK, VP, spare(PT_AT, [3, 4, TT]), spare(PB_AT, [4, TT]), small[:, 1:5], small[:, 5:9],
                       small[:, 9:13])
        SSM_Z, SSM_XBC = (6, 7), (4, 5, 2, 3)
        SBQ = MIX[:, 8:12, 0:SEQ]
        DX, POOLED = G[:, 0:4, :], G[:, 4:8, :]
        PW0, PW1 = PT[:, 0, :, :], PT[:, 1, :, :]
        places = {SEQ: PS[:].rearrange("p b (h t) -> p (b h) t", h=2), TT: PS[:, :, 0:TT]}

        S = Signals(*[ctx.enter_context(nc.semaphore(n)) for n in SIGNALS.split()])

        def C(name, width, rows=P):
            return con[0:rows, CC[name]:CC[name] + width]

        def A(name, i=0, rows=P):
            return par[0:rows, PC[name] + i:PC[name] + i + 1]

        ident, ones, blk = C("ident", P), C("ones", P), C("blk", P)

        def wat(slot, n, w):
            return wa[:, slot, 0:n * w].rearrange("p (k c) -> p k c", k=n)

        WA = (S.wa0, S.wa1)
        FREES = {"prod_done": S.prod_done, "w_lo": S.w_lo}
        rope64 = (C("rot", P), rope[:, 0, :], rope[:, 1, :])
        rope_mla = (C("rot_mla", 96, 96), rope[0:96, 2, :], rope[0:96, 3, :])
        rope_ret = (C("rot", P), C("rcos", TT), C("rsin", TT))

        def norm_plan(lane, T, n, src, dst, ms=None, gains=None, rows=P, width=P, one=None, groups=None, rot=None,
                      norm=True, post=None):
            src = lane.at + src if isinstance(src, int) else src
            ms = src if ms is None else lane.at + ms
            groups = tuple(range(n)) if groups is None else groups
            widths = width if isinstance(width, tuple) else (width,)
            return NormPlan(lane, T, n, src, ms, dst, gains, rows, widths, ones if one is None else one, groups, rot,
                            norm, post)

        def per_head(a, n):
            return a.unsqueeze(1).to_broadcast([a.shape[0], n, a.shape[1]])

        def moba_qk(l):
            return norm_plan(lane_a, SEQ, 4, 0, QK[:, 0:4, 0:SEQ], gains=[A(f"mobaq{l}")] * 2 + [A(f"mobak{l}")] * 2,
                             width=HD, one=blk, rot=rope64)

        def head_norm(lane, l, m):
            return norm_plan(lane, SEQ, 2, 0, MIX[:, 2 * m:2 * m + 2, 0:SEQ],
                             gains=[A(f"headg{l}", 2 * m), A(f"headg{l}", 2 * m + 1)], width=HD, one=blk)

        def mla_c(l):
            return norm_plan(lane_b1, SEQ, 3, 0, CQKV[:, :, 0:SEQ],
                             gains=[A(f"mlacq{l}"), A(f"mlacq{l}", 1), A(f"mlackv{l}")], groups=(0, 0, 1), width=(192, 128))

        def mla_qk(l, k):
            return norm_plan(lane_b1, SEQ, 4, 4 * k, lane_b1.QK[0:96, 4 * k:4 * k + 4, 0:SEQ],
                             gains=[A(f"mlak{l}" if k else f"mlaq{l}", 0, 96)] * 4, rows=96, width=96, rot=rope_mla)

        def ssm_out(l):
            return norm_plan(lane_b1, SEQ, 2, wb[0][:, 0:2, 0:SEQ], MIX[:, 6:8, 0:SEQ], ms=0,
                             gains=[A(f"ssmg{l}", i) for i in range(2)], width=256, groups=(0, 0))

        def qk2(lane, name, n, t0):
            return norm_plan(lane, TT, n, 0, QK[:, t0:t0 + n, :], gains=[A(name)] * n, width=HD, one=blk)

        def ret_qk(k):
            return norm_plan(lane_b2, TT, 4, 0, lane_b2.QK[:, 4 * k:4 * k + 4, :], rot=rope_ret, norm=False,
                             post=None if k else C("rq", 4 * TT).rearrange("p (m t) -> p m t", m=4))

        def ret_out(g):
            return norm_plan(lane_b2, TT, 4, 0, MIX[:, 4 + 4 * g:8 + 4 * g, :], width=P, post=G[:, 4 * g:4 * g + 4, :])

        def soft_plan(lane, T, tiles, heads, masks, scale, head0=0, sink=False, copy_to=None):
            return SoftPlan(lane, T, tiles, heads, masks, scale, head0, sink, copy_to)

        def half(t, h, qk=QK):
            return qk[HD * (h % 2):HD * (h % 2) + HD, t, :]

        def soft1():
            return [C("softmask", 256)[:, P:2 * P], C("softmask", 256)]

        def moba_soft():
            return soft_plan(lane_a, SEQ, TILES1, [(half(h // 2, h), half(2 + h // 2, h)) for h in HEADS1], soft1(),
                             HD ** -0.5)

        def mla_soft():
            qk = lane_b1.QK
            return soft_plan(lane_b1, SEQ, TILES1, [(qk[0:96, h, :], qk[0:96, 4 + h, :]) for h in HEADS1], soft1(),
                             96 ** -0.5)

        def dsa_soft(g):
            return soft_plan((lane_a, lane_b3)[g], TT, TILES2,
                             [(half(h // 2, h), half(4 + h // 2, h)) for h in range(4 * g, 4 * g + 4)],
                             [picked[:, i, :] for i in range(3)], HD ** -0.5, 4 * g, copy_to=MIX[:, 2 * g:2 * g + 2, :])

        def swa_soft(g):
            return soft_plan((lane_a, lane_b3)[g], TT, TILES2,
                             [(half(h // 2, h), half(4 + g, h)) for h in range(4 * g, 4 * g + 4)],
                             [mask[:, i, :] for i in range(3)], HD ** -0.5, 4 * g, sink=True,
                             copy_to=MIX[:, 2 * g:2 * g + 2, :])

        def score_place(a, h, rows, keys):
            return places[a.T][0:rows, a.lane.at + h, 0:keys]

        def transpose_bank(a, kt):
            return (a.lane.at // 2 if a.T == SEQ else a.lane.at) + kt

        def counter():
            seen = {}

            def upto(s, n=1):
                seen[id(s)] = seen.get(id(s), 0) + n
                return seen[id(s)]
            return upto

        def chunk_counter():
            taken = [0]

            def take(n=1):
                taken[0] += n
                return taken[0] - n
            return take

        block = ctx.enter_context(nc.Block())

        @block.sync
        def _(sp):
            sp.dma_start(X[:, :, META:TT], xin[:, 0:KD * SEQ].rearrange("p (k t) -> p k t", k=KD)).then_inc(S.x_in, 16)
            sp.dma_start(con[:, 0:CC["tri"]], consts[:, 0:CC["tri"]]).then_inc(S.con_in, 16)
            sp.dma_start(par[:], params).then_inc(S.par_in, 16)
            sp.dma_start(posi, positions.to_broadcast([P, SEQ])).then_inc(S.pos_in, 16)
            take = chunk_counter()

            def slot_free(c):
                if c >= 2:
                    name, value = chunks[c - 2][2]
                    sp.wait_ge(FREES[name], value)

            def load_mix(n):
                for _ in range(n):
                    c = take()
                    source, width, _done = chunks[c]
                    slot_free(c)
                    src = wmix[mix_at[source[1]]:mix_at[source[1]] + P * width].rearrange("(p w) -> p w", p=P)
                    sp.dma_start(wa[:, c % 2, 0:width], src).then_inc(WA[c % 2], 16)

            def load_ffn(f):
                c = take(NSPLIT)
                for j in range(2):
                    slot_free(c + j)
                    sp.dma_start(wa[:, (c + j) % 2, 0:WIN], wfi[f * KF + j]).then_inc(WA[(c + j) % 2], 16)
                with sp.Fori(0, (KF - 2) // 4) as i:
                    for r in range(4):
                        slot = (c + r) % 2
                        sp.wait_ge(S.w_lo, 4 * i + (NSPLIT * f + r + 1))
                        sp.dma_start(wa[:, slot, 0:WIN], wfi[bass.ds(i * 4 + (f * KF + 2 + r), 1)].rearrange(
                            "o p w -> (o p) w")).then_inc(WA[slot], 16)
                for m in range(KD):
                    slot_free(c + KF + m)
                    sp.dma_start(wa[:, (c + m) % 2, 0:WOUT], wfo[f * KD + m]).then_inc(WA[(c + m) % 2], 16)

            def load_mla(l):
                if l:
                    sp.wait_ge(S.ffn_done, NSPLIT * l)
                sp.dma_start(wm[:], wmla[l]).then_inc((S.wm_in0, S.wm_in1)[l], 16)

            load_mix(2)
            load_mla(0)
            sp.dma_start(X[:, :, 0:META], xin[:, KD * SEQ:KD * TT].rearrange("p (k t) -> p k t", k=KD)).then_inc(S.meta_in, 16)
            sp.dma_start(con[:, CC["tri"]:], consts[:, CC["tri"]:]).then_inc(S.con2_in, 16)
            sp.dma_start(mask[:].rearrange("p q t -> p (q t)"), masks[0]).then_inc(S.mask_in, 16)
            load_mix(len(MIX1) - 2)
            load_ffn(0)
            load_mix(2)
            load_mla(1)
            load_mix(len(MIX1) - 2)
            load_ffn(1)
            load_ffn(2)
            load_mix(len(MIX_EVEN))
            load_ffn(3)
            sp.wait_ge(S.picked_ready, 3)
            sp.dma_start(mask[:].rearrange("p q t -> p (q t)"), masks[1]).then_inc(S.swa_in, 16)
            load_ffn(4)
            load_mix(len(MIX_ODD))
            load_ffn(5)
            sp.wait_ge(S.x_tile, KD * 5 * DEPTH)
            sp.dma_start(out, X[:, :, META:TT]).then_inc(S.out_written, 16)
            sp.wait_ge(S.out_written, 16)

        @block.tensor
        def _(pe):
            upto, take = counter(), chunk_counter()
            acts, xs, ffns, norms = [4], [0], [0], [0]

            def landed(c):
                pe.wait_ge(WA[c % 2], 16 * (c // 2 + 1))
                return c % 2

            def input_norm(T, bank=0):
                pe.wait_ge(S.sq_sum, upto(S.sq_sum, KD))
                pe.matmul(PS[:, bank, 0:T], ones, sqsum[:, 0:T], start=True, stop=True).then_inc(S.sumsq, 1)

            def out_tile(w, j, m, T, ks, first, last, m0):
                for k in ks:
                    mm = pe.matmul(PS[:, m, 0:T], w[:, k, P * j:P * j + P], MIX[:, k, m0:m0 + T],
                                   start=first and k == ks[0], stop=last and k == ks[-1])
                return mm

            def out_ahead(base, first, ahead, T, kt, per, n, ks):
                for m in range(n):
                    if m % per == 0:
                        ahead.append(use(first + m // per, base, kt, P * per))
                    out_tile(ahead[-1], m % per, m, T, ks, True, False, 0)
                    yield

            def project_out(base, first, T, kt, per=2, ahead=(), done=(), m0=0):
                left = [k for k in range(kt) if k not in done]
                for m in range(KD):
                    started = m // per < len(ahead)
                    if m % per == 0:
                        w = ahead[m // per] if started else use(first + m // per, base, kt, P * per)
                    mm = out_tile(w, m % per, m, T, left if started else range(kt), not started, True, m0)
                    if m % 2:
                        mm.then_inc(S.prod_done, 1)
                xs[0] += KD

            second_half = [None]

            def tiles(w, cuts, T, src=None, kt=KD, rows=P):
                src = H if src is None else src
                for c0, m, place in cuts:
                    for k in range(kt):
                        if k == 4 and second_half[0] is not None:
                            pe.wait_ge(S.h_ready, second_half[0])
                            second_half[0] = None
                        mm = pe.matmul(places[T][0:m, place, 0:T], w[0:rows, k, c0:c0 + m], src[0:rows, k, 0:T],
                                       start=k == 0, stop=k == kt - 1)
                return mm

            def tokens(w, c0, n, toks, spots, src=None, kt=KD):
                src = H if src is None else src
                for (t0, tl), (bank, at) in zip(toks, spots):
                    for k in range(kt):
                        mm = pe.matmul(PS[0:tl, bank, at:at + n], src[:, k, t0:t0 + tl], w[:, k, c0:c0 + n],
                                       start=k == 0, stop=k == kt - 1)
                return mm

            def use(c, base, n, w):
                assert take() == base + c
                return wat(landed(base + c), n, w)

            def others_or(fill, n=1):
                for i in range(n):
                    if i % 2 == (n > 2):
                        next(fill, None)
                    yield

            def norm_rope(q, fill=iter(())):
                ps, W = places[q.T], q.lane.W
                if q.norm:
                    yield from others_or(fill)
                    pe.wait_ge(S.nr_sq, upto(S.nr_sq))
                    for i, g in enumerate(q.groups):
                        mm = pe.matmul(ps[0:q.rows, q.ms + g, 0:q.T], q.one[0:q.rows, 0:q.rows], W[1][0:q.rows, i, 0:q.T],
                                       start=g not in q.groups[:i], stop=g not in q.groups[i + 1:])
                    mm.then_inc(S.nr_ms, 1)
                    yield from others_or(fill, 2)
                if q.rot:
                    yield from others_or(fill)
                    pe.wait_ge(S.nr_n, upto(S.nr_n))
                    for i in range(q.n):
                        mm = pe.matmul(ps[0:q.rows, q.ms + i, 0:q.T], q.rot[0], W[2][0:q.rows, i, 0:q.T], start=True,
                                       stop=True)
                    mm.then_inc(S.nr_rot, 1)
                    yield from others_or(fill)
                yield from others_or(fill)
                pe.wait_ge(S.nr_done, upto(S.nr_done))

            def values(lane, T, toks, head0=0, place=0):
                for pair in range(2):
                    seq = [(kt, h) for kt in range(len(toks)) for h in (2 * pair, 2 * pair + 1)]
                    for i, (kt, h) in enumerate(seq):
                        t0, tl = toks[kt]
                        mm = pe.matmul(places[T][:, lane.at + place + pair, t0:T], lane.VP[0:tl, kt, head0 + h, :],
                                       lane.PT[0:tl, kt, HEADS1[h] if T == SEQ else h, t0:T], start=i == 0, stop=i == len(seq) - 1)
                mm.then_inc(S.pv_done, 1)

            def softmax(a, fill=iter(())):
                for qt, (q0, ql) in enumerate(a.tiles):
                    keys = q0 + ql
                    if qt:
                        pe.wait_ge(S.sm_ptc, upto(S.sm_ptc))
                    for h, (q, k) in enumerate(a.heads):
                        mm = pe.matmul(score_place(a, h, ql, keys), q[:, q0:q0 + ql], k[:, 0:keys], start=True, stop=True)
                    mm.then_inc(S.sm_qk, 1)
                    yield from others_or(fill, 4)
                    pe.wait_ge(S.sm_p, upto(S.sm_p))
                    for kt in range(qt + 1):
                        t0, tl = a.tiles[kt]
                        for h in range(4):
                            mm = pe.transpose(PS[0:tl, transpose_bank(a, kt), h * P:h * P + ql],
                                              a.lane.PB[0:ql, h, t0:t0 + tl], ident[0:ql, 0:ql])
                    mm.then_inc(S.sm_pt, 1)
                    yield from others_or(fill, 2)
                pe.wait_ge(S.sm_ptc, upto(S.sm_ptc))
                values(a.lane, a.T, a.tiles, a.head0)
                yield
                if a.copy_to is not None:
                    yield
                    pe.wait_ge(S.pv_copied, upto(S.pv_copied))

            def moba_and_sticks(l, base, ahead):
                def both_v():
                    w = use(2, base, KD, 512)
                    for bank, (t0, tl) in zip((2, 3), TILES1):
                        for k in range(KD):
                            mm = pe.matmul(PS[:, bank, :], H[:, k, t0:t0 + tl], w[:, k, :], start=k == 0, stop=k == KD - 1)
                            if k == KD - 1 and bank == 3:
                                mm.then_inc(S.prod_done, 1)
                            if k % 4 == 3:
                                yield

                def sticks_qk():
                    w = use(3, base, KD, 512)
                    for i in range(4):
                        mm = tiles(w, [(P * i, P, 4 + i)], SEQ)
                        if i == 3:
                            mm.then_inc(S.prod_done, 1)
                        yield

                tiles(use(0, base, KD, 512), [(P * i, P, i) for i in range(4)], SEQ).then_inc(S.prod_done, 1)
                yield
                yield from norm_rope(moba_qk(l), both_v())
                pe.wait_ge(S.v_ready, upto(S.v_ready))
                yield from softmax(moba_soft(), sticks_qk())
                yield from norm_rope(head_norm(lane_a, l, 0))
                yield
                pe.wait_ge(S.qk_ready, upto(S.qk_ready))
                for kt in (1, 0):
                    R = SEQ - P * kt
                    if kt == 0:
                        pe.wait_ge(S.sb_a, upto(S.sb_a))
                    for i, h in enumerate(HEADS1):
                        mm = pe.matmul(places[SEQ][:, i, 0:R], half(2 + h // 2, h, SBQ)[:, P * kt:P * kt + P],
                                       half(h // 2, h, SBQ)[:, P * kt:SEQ], start=True, stop=True)
                    mm.then_inc(S.sb_z, 1)
                    yield from others(4)
                    pe.wait_ge(S.sb_sp, upto(S.sb_sp))
                    for j in range(2):
                        o = PS[:, 2 + j, 0:2 * R].rearrange("p (h t) -> p h t", h=2)
                        own = W2 if kt == 0 else QK[:, 4:8, :]
                        mm = pe.matmul(o, C("later", P), own[:, 2 * j:2 * j + 2, 0:R], start=True, stop=kt == 1)
                        if kt == 0:
                            mm = pe.matmul(o[:, :, P:SEQ], ones, QK[:, 4 + 2 * j:6 + 2 * j, 0:P], start=False, stop=True)
                    mm.then_inc(S.sb_tail, 1)
                    yield from others(4)
                pe.wait_ge(S.sb_a, upto(S.sb_a))
                values(lane_a, SEQ, TILES1, 4)
                yield
                yield from norm_rope(head_norm(lane_a, l, 2))
                yield from out_ahead(base, 6, ahead, SEQ, KD, PER1, 4, range(6))

            def mla_and_ssm(l, base):
                at, qk = lane_b1.at, lane_b1.QK

                def mla_v():
                    tokens(wm[:, 1152:1408].unsqueeze(1), 0, 256, TILES1, [(at // 2, 0), (at // 2, 256)],
                           src=CKV.unsqueeze(1), kt=1).then_inc(S.sub_done, 1)
                    yield

                def ssm_in(c, width, places_):
                    w = use(c, base, KD, width)
                    for i, place in enumerate(places_):
                        mm = tiles(w, [(P * i, P, at + place)], SEQ)
                        if i == len(places_) - 1:
                            mm.then_inc(S.prod_done, 1)
                        yield

                tiles(use(1, base, KD, 484), [(0, P, at), (P, P, at + 1), (2 * P, P, at + 2), (3 * P, 96, at + 4),
                                              (3 * P + 96, 4, at + 5)], SEQ).then_inc(S.prod_done, 1)
                yield
                yield from norm_rope(mla_c(l))
                pe.wait_ge(S.kr_ready, upto(S.kr_ready))
                pe.wait_ge((S.wm_in0, S.wm_in1)[l], 16)
                tiles(wm[:, 0:768].rearrange("p (k c) -> p k c", k=2), [(96 * h, 96, at + h) for h in range(4)], SEQ,
                      src=CQ, kt=2, rows=96)
                for h in range(4):
                    o = places[SEQ][0:96, at + 4 + h, :]
                    pe.matmul(o, wm[:, 768 + 96 * h:864 + 96 * h], CKV[:, 0:SEQ], start=True, stop=False)
                    mm = pe.matmul(o, ident[0:96, 0:96], KR[0:96, 0:SEQ], start=False, stop=True)
                mm.then_inc(S.sub_done, 1)
                yield
                yield from norm_rope(mla_qk(l, 0))
                yield from norm_rope(mla_qk(l, 1), mla_v())
                pe.wait_ge(S.vb_ready, upto(S.vb_ready))
                yield from softmax(mla_soft(), ssm_in(4, 512, SSM_Z + SSM_XBC[0:2]))
                yield from norm_rope(head_norm(lane_b1, l, 1), ssm_in(5, 256, SSM_XBC[2:4]))
                yield from others(4)
                pe.wait_ge(S.ssm_dt, upto(S.ssm_dt))
                pe.wait_ge(S.ssm_xc, upto(S.ssm_xc))
                for kt in range(2):
                    pe.transpose(PS[:, at // 2 + 1, 4 * kt:4 * kt + 4], dt_[:, P * kt:P * kt + P], ident[0:4, 0:4])
                    pe.transpose(PS[:, at // 2 + 1, 8 + 4 * kt:12 + 4 * kt], acum[:, P * kt:P * kt + P], ident[0:4, 0:4])
                    for n in range(2):
                        c0 = (2 * kt + n) * P
                        mm = pe.transpose(PS[:, at // 2, c0:c0 + P], qk[:, n, P * kt:P * kt + P], ident)
                mm.then_inc(S.ssm_tr, 1)
                yield from others(2)
                for h in range(4):
                    pe.matmul(places[SEQ][:, at + 4 + h, :], C("sel", 512, 4)[:, P * h:P * h + P], acum[:, 0:SEQ],
                              start=True, stop=True)
                pe.wait_ge(S.vb_ready, upto(S.vb_ready))
                for kt in range(2):
                    for g in range(2):
                        lo, c0 = HD * g, 256 * kt
                        mm = pe.matmul(PS[:, at // 2 + g, c0:c0 + SEQ - P * kt], qk[lo:lo + HD, 2, P * kt:P * kt + P],
                                       qk[lo:lo + HD, 3, P * kt:SEQ], start=True, stop=True)
                mm.then_inc(S.ssm_cb, 1)
                yield from others(4)
                pe.wait_ge(S.ssm_m, upto(S.ssm_m))
                values(lane_b1, SEQ, TILES1, 0, place=4)
                yield
                yield from norm_rope(ssm_out(l))

            def mixer1(l):
                norms[0] += 1
                input_norm(SEQ)
                pe.wait_ge(S.h_ready, upto(S.h_ready))
                second_half[0] = upto(S.h_ready)
                base = take(0)
                ahead = []
                together(moba_and_sticks(l, base, ahead), mla_and_ssm(l, base))
                project_out(base, 6, SEQ, KD, PER1, ahead, range(6))

            def sparse(base, ahead):
                w = use(0, base, KD, 136)
                tiles(w, [(0, P, 0)], TT)
                tokens(w, P, 8, TILES2, [(1, 0), (1, 8), (1, 16)]).then_inc(S.prod_done, 1)
                yield from others(2)
                pe.wait_ge(S.ix_ready, 1)
                pe.wait_ge(S.iw_ready, 1)
                tiles(use(2, base, KD, 512), [(P * i, P, i) for i in range(4)], TT).then_inc(S.prod_done, 1)
                yield from others(2)
                pe.wait_ge(S.iq_ready, 1)
                for qt, (q0, ql) in enumerate(TILES2):
                    keys = q0 + ql
                    for g in range(2):
                        if qt or g:
                            pe.wait_ge(S.ix_relu, upto(S.ix_relu))
                        for j in range(4):
                            h = 4 * g + j
                            lo = HD * (h % 2)
                            mm = pe.matmul(PS[0:ql, j, 0:keys], IQ[lo:lo + HD, h // 2, q0:q0 + ql], IK[lo:lo + HD, 0:keys],
                                           start=True, stop=True)
                        mm.then_inc(S.ix_logit, 1)
                        yield from others(2)
                pe.wait_ge(S.ix_relu, upto(S.ix_relu))
                for k in range(2):
                    tiles(use(7 + k, base, KD, 512), [(P * i, P, i) for i in range(4)], TT).then_inc(S.prod_done, 1)
                    yield
                    yield from norm_rope(qk2(lane_a, ("evq", "evk")[k], 4, 4 * k))
                tokens(use(10, base, KD, 512), 0, 512, TILES2, [(0, 0), (1, 0), (2, 0)]).then_inc(S.prod_done, 1)
                yield from others(2)
                pe.wait_ge(S.v_ready, upto(S.v_ready))
                yield from softmax(dsa_soft(0))
                yield from out_ahead(base, 11, ahead, TT, 12, 2, 4, EARLY)

            def retention(base):
                lane = lane_b2
                at = lane.at
                for k in range(2):
                    tiles(use((1, 3)[k], base, KD, 512), [(P * i, P, at + i) for i in range(4)], TT).then_inc(S.prod_done, 1)
                    yield
                    yield from norm_rope(ret_qk(k))
                for g in range(2):
                    tokens(use(4 + g, base, KD, 512), 0, 512, TILES2, [(at, 0), (at + 1, 0), (at + 2, 0)]
                           ).then_inc(S.prod_done, 1)
                    yield from others(2)
                    pe.wait_ge(S.vb_ready, upto(S.vb_ready))
                for g in range(2):
                    tiles(use((6, 9)[g], base, KD, 512), [(P * i, P, at + i) for i in range(4)],
                          TT).then_inc(S.prod_done, 1)
                    yield from others(2)
                    pe.wait_ge(S.gate_ready, upto(S.gate_ready))
                    for kt, (t0, tl) in enumerate(TILES2):
                        if kt:
                            pe.wait_ge(S.rt_m, upto(S.rt_m))
                        for j in range(4):
                            h = 4 * g + j
                            mm = pe.matmul(PS[0:tl, at + j, 0:TT - t0], half(4 + h // 2, h, lane.QK)[:, t0:t0 + tl],
                                           half(h // 2, h, lane.QK)[:, t0:TT], start=True, stop=True)
                        mm.then_inc(S.rt_s, 1)
                        yield from others(2)
                    pe.wait_ge(S.rt_m, upto(S.rt_m))
                    for j in range(4):
                        for kt, (t0, tl) in enumerate(TILES2):
                            mm = pe.matmul(PS[:, at + j, t0:TT], lane.VP[0:tl, kt, 4 * g + j, :], lane.PT[kt][0:tl, j, :],
                                           start=kt == 0, stop=kt == 2)
                    mm.then_inc(S.rt_pv, 1)
                    yield
                    yield from norm_rope(ret_out(g))
                yield from softmax(dsa_soft(1))

            EARLY = [0, 1] + list(range(4, 12))

            def even():
                norms[0] += 1
                input_norm(TT)
                pe.wait_ge(S.h_ready, upto(S.h_ready))
                second_half[0] = upto(S.h_ready)
                base = take(0)
                ahead = []
                together(sparse(base, ahead), retention(base))
                project_out(base, 11, TT, 12, 2, ahead, EARLY)

            def window_q(base):
                tiles(use(0, base, KD, 512), [(P * i, P, i) for i in range(4)], TT).then_inc(S.prod_done, 1)
                yield from others(2)
                pe.wait_ge(S.dx_ready, upto(S.dx_ready))
                tiles(use(2, base, KD, 512), [(P * i, P, i) for i in range(4)], TT).then_inc(S.prod_done, 1)
                yield
                yield from norm_rope(qk2(lane_a, "odq", 4, 0))
                w = use(3, base, 4, P)
                pe.wait_ge(S.pool_y, upto(S.pool_y))
                for g in range(4):
                    mm = pe.matmul(PS[:, g, 0:TT], w[:, g, :], POOLED[:, g, :], start=True, stop=True)
                mm.then_inc(S.prod_done, 1)
                yield from others(2)
                pe.wait_ge(S.mix_ready, upto(S.mix_ready))

            def window_kv(base):
                at = lane_b3.at
                w = use(1, base, KD, 384)
                tiles(w, [(0, P, at), (P, P, at + 1)], TT)
                tokens(w, 256, P, TILES2, [(at + 3, 0), (at + 3, P), (at + 3, 2 * P)]).then_inc(S.prod_done, 1)
                yield
                yield from norm_rope(qk2(lane_b3, "odk", 2, 4))

            def odd():
                norms[0] += 1
                input_norm(TT)
                pe.wait_ge(S.h_ready, upto(S.h_ready))
                second_half[0] = upto(S.h_ready)
                base = take(0)
                together(window_q(base), window_kv(base))
                pe.wait_ge(S.v_ready, upto(S.v_ready))
                together(softmax(swa_soft(0)), softmax(swa_soft(1)))
                project_out(base, 4, SEQ, KD, m0=META)

            def product3(o, hi, lo, xhi, xlo, first, last):
                pe.matmul(o, hi, xhi, start=first, stop=False)
                pe.matmul(o, hi, xlo, start=False, stop=False)
                return pe.matmul(o, lo, xhi, start=False, stop=last)

            def ffn(T, plain=True):
                norms[0] += 1
                input_norm(T, 3 if plain else 0)
                take(NSPLIT)
                n = ffns[0]

                def pair(i, r, new=False):
                    pe.wait_ge(S.w_lo, i + (n + r + 1))
                    pe.wait_ge(S.act_done, i + (acts[0] + r - 3))
                    if plain and r == 1:
                        pe.wait_ge(S.rstd_ready, norms[0])
                    hi, lo = (w[r % 2][:, 0:WIN].rearrange("p (k c) -> p k c", k=KD) for w in (whi, wlo))
                    for k in range(KD):
                        if new and k % group == 0:
                            pe.wait_ge(S.h_ready, h_before + k // group + 1)
                        for j in range(2):
                            mm = product3(PS[:, 2 * r + j, 0:T], hi[:, k, P * j:P * j + P], lo[:, k, P * j:P * j + P],
                                          Hhi[:, k, 0:T], Hlo[:, k, 0:T], k == 0, k == KD - 1)
                    mm.then_inc(S.ffn_done, 1)

                group = 1 if plain else 2
                h_before = upto(S.h_ready, 0)
                upto(S.h_ready, KD // group)
                with pe.Fori(0, KF // 4) as i:
                    for r in range(4):
                        pair(4 * i, r, r == 0)
                for r in range(2):
                    pair(KF - 2, r)
                acts[0] += KF
                with pe.Fori(0, 2) as i:
                    for r in range(4):
                        pe.wait_ge(S.w_lo, 4 * i + (n + KF + r + 1))
                        pe.wait_ge(S.x_tile, 4 * i + (xs[0] - 4 + r + 1)) if xs[0] >= 4 else None
                        hi, lo = (w[r % 2][:, 0:WOUT].rearrange("p (k c) -> p k c", k=KF) for w in (whi, wlo))
                        for k in range(KF):
                            if r == 0 and k == 0:
                                pe.wait_ge(S.act_done, acts[0] - 2)
                            if r == 0 and k == KF - 2:
                                pe.wait_ge(S.act_done, acts[0])
                            mm = product3(PS[:, 4 + r, 0:T], hi[:, k, :], lo[:, k, :], hidhi[:, k, 0:T], hidlo[:, k, 0:T],
                                          k == 0, k == KF - 1)
                        mm.then_inc(S.ffn_done, 1)
                xs[0] += KD
                ffns[0] += NSPLIT

            pe.wait_ge(S.con_in, 16)
            for l in range(DEPTH):
                mixer1(l)
                ffn(SEQ, plain=False)
            ffn(TT)
            even()
            ffn(TT)
            ffn(TT)
            odd()
            ffn(SEQ)

        @block.scalar
        def _(act):
            upto, take = counter(), chunk_counter()
            acts, ffns = [4], [0]

            def chain(ins):
                ins.then_inc(S.act_chain, 1)
                act.wait_ge(S.act_chain, upto(S.act_chain))

            def product(c):
                act.wait_ge(S.prod_done, chunks[c][2][1])

            def use_exp_and_ln():
                act.preload_act_table_set("natural_log_exp_and_others")

            def square(T, t0, m):
                act.wait_ge(S.x_tile, upto(S.x_tile))
                count = upto(S.sq_tile)
                if count > 2:
                    act.wait_ge(S.sq_sum, count - 2)
                act.activation(sq[:, m % 2, 0:T], X[:, m, t0:t0 + T], ACT.Square).then_inc(S.sq_tile, 1)

            def reciprocal_root(T, bank=0):
                act.wait_ge(S.sumsq, upto(S.sumsq))
                chain(act.activation(rstd[:, 0:T], PS[:, bank, 0:T], ACT.Ln, bias=C("eps", 1), scale=1.0 / D))
                act.activation(rstd[:, 0:T], rstd[:, 0:T], ACT.Exp, scale=-0.5).then_inc(S.rstd_ready, 1)

            def round_chunk(c, n, width, i=0):
                slot = c % 2
                act.wait_ge(WA[slot], 8 * i + 16 * (c // 2 + 1))
                if n >= 2:
                    act.wait_ge(S.ffn_done, i + (n - 1))
                act.copy(whi[n % 2][:, 0:width], wa[:, slot, 0:width]).then_inc(S.w_hi, 1)

            def round_tile(T, m):
                act.wait_ge(S.xg_ready, upto(S.xg_ready))
                act.copy(Hhi[:, m, 0:T], W0[:, m % 4, 0:T]).then_inc(S.hi_part, 1)

            def finish(T, t0, tail, kind, following):
                use_exp_and_ln()
                for m in tail:
                    square(T, t0, m)
                    if kind == "plain":
                        round_tile(T, m)
                reciprocal_root(T, 3 if kind == "plain" else 0)
                if kind == "conv":
                    round_input(T)
                if kind != "mixer":
                    round_chunk(following[0] + 1, following[1] + 1, WIN)

            def norm_rope(q):
                W = q.lane.W
                if q.norm:
                    squares, raw = (W[i][0:q.rows, 0:q.n, 0:q.T] for i in (1, 0))
                    if isinstance(q.src, int):
                        src = places[q.T][0:q.rows, q.src:q.src + q.n, 0:q.T]
                        act.activation(squares, src, ACT.Square)
                        act.copy(raw, src).then_inc(S.nr_sq, 1)
                    else:
                        act.activation(squares, q.src, ACT.Square).then_inc(S.nr_sq, 1)
                    yield from others(2)
                    act.wait_ge(S.nr_ms, upto(S.nr_ms))
                    m = q.groups[-1] + 1
                    w = W[1][0:q.rows, 0:m, 0:q.T]
                    step = m // len(q.widths)
                    for i, width in enumerate(q.widths):
                        ins = act.activation(w[:, i * step:(i + 1) * step, :],
                                             places[q.T][0:q.rows, q.ms + i * step:q.ms + (i + 1) * step, 0:q.T], ACT.Ln,
                                             bias=C("eps", 1, q.rows), scale=1.0 / width)
                    chain(ins)
                    act.activation(w, w, ACT.Exp, scale=-0.5).then_inc(S.nr_rs, 1)
                    yield
                if q.rot:
                    yield from others(2)
                yield
                act.wait_ge(S.nr_done, upto(S.nr_done))

            def softmax(a):
                pb, negmax, rowsum, sinkex = a.lane.PB, a.lane.negmax, a.lane.rowsum, a.lane.sinkex
                for qt, (q0, ql) in enumerate(a.tiles):
                    keys = q0 + ql
                    yield from others(2)
                    act.wait_ge(S.sm_nb, upto(S.sm_nb))
                    for h in range(4):
                        ex = act.activation(pb[0:ql, h, 0:keys], pb[0:ql, h, 0:keys], ACT.Exp, bias=negmax[0:ql, h:h + 1],
                                            scale=a.scale, accum_out=rowsum[0:ql, h:h + 1])
                    if a.sink:
                        act.activation(sinkex[0:ql, :], sinkex[0:ql, :], ACT.Exp).then_inc(S.sm_exp, 1)
                    else:
                        ex.then_inc(S.sm_exp, 1)
                    yield from others(3)
                    act.wait_ge(S.sm_pt, upto(S.sm_pt))
                    for kt in range(qt + 1):
                        t0, tl = a.tiles[kt]
                        cp = act.copy(a.lane.PT[0:tl, kt, :, q0:q0 + ql],
                                      PS[0:tl, transpose_bank(a, kt), :].rearrange("p (h q) -> p h q", h=4)[:, :, 0:ql])
                    cp.then_inc(S.sm_ptc, 1)
                    yield
                yield
                done = upto(S.pv_done)
                if a.copy_to is not None:
                    yield
                else:
                    act.wait_ge(S.pv_done, done)

            def moba_and_sticks(l, base):
                yield
                product(base)
                yield from norm_rope(moba_qk(l))
                yield from softmax(moba_soft())
                yield from norm_rope(head_norm(lane_a, l, 0))
                product(base + 3)
                act.copy(SBQ, places[SEQ][:, 4:8, :]).then_inc(S.qk_ready, 1)
                yield
                for kt in (1, 0):
                    R = SEQ - P * kt
                    w = W1[:, :, 0:R]
                    yield from others(2)
                    act.wait_ge(S.sb_na, upto(S.sb_na))
                    chain(act.activation(w, w, ACT.Exp))
                    act.activation(w, w, ACT.Ln, bias=1.0).then_inc(S.sb_l, 1)
                    yield from others(4)
                    act.wait_ge(S.sb_arg, upto(S.sb_arg))
                    act.activation(w, W0[:, :, 0:R], ACT.Exp).then_inc(S.sb_e, 1)
                    yield from others(2)
                yield
                act.wait_ge(S.pv_done, upto(S.pv_done))
                yield from norm_rope(head_norm(lane_a, l, 2))

            def mla_and_ssm(l, base):
                at, (w0, w1, w2), qk, ps = lane_b1.at, wb, lane_b1.QK, places[SEQ]
                yield
                product(base + 1)
                act.copy(KR[0:96, 0:SEQ], ps[0:96, at + 4, :])
                act.copy(rawdt[:, 0:SEQ], ps[0:4, at + 5, :]).then_inc(S.kr_ready, 1)
                yield from norm_rope(mla_c(l))
                yield
                act.wait_ge(S.sub_done, upto(S.sub_done))
                yield from norm_rope(mla_qk(l, 0))
                yield from norm_rope(mla_qk(l, 1))
                upto(S.sub_done)
                yield from softmax(mla_soft())
                yield from norm_rope(head_norm(lane_b1, l, 1))
                yield
                product(base + 5)
                act.wait_ge(S.ssm_na, upto(S.ssm_na))
                for n in range(4):
                    ins = act.activation(w0[:, n, 0:SEQ], ps[:, at + SSM_XBC[n], :], ACT.Identity, bias=A(f"ssmb{l}", n),
                                         scale=A(f"ssmw{l}", 4 * n + 3))
                ins.then_inc(S.ssm_init, 1)
                chain(act.activation(dts[:, 0:SEQ], dts[:, 0:SEQ], ACT.Exp))
                act.activation(dts[:, 0:SEQ], dts[:, 0:SEQ], ACT.Ln, bias=1.0)
                act.activation(ea, A(f"alog{l}", 0, 4), ACT.Exp).then_inc(S.ssm_l, 1)
                yield from others(2)
                act.wait_ge(S.ssm_conv, upto(S.ssm_conv))
                act.activation(ZS[:, :, 0:SEQ], ps[:, at + 6:at + 8, :], ACT.Silu)
                act.activation(qk[:, 0:4, 0:SEQ], w0[:, :, 0:SEQ], ACT.Silu).then_inc(S.ssm_xc, 1)
                use_exp_and_ln()
                yield from others(5)
                act.wait_ge(S.ssm_arg, upto(S.ssm_arg))
                act.activation(w1[:, :, 0:SEQ], w0[:, :, 0:SEQ], ACT.Exp)
                act.activation(w2[:, :, 0:P], w2[:, :, 0:P], ACT.Exp).then_inc(S.ssm_e, 1)
                yield from others(4)
                upto(S.pv_done)
                act.wait_ge(S.ssm_y, upto(S.ssm_y))
                yield from norm_rope(ssm_out(l))

            def mixer1(l):
                base = take(6)
                together(moba_and_sticks(l, base), mla_and_ssm(l, base))
                project_out(SEQ, META, "conv", PER1)

            def sparse(base):
                yield
                product(base)
                act.copy(IK, PS[:, 0, 0:TT]).then_inc(S.ix_ready, 1)
                yield from others(2)
                product(base + 2)
                act.copy(IQ[:, :, :], PS[:, 0:4, 0:TT]).then_inc(S.iq_ready, 1)
                yield
                for qt, (q0, ql) in enumerate(TILES2):
                    for g in range(2):
                        yield
                        act.wait_ge(S.ix_logit, upto(S.ix_logit))
                        if qt or g:
                            act.wait_ge(S.ix_acc, upto(S.ix_acc))
                        act.activation(W0[0:ql, :, 0:q0 + ql], PS[0:ql, 0:4, 0:q0 + ql], ACT.Relu).then_inc(S.ix_relu, 1)
                        yield
                act.wait_ge(S.ix_acc, upto(S.ix_acc))
                for k in range(2):
                    yield
                    product(base + 7 + k)
                    yield from norm_rope(qk2(lane_a, ("evq", "evk")[k], 4, 4 * k))
                yield from others(2)
                yield from softmax(dsa_soft(0))

            def retention(base):
                at = lane_b2.at
                for k in range(2):
                    yield
                    yield from norm_rope(ret_qk(k))
                yield from others(4)
                for g in range(2):
                    yield
                    product(base + (6, 9)[g])
                    act.activation(G[:, 4 * g:4 * g + 4, :], PS[:, at:at + 4, 0:TT], ACT.Silu).then_inc(S.gate_ready, 1)
                    use_exp_and_ln()
                    yield
                    yield from others(2 * len(TILES2) + 1)
                    act.wait_ge(S.rt_pv, g + 1)
                    yield from norm_rope(ret_out(g))
                yield from softmax(dsa_soft(1))

            def even():
                base = take(11)
                together(sparse(base), retention(base))
                project_out(TT, 0, "plain")

            def window_q(base):
                yield
                product(base)
                act.copy(DX, PS[:, 0:4, 0:TT]).then_inc(S.dx_ready, 1)
                yield from others(2)
                product(base + 2)
                yield from norm_rope(qk2(lane_a, "odq", 4, 0))

            def window_kv(base):
                yield
                product(base + 1)
                yield from norm_rope(qk2(lane_b3, "odk", 2, 4))

            def odd():
                base = take(4)
                together(window_q(base), window_kv(base))
                together(softmax(swa_soft(0)), softmax(swa_soft(1)))
                project_out(SEQ, META, "plain")

            def project_out(T, t0, kind, per=2):
                c = take(KD // per) + KD // per
                for m in range(6):
                    square(T, t0, m)
                    if kind == "plain":
                        round_tile(T, m)
                round_chunk(c, ffns[0], WIN)
                finish(T, t0, range(6, 8), kind, (c, ffns[0]))

            def ffn(T, nxt, conv=None):
                c, n = take(NSPLIT), ffns[0]
                ffns[0] += NSPLIT

                def pair(i, r, prepare):
                    if conv is None:
                        prepare()
                    act.wait_ge(S.ffn_done, i + (n + r + 1))
                    act.wait_ge(S.act_done, i + (acts[0] + r - 1))
                    for j in range(2 if conv is not None else 0):
                        at = PC[conv] + 4 * j
                        tap = par[:, bass.ds(i * 8 + (8 * r + at + 2), 1)]
                        bias = par[:, bass.ds(i * 8 + (8 * r + at + 3), 1)]
                        ins = act.activation(W1[:, 2 * (r % 2) + j, 0:T], PS[:, 2 * r + j, 0:T], ACT.Identity, bias=bias,
                                             scale=tap)
                    if conv is not None:
                        ins.then_inc(S.conv_init, 1)
                        prepare()
                    act.wait_ge(S.gate_in, i + (convs[0] + r + 1))
                    act.activation(W2[:, r % 2, 0:T], W1[:, 2 * (r % 2), 0:T], ACT.Silu).then_inc(S.silu_done, 1)

                act.preload_act_table(ACT.Silu)
                with act.Fori(0, KF // 4) as i:
                    for r in range(4):
                        pair(4 * i, r, lambda: round_chunk(c + r + 2, n + r + 2, WIN, 4 * i))
                for r in range(2):
                    pair(KF - 2, r, lambda: round_chunk(c + KF + r, n + KF + r, WOUT))
                acts[0] += KF
                convs[0] += KF
                for m in range(KD - 1):
                    if m < KD - 2:
                        round_chunk(c + KF + m + 2, n + KF + m + 2, WOUT)
                    elif nxt and nxt[2] != "mixer":
                        round_chunk(c + NSPLIT, n + NSPLIT, WIN)
                    if nxt:
                        square(nxt[0], nxt[1], m)
                    if nxt and nxt[2] == "plain":
                        round_tile(nxt[0], m)
                if nxt:
                    finish(*nxt[:2], [KD - 1], nxt[2], (c + NSPLIT, n + NSPLIT))

            def round_input(T):
                for j in range(4):
                    act.wait_ge(S.hn_part, upto(S.hn_part))
                    act.copy(Hhi[:, 2 * j:2 * j + 2, 0:T], (W0, W1)[j // 2][:, 2 * (j % 2):2 * (j % 2) + 2, 0:T]
                             ).then_inc(S.hi_part, 1)

            convs = [0]
            act.wait_ge(S.x_in, 16)
            use_exp_and_ln()
            for m in range(KD):
                count = upto(S.sq_tile)
                if count > 2:
                    act.wait_ge(S.sq_sum, count - 2)
                act.activation(sq[:, m % 2, 0:SEQ], X[:, m, META:TT], ACT.Square).then_inc(S.sq_tile, 1)
            act.wait_ge(S.con_in, 16)
            reciprocal_root(SEQ)
            act.wait_ge(S.rope_ang, 1)
            for j in range(2):
                act.activation(rope[:, 2 * j + 1, :], W1[:, j, 0:SEQ], ACT.Sin)
                ins = act.activation(rope[:, 2 * j, :], W2[:, j, 0:SEQ], ACT.Sin, bias=C("halfpi", 1), scale=-1.0)
            ins.then_inc(S.rope_ready, 1)
            act.wait_ge(S.rope_ready, 1)
            use_exp_and_ln()
            act.wait_ge(S.par_in, 16)
            act.wait_ge(S.meta_in, 16)
            for l in range(DEPTH):
                mixer1(l)
                ffn(SEQ, (SEQ, META, "mixer") if l < DEPTH - 1 else (TT, 0, "plain"), f"fconv{l}")
            ffn(TT, (TT, 0, "mixer"))
            even()
            ffn(TT, (TT, 0, "plain"))
            ffn(TT, (TT, 0, "mixer"))
            odd()
            ffn(SEQ, None)

        @block.vector
        def _(dve):
            upto, take = counter(), chunk_counter()
            xs, convs, silus, ffns = [0], [0], [0], [0]

            def chain(ins):
                ins.then_inc(S.dve_chain, 1)
                dve.wait_ge(S.dve_chain, upto(S.dve_chain))

            def product(c):
                dve.wait_ge(S.prod_done, chunks[c][2][1])

            def input_norm(T, t0, gain):
                dve.wait_ge(S.rstd_ready, upto(S.rstd_ready))
                for k in range(KD):
                    ins = dve.scalar_tensor_tensor(out=H[:, k, 0:T], in0=X[:, k, t0:t0 + T], scalar=A(gain, k),
                                                   in1=rstd[:, 0:T], op0=ALU.mult, op1=ALU.mult)
                    if k % 4 == 3:
                        ins.then_inc(S.h_ready, 1)

            def input_norm_split(T, t0, gain, c, n):
                dve.wait_ge(S.rstd_ready, upto(S.rstd_ready))
                def tiles(j):
                    return (W0, W1)[j // 2][:, 2 * (j % 2):2 * (j % 2) + 2, 0:T]

                def normed(j):
                    for i in range(2):
                        k = 2 * j + i
                        ins = dve.scalar_tensor_tensor(out=tiles(j)[:, i, :], in0=X[:, k, t0:t0 + T], scalar=A(gain, k),
                                                       in1=rstd[:, 0:T], op0=ALU.mult, op1=ALU.mult)
                    ins.then_inc(S.hn_part, 1)

                normed(0)
                for j in range(4):
                    if j < 3:
                        normed(j + 1)
                    dve.wait_ge(S.hi_part, upto(S.hi_part))
                    dve.tensor_tensor(out=Hlo[:, 2 * j:2 * j + 2, 0:T], in0=tiles(j),
                                      in1=Hhi[:, 2 * j:2 * j + 2, 0:T].bitcast(F32), op=ALU.subtract).then_inc(S.h_ready, 1)
                rest_of_chunk(c, n, WIN)

            def rest_of_chunk(c, n, width, i=0):
                dve.wait_ge(S.w_hi, i + (n + 1))
                dve.tensor_tensor(out=wlo[n % 2][:, 0:width], in0=wa[:, c % 2, 0:width],
                                  in1=whi[n % 2][:, 0:width].bitcast(F32), op=ALU.subtract).then_inc(S.w_lo, 1)

            def clear_sum(T):
                dve.memset(sqsum[:, 0:T], 0.0).then_inc(S.dve_chain, 1)
                dve.wait_ge(S.dve_chain, upto(S.dve_chain))

            def add_square(T):
                count = upto(S.sq_tile)
                dve.wait_ge(S.sq_tile, count)
                dve.tensor_tensor(out=sqsum[:, 0:T], in0=sqsum[:, 0:T], in1=sq[:, (count - 1) % 2, 0:T],
                                  op=ALU.add).then_inc(S.sq_sum, 1)
                dve.wait_ge(S.sq_sum, count)

            def add_tile(m, T, t0, scale, product):
                x = X[:, m, t0:t0 + T]
                dve.scalar_tensor_tensor(out=x, in0=product, scalar=scale, in1=x, op0=ALU.mult,
                                         op1=ALU.add).then_inc(S.x_tile, 1)
                xs[0] += 1

            def gained_tile(m, T, t0, gain, added):
                dve.wait_ge(S.x_tile, added)
                dve.tensor_scalar(W0[:, m % 4, 0:T], X[:, m, t0:t0 + T], A(gain, m), None, ALU.mult).then_inc(S.xg_ready, 1)

            def rest_of_tile(m, T):
                dve.wait_ge(S.hi_part, upto(S.hi_part))
                dve.tensor_tensor(out=Hlo[:, m, 0:T], in0=W0[:, m % 4, 0:T], in1=Hhi[:, m, 0:T].bitcast(F32),
                                  op=ALU.subtract).then_inc(S.h_ready, 1)

            def project_out(T, t0, gain, per=2):
                c = take(KD // per)
                before = chunks[c][2][1] - per // 2
                clear_sum(T)
                for j in range(KD // 2):
                    dve.wait_ge(S.prod_done, before + j + 1)
                    for m in (2 * j, 2 * j + 1):
                        add_tile(m, T, t0, 1.0, PS[:, m, 0:T])
                        if gain:
                            gained_tile(m, T, t0, gain, xs[0])
                    for m in (2 * j, 2 * j + 1):
                        add_square(T)
                        if gain:
                            rest_of_tile(m, T)
                    if j == 2:
                        rest_of_chunk(c + KD // per, ffns[0], WIN)

            def norm_rope(q):
                W, ps = q.lane.W, places[q.T]
                w0, w1, w2 = (w[0:q.rows, 0:q.n, 0:q.T] for w in W)
                tail = q.rot or q.post is not None
                if q.norm:
                    yield from others(3)
                    dve.wait_ge(S.nr_rs, upto(S.nr_rs))
                    for i in range(q.n):
                        rs = W[1][0:q.rows, q.groups[i], 0:q.T]
                        o = (W[2][0:q.rows, i, 0:q.T] if tail else q.dst[:, i, :])
                        if q.gains:
                            ins = dve.scalar_tensor_tensor(out=o, in0=W[0][0:q.rows, i, 0:q.T], scalar=q.gains[i], in1=rs,
                                                           op0=ALU.mult, op1=ALU.mult)
                        else:
                            ins = dve.tensor_tensor(out=o, in0=W[0][0:q.rows, i, 0:q.T], in1=rs, op=ALU.mult)
                else:
                    ins = dve.tensor_copy(w2, ps[0:q.rows, q.src:q.src + q.n, 0:q.T])
                if not tail:
                    ins.then_inc(S.nr_done, 1)
                    dve.wait_ge(S.nr_done, upto(S.nr_done))
                    yield
                    return
                if q.rot:
                    ins.then_inc(S.nr_n, 1)
                    dve.wait_ge(S.nr_n, upto(S.nr_n))
                    _, cos, sin = q.rot
                    dve.tensor_tensor(out=w0, in0=w2, in1=per_head(cos, q.n), op=ALU.mult)
                    yield from others(2)
                    dve.wait_ge(S.nr_rot, upto(S.nr_rot))
                    chain(dve.tensor_tensor(out=w1, in0=ps[0:q.rows, q.ms:q.ms + q.n, 0:q.T], in1=per_head(sin, q.n),
                                            op=ALU.mult))
                    if q.post is None:
                        dve.tensor_tensor(out=q.dst, in0=w0, in1=w1, op=ALU.add).then_inc(S.nr_done, 1)
                        dve.wait_ge(S.nr_done, upto(S.nr_done))
                        yield
                        return
                    chain(dve.tensor_tensor(out=w2, in0=w0, in1=w1, op=ALU.add))
                else:
                    chain(ins)
                dve.tensor_tensor(out=q.dst, in0=w2, in1=q.post, op=ALU.mult).then_inc(S.nr_done, 1)
                dve.wait_ge(S.nr_done, upto(S.nr_done))
                yield

            def softmax(a):
                lane, transposed = a.lane, 0
                negmax, rowsum, sinkex = lane.negmax, lane.rowsum, lane.sinkex
                for qt, (q0, ql) in enumerate(a.tiles):
                    keys = q0 + ql
                    pb = lane.PB[0:ql, :, 0:keys]
                    yield
                    dve.wait_ge(S.sm_qk, upto(S.sm_qk))
                    if qt:
                        dve.wait_ge(S.sm_pt, transposed)
                    chain(dve.tensor_tensor(out=pb, in0=places[a.T][0:ql, lane.at:lane.at + 4, 0:keys],
                                            in1=per_head(a.masks[qt][0:ql, 0:keys], 4), op=ALU.add))
                    chain(dve.tensor_reduce(out=negmax[0:ql, :], in_=pb, axis=AX.X, op=ALU.max))
                    if a.sink:
                        sk = par[0:ql, PC["sink"] + a.head0:PC["sink"] + a.head0 + 4]
                        chain(dve.tensor_scalar(negmax[0:ql, :], negmax[0:ql, :], a.scale, None, ALU.mult))
                        chain(dve.tensor_tensor(out=negmax[0:ql, :], in0=negmax[0:ql, :], in1=sk, op=ALU.max))
                        chain(dve.tensor_scalar(negmax[0:ql, :], negmax[0:ql, :], -1.0, None, ALU.mult))
                        dve.tensor_tensor(out=sinkex[0:ql, :], in0=negmax[0:ql, :], in1=sk, op=ALU.add).then_inc(S.sm_nb, 1)
                    else:
                        dve.tensor_scalar(negmax[0:ql, :], negmax[0:ql, :], -a.scale, None, ALU.mult).then_inc(S.sm_nb, 1)
                    yield from others(2)
                    dve.wait_ge(S.sm_exp, upto(S.sm_exp))
                    if a.sink:
                        chain(dve.tensor_tensor(out=rowsum[0:ql, :], in0=rowsum[0:ql, :], in1=sinkex[0:ql, :], op=ALU.add))
                    chain(dve.reciprocal(rowsum[0:ql, :], rowsum[0:ql, :]))
                    dve.tensor_tensor(out=pb, in0=pb, in1=rowsum[0:ql, :].unsqueeze(2).to_broadcast([ql, 4, keys]),
                                      op=ALU.mult).then_inc(S.sm_p, 1)
                    transposed = upto(S.sm_pt)
                    yield from others(3)
                yield
                done = upto(S.pv_done)
                if a.copy_to is not None:
                    dve.wait_ge(S.pv_done, done)
                    dve.tensor_copy(a.copy_to, places[a.T][:, lane.at:lane.at + 2, 0:a.T]).then_inc(S.pv_copied, 1)
                    yield

            def copy_heads(vp, rows, kt, head0, n, src):
                s = src.rearrange("p (h d) -> p h d", h=n)
                dve.tensor_copy(vp[0:rows, kt, head0:head0 + n:2, 0:HD], s[:, 0:n:2, :])
                return dve.tensor_copy(vp[0:rows, kt, head0 + 1:head0 + n:2, HD:P], s[:, 1:n:2, :])

            def clear_values():
                dve.memset(VP[:], 0.0).then_inc(S.v_zero, 1)
                dve.wait_ge(S.v_zero, upto(S.v_zero))

            def moba_and_sticks(l, base):
                yield
                yield from norm_rope(moba_qk(l))
                product(base + 2)
                for kt in range(2):
                    ins = copy_heads(VP, P, kt, 0, 8, PS[:, 2 + kt, :])
                ins.then_inc(S.v_ready, 1)
                yield from softmax(moba_soft())
                yield from norm_rope(head_norm(lane_a, l, 0))
                yield
                for kt in (1, 0):
                    yield
                    R = SEQ - P * kt
                    w0, w1 = W0[:, :, 0:R], W1[:, :, 0:R]
                    sp_ = (W2 if kt == 0 else QK[:, 4:8, :])[:, :, 0:R]
                    strict = per_head(C("strict", SEQ)[:, 0:R], 4)
                    dve.wait_ge(S.sb_z, upto(S.sb_z))
                    chain(dve.tensor_scalar(w0, places[SEQ][:, 0:4, 0:R], HD ** -0.5, None, ALU.mult))
                    dve.scalar_tensor_tensor(out=w1, in0=w0, scalar=-1.0, in1=w0, op0=ALU.mult,
                                             op1=ALU.min).then_inc(S.sb_na, 1)
                    yield from others(2)
                    dve.wait_ge(S.sb_l, upto(S.sb_l))
                    chain(dve.scalar_tensor_tensor(out=sp_, in0=w0, scalar=0.0, in1=w1, op0=ALU.max, op1=ALU.add))
                    dve.tensor_tensor(out=sp_, in0=sp_, in1=strict, op=ALU.mult).then_inc(S.sb_sp, 1)
                    chain(dve.scalar_tensor_tensor(out=w0, in0=w0, scalar=0.0, in1=w1, op0=ALU.min, op1=ALU.subtract))
                    yield from others(2)
                    dve.wait_ge(S.sb_tail, upto(S.sb_tail))
                    for j in range(2):
                        ins = dve.tensor_tensor(out=W0[:, 2 * j:2 * j + 2, 0:R], in0=W0[:, 2 * j:2 * j + 2, 0:R],
                                                in1=PS[:, 2 + j, 0:2 * R].rearrange("p (h t) -> p h t", h=2),
                                                op=ALU.subtract)
                    ins.then_inc(S.sb_arg, 1)
                    yield from others(2)
                    dve.wait_ge(S.sb_e, upto(S.sb_e))
                    dve.tensor_tensor(out=PT[:, kt, :, P * kt:SEQ], in0=w1, in1=strict, op=ALU.mult).then_inc(S.sb_a, 1)
                    dve.wait_ge(S.sb_a, upto(S.sb_a))
                    yield
                yield
                upto(S.pv_done)
                yield from norm_rope(head_norm(lane_a, l, 2))

            def mla_and_ssm(l, base):
                at, (w0, w1, w2), qk, ps = lane_b1.at, wb, lane_b1.QK, places[SEQ]
                bank = at // 2
                yield
                yield from norm_rope(mla_c(l))
                yield
                upto(S.sub_done)
                yield from norm_rope(mla_qk(l, 0))
                yield from norm_rope(mla_qk(l, 1))
                dve.wait_ge(S.sub_done, upto(S.sub_done))
                for kt in range(2):
                    ins = copy_heads(lane_b1.VP, P, kt, 0, 4, PS[:, bank, 256 * kt:256 * kt + 256])
                ins.then_inc(S.vb_ready, 1)
                yield from softmax(mla_soft())
                yield from norm_rope(head_norm(lane_b1, l, 1))
                chain(dve.tensor_scalar(rawdt[:, 0:SEQ], rawdt[:, 0:SEQ], A(f"dtb{l}", 0, 4), None, ALU.add))
                dve.scalar_tensor_tensor(out=dts[:, 0:SEQ], in0=rawdt[:, 0:SEQ], scalar=-1.0, in1=rawdt[:, 0:SEQ],
                                         op0=ALU.mult, op1=ALU.min).then_inc(S.ssm_na, 1)
                yield from others(2)
                dve.wait_ge(S.ssm_init, upto(S.ssm_init))
                for s in range(1, 4):
                    for n in range(4):
                        ins = dve.scalar_tensor_tensor(out=w0[:, n, s:SEQ], in0=ps[:, at + SSM_XBC[n], 0:SEQ - s],
                                                       scalar=A(f"ssmw{l}", 4 * n + 3 - s), in1=w0[:, n, s:SEQ],
                                                       op0=ALU.mult, op1=ALU.add)
                    if s < 3:
                        chain(ins)
                ins.then_inc(S.ssm_conv, 1)
                dve.wait_ge(S.ssm_l, upto(S.ssm_l))
                chain(dve.scalar_tensor_tensor(out=dt_[:, 0:SEQ], in0=rawdt[:, 0:SEQ], scalar=0.0, in1=dts[:, 0:SEQ],
                                               op0=ALU.max, op1=ALU.add))
                chain(dve.tensor_scalar(dts[:, 0:SEQ], dt_[:, 0:SEQ], ea, -1.0, ALU.mult, ALU.mult))
                dve.tensor_tensor_scan(acum[:, 0:SEQ], C("ones", P, 4)[:, 0:1].to_broadcast([4, SEQ]), dts[:, 0:SEQ], 0.0,
                                       ALU.mult, ALU.add).then_inc(S.ssm_dt, 1)
                yield from others(3)
                dve.wait_ge(S.ssm_tr, upto(S.ssm_tr))
                chain(dve.tensor_copy(cols, PS[:, bank + 1, 0:16]))
                for kt in range(2):
                    ins = copy_heads(lane_b1.VP, P, kt, 0, 4, PS[:, bank, 256 * kt:256 * kt + 256])
                ins.then_inc(S.vb_ready, 1)
                yield from others(2)
                dve.wait_ge(S.ssm_cb, upto(S.ssm_cb))
                for kt, w in ((0, w0), (1, w2)):
                    R = SEQ - P * kt
                    for h in range(4):
                        ins = dve.scalar_tensor_tensor(out=w[:, h, 0:R], in0=ps[:, at + 4 + h, P * kt:SEQ],
                                                       scalar=cols[:, 8 + 4 * kt + h:9 + 4 * kt + h],
                                                       in1=C("ssmmask", SEQ)[:, 0:R], op0=ALU.subtract, op1=ALU.min)
                ins.then_inc(S.ssm_arg, 1)
                yield from others(2)
                dve.wait_ge(S.ssm_e, upto(S.ssm_e))
                for kt, w in ((0, w1), (1, w2)):
                    R = SEQ - P * kt
                    for h in range(4):
                        ins = dve.scalar_tensor_tensor(out=lane_b1.PT[:, kt, HEADS1[h], P * kt:SEQ],
                                                       in0=PS[:, bank + h // 2, 256 * kt:256 * kt + R],
                                                       scalar=cols[:, 4 * kt + h:4 * kt + h + 1], in1=w[:, h, 0:R],
                                                       op0=ALU.mult, op1=ALU.mult)
                ins.then_inc(S.ssm_m, 1)
                yield from others(2)
                dve.wait_ge(S.pv_done, upto(S.pv_done))
                for n in range(2):
                    ins = dve.scalar_tensor_tensor(out=w0[:, n, 0:SEQ], in0=qk[:, n, 0:SEQ], scalar=A(f"dskip{l}", n),
                                                   in1=ps[:, at + 4 + n, :], op0=ALU.mult, op1=ALU.add)
                chain(ins)
                dve.tensor_tensor(out=w0[:, 0:2, 0:SEQ], in0=w0[:, 0:2, 0:SEQ], in1=ZS[:, :, 0:SEQ],
                                  op=ALU.mult).then_inc(S.ssm_y, 1)
                dve.wait_ge(S.ssm_y, upto(S.ssm_y))
                yield from norm_rope(ssm_out(l))

            def rope_angles():
                pos, turns, ang, mag = W0[:, 0, 0:SEQ], W0[:, 1, 0:SEQ], W1, W2
                chain(dve.tensor_copy(pos, posi))
                two_pi = 2 * np.pi
                c1 = 6.28125
                c2 = float(np.float32(int((two_pi - c1) * 2 ** 20) / 2 ** 20))
                c3 = float(np.float32(two_pi - c1 - c2))
                magic = float(1.5 * 2 ** 23)
                for j in range(2):
                    a, m = ang[:, j, 0:SEQ], mag[:, j, 0:SEQ]
                    chain(dve.tensor_scalar(a, pos, C("inv", 2)[:, j:j + 1], None, ALU.mult))
                    chain(dve.tensor_scalar(turns, a, float(1 / two_pi), magic, ALU.mult, ALU.add))
                    chain(dve.tensor_scalar(turns, turns, magic, None, ALU.subtract))
                    for part in (c1, c2, c3):
                        chain(dve.scalar_tensor_tensor(out=a, in0=turns, scalar=-part, in1=a, op0=ALU.mult, op1=ALU.add))
                    chain(dve.tensor_scalar(a, a, 3.1415925, -3.1415925, ALU.min, ALU.max))
                    ins = dve.scalar_tensor_tensor(out=m, in0=a, scalar=-1.0, in1=a, op0=ALU.mult, op1=ALU.max)
                ins.then_inc(S.rope_ang, 1)
                dve.wait_ge(S.rope_ready, 1)

            def mixer1(l):
                input_norm(SEQ, META, f"mixg{l}")
                if l == 0:
                    dve.wait_ge(S.pos_in, 16)
                    rope_angles()
                clear_values()
                base = take(6)
                together(moba_and_sticks(l, base), mla_and_ssm(l, base))
                project_out(SEQ, META, None, PER1)

            def sparse(base):
                yield
                product(base)
                for qt, (q0, ql) in enumerate(TILES2):
                    ins = dve.tensor_scalar(iwc[0:ql, 8 * qt:8 * qt + 8], PS[0:ql, 1, 8 * qt:8 * qt + 8],
                                            8 ** -0.5 * HD ** -0.5, None, ALU.mult)
                ins.then_inc(S.iw_ready, 1)
                dve.wait_ge(S.iw_ready, 1)
                dve.wait_ge(S.mask_in, 16)
                yield from others(3)
                for qt, (q0, ql) in enumerate(TILES2):
                    keys = q0 + ql
                    sc, adm, pk = W2[0:ql, 0, 0:keys], mask[0:ql, qt, 0:keys], picked[0:ql, qt, 0:keys]
                    for g in range(2):
                        yield from others(2)
                        dve.wait_ge(S.ix_relu, upto(S.ix_relu))
                        for j in range(4):
                            h = 4 * g + j
                            ins = dve.scalar_tensor_tensor(out=sc, in0=W0[0:ql, j, 0:keys],
                                                           scalar=iwc[0:ql, 8 * qt + h:8 * qt + h + 1],
                                                           in1=adm if h == 0 else sc, op0=ALU.mult, op1=ALU.add)
                            if j < 3:
                                chain(ins)
                        ins.then_inc(S.ix_acc, 1)
                        dve.wait_ge(S.ix_acc, upto(S.ix_acc))
                    for _ in range(TOPK // 8):
                        chain(dve.max(out=top8[0:ql, :], in_=sc))
                        chain(dve.match_replace(out=sc, in_to_replace=top8[0:ql, :], in_values=sc, imm_value=TAKEN))
                    chain(dve.tensor_scalar(pk, sc, TAKEN / 2, NEG, ALU.is_ge, ALU.mult))
                    dve.tensor_tensor(out=pk, in0=pk, in1=adm, op=ALU.add).then_inc(S.picked_ready, 1)
                    dve.wait_ge(S.picked_ready, upto(S.picked_ready))
                for k in range(2):
                    yield
                    yield from norm_rope(qk2(lane_a, ("evq", "evk")[k], 4, 4 * k))
                yield
                product(base + 10)
                for kt, (t0, tl) in enumerate(TILES2):
                    ins = copy_heads(VP, tl, kt, 0, 8, PS[0:tl, kt, :])
                ins.then_inc(S.v_ready, 1)
                yield
                yield from softmax(dsa_soft(0))

            def retention(base):
                lane = lane_b2
                at = lane.at
                for k in range(2):
                    yield
                    product(base + (1, 3)[k])
                    yield from norm_rope(ret_qk(k))
                for g in range(2):
                    yield
                    product(base + 4 + g)
                    for kt, (t0, tl) in enumerate(TILES2):
                        ins = dve.tensor_copy(lane.VP[0:tl, kt, 4 * g:4 * g + 4, :],
                                              PS[0:tl, at + kt, :].rearrange("p (h d) -> p h d", h=4))
                    ins.then_inc(S.vb_ready, 1)
                    yield
                for g in range(2):
                    yield from others(2)
                    for kt, (t0, tl) in enumerate(TILES2):
                        yield
                        dve.wait_ge(S.rt_s, upto(S.rt_s))
                        for j in range(4):
                            c0 = CC["kdec"] + 8 * kt + 4 * g + j
                            ins = dve.scalar_tensor_tensor(out=lane.PT[kt][0:tl, j, :], in0=PS[0:tl, at + j, 0:TT - t0],
                                                           scalar=con[0:tl, c0:c0 + 1], in1=C("tri", TT)[0:tl, 0:TT - t0],
                                                           op0=ALU.mult, op1=ALU.mult)
                        ins.then_inc(S.rt_m, 1)
                        yield
                    yield
                    dve.wait_ge(S.gate_ready, upto(S.gate_ready))
                    yield from norm_rope(ret_out(g))
                yield from softmax(dsa_soft(1))

            def even():
                input_norm(TT, 0, "mix2g0")
                dve.wait_ge(S.con2_in, 16)
                clear_values()
                base = take(11)
                together(sparse(base), retention(base))
                project_out(TT, 0, "ffn2g0")

            def window_q(base):
                yield from others(3)
                yield from norm_rope(qk2(lane_a, "odq", 4, 0))
                yield
                product(base + 3)
                for g in range(4):
                    ins = dve.tensor_scalar(MIX[:, 4 + g, :], PS[:, g, 0:TT], A("dscale", g), None, ALU.mult)
                ins.then_inc(S.mix_ready, 1)
                yield

            def window_kv(base):
                yield
                product(base + 1)
                for kt, (t0, tl) in enumerate(TILES2):
                    for g in range(2):
                        src = PS[0:tl, 7, P * kt + HD * g:P * kt + HD * g + HD].unsqueeze(1).to_broadcast([tl, 2, HD])
                        dve.tensor_copy(VP[0:tl, kt, 4 * g:4 * g + 4:2, 0:HD], src)
                        ins = dve.tensor_copy(VP[0:tl, kt, 4 * g + 1:4 * g + 4:2, HD:P], src)
                ins.then_inc(S.v_ready, 1)
                yield from norm_rope(qk2(lane_b3, "odk", 2, 4))

            def pooling():
                yield from others(2)
                dve.wait_ge(S.dx_ready, 1)
                src, bufs = DX, [PW0, PW1, PW0, PW1]
                for lv, w in enumerate(bufs):
                    s = 1 << lv
                    dve.tensor_copy(w[:, lv:4, 0:s], src[:, lv:4, 0:s])
                    chain(dve.tensor_tensor(out=w[:, lv:4, s:TT], in0=src[:, lv:4, s:TT], in1=src[:, lv:4, 0:TT - s],
                                            op=ALU.add))
                    fix = C("cfix", 64)[:, 16 * lv:16 * lv + 16]
                    dve.tensor_copy(POOLED[:, lv, 16:TT], w[:, lv, 16:TT])
                    chain(dve.tensor_tensor(out=POOLED[:, lv, 0:16], in0=w[:, lv, 0:16], in1=fix, op=ALU.mult))
                    ins = dve.scalar_tensor_tensor(out=POOLED[:, lv, :], in0=POOLED[:, lv, :], scalar=1.0 / (2 << lv),
                                                   in1=DX[:, lv, :], op0=ALU.mult, op1=ALU.subtract)
                    src = w
                    if lv < 3:
                        yield
                ins.then_inc(S.pool_y, 1)

            def odd():
                input_norm(TT, 0, "mix2g1")
                clear_values()
                base = take(4)
                together(window_q(base), window_kv(base), pooling())
                dve.wait_ge(S.swa_in, 16)
                together(softmax(swa_soft(0)), softmax(swa_soft(1)))
                project_out(SEQ, META, "ffn2g1")

            def ffn(T, t0, gain, scale, nxt, conv=None):
                c, n = take(NSPLIT), ffns[0]
                ffns[0] += NSPLIT
                if conv is not None:
                    input_norm_split(T, t0, gain, c + 1, n + 1)
                else:
                    rest_of_chunk(c + 1, n + 1, WIN)
                    dve.wait_ge(S.rstd_ready, upto(S.rstd_ready))

                def pair(i, r, hi, lo, prepare):
                    gate_up = W1[:, 2 * (r % 2):2 * (r % 2) + 2, 0:T]
                    if conv is None:
                        prepare()
                        dve.wait_ge(S.ffn_done, i + (n + r + 1))
                        dve.tensor_tensor(out=gate_up[:, 0, :], in0=PS[:, 2 * r, 0:T], in1=rstd[:, 0:T],
                                          op=ALU.mult).then_inc(S.gate_in, 1)
                        link(dve.tensor_tensor(out=gate_up[:, 1, :], in0=PS[:, 2 * r + 1, 0:T], in1=rstd[:, 0:T],
                                               op=ALU.mult), i, r, 0)
                    else:
                        dve.wait_ge(S.conv_init, i + (convs[0] + r + 1))
                        for s in (1, 2):
                            for j in range(2):
                                tap = par[:, bass.ds(i * 8 + (8 * r + PC[conv] + 4 * j + 2 - s), 1)]
                                w = gate_up[:, j, s:T]
                                ins = dve.scalar_tensor_tensor(out=w, in0=PS[:, 2 * r + j, 0:T - s], scalar=tap, in1=w,
                                                               op0=ALU.mult, op1=ALU.add)
                            if s == 1:
                                link(ins, i, r, 0)
                        ins.then_inc(S.gate_in, 1)
                        prepare()
                    dve.wait_ge(S.silu_done, i + (silus[0] + r + 1))
                    full = W2[:, 2 + r % 2, 0:T]
                    link(dve.tensor_tensor(out=full, in0=W2[:, r % 2, 0:T], in1=gate_up[:, 1, :], op=ALU.mult), i, r, 1)
                    link(dve.tensor_copy(hi, full), i, r, 2)
                    dve.tensor_tensor(out=lo, in0=full, in1=hi.bitcast(F32), op=ALU.subtract).then_inc(S.act_done, 1)

                per = 3
                chained = upto(S.dve_chain, 0)

                def link(ins, i, r, step):
                    ins.then_inc(S.dve_chain, 1)
                    dve.wait_ge(S.dve_chain, per * i + (chained + per * r + step + 1))

                with dve.Fori(0, KF // 4) as i:
                    for r in range(4):
                        hi, lo = (t[:, bass.ds(4 * i + r, 1), 0:T].rearrange("p o t -> p (o t)") for t in (hidhi, hidlo))
                        pair(4 * i, r, hi, lo, lambda: rest_of_chunk(c + r + 2, n + r + 2, WIN, 4 * i))
                for r in range(2):
                    pair(KF - 2, r, hidhi[:, KF - 2 + r, 0:T], hidlo[:, KF - 2 + r, 0:T],
                         lambda: rest_of_chunk(c + KF + r, n + KF + r, WOUT))
                upto(S.dve_chain, per * KF)
                silus[0] += KF
                if conv is not None:
                    convs[0] += KF
                if nxt:
                    dve.wait_ge(S.meta_in, 16)
                    clear_sum(nxt[0])
                for m in range(KD):
                    if m < KD - 2:
                        rest_of_chunk(c + KF + m + 2, n + KF + m + 2, WOUT)
                    elif m == KD - 2 and nxt and nxt[1]:
                        rest_of_chunk(c + NSPLIT, n + NSPLIT, WIN)
                    dve.wait_ge(S.ffn_done, n + KF + m + 1)
                    add_tile(m, T, t0, scale, PS[:, 4 + m % 4, 0:T])
                    if nxt and nxt[1]:
                        gained_tile(m, nxt[0], 0, nxt[1], xs[0])
                    if nxt:
                        add_square(nxt[0])
                    if nxt and nxt[1]:
                        rest_of_tile(m, nxt[0])

            for m in range(4):
                dve.memset(W0[:, m, :], 0.0).then_inc(S.act_done, 1)
            dve.wait_ge(S.act_done, 4)
            clear_sum(SEQ)
            for m in range(KD):
                add_square(SEQ)
            dve.wait_ge(S.con_in, 16)
            dve.wait_ge(S.par_in, 16)
            dve.wait_ge(S.x_in, 16)
            for l in range(DEPTH):
                mixer1(l)
                ffn(SEQ, META, f"ffng{l}", 1.0, (SEQ, None) if l < DEPTH - 1 else (TT, "ffn1g0"), conv=f"fconv{l}")
            ffn(TT, 0, None, 0.5, (TT, None))
            even()
            ffn(TT, 0, None, 0.5, (TT, "ffn1g1"))
            ffn(TT, 0, None, 0.5, (TT, None))
            odd()
            ffn(SEQ, META, None, 0.5, None)


def tile_rows(w, rows=P):
    k = w.shape[0] // rows
    out = np.zeros((P, k, w.shape[1]), w.dtype)
    out[:rows] = w.reshape(k, rows, w.shape[1]).transpose(1, 0, 2)
    return out.reshape(P, -1)


def layout_weights(i):
    mix = []

    def add(w, rows=P):
        mix.append(tile_rows(w, rows).ravel())

    for l in range(DEPTH):
        w = i["w_in"][l]
        moba, mla, sbk, ssm = 0, 768, 1120, 1888
        add(w[:, moba:moba + 512])
        pad = np.zeros((D, 64), w.dtype)
        add(np.concatenate([w[:, mla:mla + 96], pad[:, 0:32], w[:, mla + 96:mla + 192], pad[:, 0:32],
                            w[:, mla + 192:mla + 320], pad, w[:, mla + 320:mla + 352], w[:, ssm + 768:ssm + 772]], 1))
        add(np.concatenate([w[:, moba + 512:moba + 768], w[:, sbk + 512:sbk + 768]], 1))
        add(w[:, sbk:sbk + 512])
        add(w[:, ssm:ssm + 512])
        add(w[:, ssm + 512:ssm + 768])
        for c0 in range(0, D, P * PER1):
            add(i["w_out"][l][:, c0:c0 + P * PER1])
    w = i["ev_w_in_2"][0]
    b0 = 2120
    add(np.concatenate([w[:, 2048:2112], w[:, 2048:2112], w[:, 2112:2120]], 1))
    for c0 in (b0, 1536, b0 + 512, b0 + 1024, b0 + 1536, b0 + 2048, 0, 512, b0 + 2560, 1024):
        add(w[:, c0:c0 + 512])
    for j in range(4):
        add(i["ev_w_out_2"][0][:, 256 * j:256 * j + 256])
    w = i["od_w_in_2"][0]
    add(w[:, 768:1280])
    add(np.concatenate([w[:, 512:576]] * 2 + [w[:, 576:640]] * 2 + [w[:, 640:768]], 1))
    add(w[:, 0:512])
    add(i["od_d_mix_2"][0].transpose(1, 0, 2).reshape(P, 512))
    for j in range(4):
        add(i["od_w_out_2"][0][:, 256 * j:256 * j + 256])
    ins = [i["ffn_w_in"][0], i["ffn_w_in"][1], i["ffn1_w_in_2"][0], i["ffn2_w_in_2"][0], i["ffn1_w_in_2"][1], i["ffn2_w_in_2"][1]]
    outs = [i["ffn_w_out"][0], i["ffn_w_out"][1], i["ffn1_w_out_2"][0], i["ffn2_w_out_2"][0], i["ffn1_w_out_2"][1],
            i["ffn2_w_out_2"][1]]
    wfi = np.stack([tile_rows(np.concatenate([w[:, P * j:P * j + P], w[:, FF + P * j:FF + P * j + P]], 1))
                    for w in ins for j in range(KF)])
    wfo = np.stack([tile_rows(w[:, P * j:P * j + P]) for w in outs for j in range(KD)])
    wmla = []
    for l in range(DEPTH):
        kv = i["mla_w_ukv"][l].reshape(P, 4, 128)
        wmla.append(np.concatenate([
            tile_rows(i["mla_w_uq"][l], 96),
            np.pad(kv[:, :, 0:64], ((0, 0), (0, 0), (0, 32))).reshape(P, 384),
            kv[:, :, 64:128].reshape(P, 256)], 1))
    return np.concatenate(mix), wfi, wfo, np.stack(wmla)


def layout_params(i):
    par = np.zeros((P, PC["end"]), np.float32)

    def put(name, a, at=0):
        a = np.asarray(a)
        par[:a.shape[1], PC[name] + at:PC[name] + at + a.shape[0]] = a.T

    for l in range(DEPTH):
        put(f"mixg{l}", i["mix_norm_g"][l].reshape(8, P))
        put(f"ffng{l}", i["ffn_norm_g"][l].reshape(8, P))
        put(f"mobaq{l}", np.tile(i["moba_qk_g"][l, 0], 2)[None])
        put(f"mobak{l}", np.tile(i["moba_qk_g"][l, 1], 2)[None])
        put(f"mlacq{l}", i["mla_q_norm_g"][l].reshape(2, 96))
        put(f"mlackv{l}", i["mla_kv_norm_g"][l][None])
        put(f"mlaq{l}", i["mla_qk_g"][l, 0][None])
        put(f"mlak{l}", i["mla_qk_g"][l, 1][None])
        put(f"ssmw{l}", i["ssm_conv_w"][l].reshape(4, 4, P).transpose(1, 0, 2).reshape(16, P))
        put(f"ssmb{l}", i["ssm_conv_b"][l].reshape(4, P))
        put(f"dtb{l}", i["ssm_dt_bias"][l][None])
        put(f"alog{l}", i["ssm_a_log"][l][None])
        put(f"dskip{l}", np.repeat(i["ssm_d"][l], HD).reshape(2, P))
        put(f"ssmg{l}", i["ssm_norm_g"][l].reshape(2, P))
        put(f"headg{l}", i["head_out_g"][l].reshape(6, P))
        taps = np.concatenate([i["ffn_conv_w"][l], i["ffn_conv_b"][l][None]]).reshape(4, 2, KF, P).transpose(2, 1, 0, 3)
        put(f"fconv{l}", taps.reshape(KF * 8, P))
        put(f"ffn1g{l}", i["ffn1_norm_2"][l].reshape(8, P))
        put(f"mix2g{l}", i["mix_norm_2"][l].reshape(8, P))
        put(f"ffn2g{l}", i["ffn2_norm_2"][l].reshape(8, P))
    for name, key in (("evq", "ev_a_q_norm_2"), ("evk", "ev_a_k_norm_2"), ("odq", "od_c_q_norm_2"), ("odk", "od_c_k_norm_2")):
        put(name, np.tile(i[key][0], 2)[None])
    put("sink", np.repeat(i["od_c_sinks_2"][0][:, None], P, 1))
    put("dscale", i["od_d_scale_2"][0].reshape(4, P))
    return par


def kernel(**inputs):
    import concourse.bacc as bacc
    from concourse.bass_utils import run_bass_kernel_spmd

    i = {k: np.asarray(v) for k, v in inputs.items()}
    wmix, wfi, wfo, wmla = layout_weights(i)

    def features(x):
        return x.T.reshape(KD, P, x.shape[0]).transpose(1, 0, 2).reshape(P, -1)

    arrays = {
        "wmix": wmix, "wfi": wfi, "wfo": wfo, "wmla": wmla, "params": layout_params(i), "consts": constants(),
        "masks": chunk_masks(), "xin": np.concatenate([features(i["x"][0]), features(i["meta_tokens_2"])], 1),
        "pos": i["positions"],
    }
    nc = bacc.Bacc("TRN2", target_bir_lowering=False, num_devices=1)
    arrays = {f"in_{n}": np.ascontiguousarray(a) for n, a in arrays.items()}
    args = [nc.dram_tensor(n, a.shape, mybir.dt.from_np(a.dtype), kind="ExternalInput").ap() for n, a in arrays.items()]
    out = nc.dram_tensor("out_y", (P, KD, SEQ), F32, kind="ExternalOutput").ap()
    build_program(nc, *args, out)
    r = run_bass_kernel_spmd(nc, [arrays], core_ids=[0])
    y = r.results[0]["out_y"]
    return y.transpose(1, 0, 2).reshape(D, SEQ).T.reshape(1, SEQ, D)
```
